# Optimizing a Trainium2 kernel written in Bass

```python
import math
import jax, jax.numpy as jnp
from jax import lax
import numpy as np

D_MODEL = 2048
BATCH = 1
SEQ = 256
DEPTH = 2

N_EVEN = (DEPTH + 1) // 2
N_ODD = DEPTH // 2
HEAD_DIM = 128
FOX_HEADS = (D_MODEL // 2) // HEAD_DIM
RET_HEADS = (D_MODEL // 2) // HEAD_DIM
FOX_WIDTH = FOX_HEADS * HEAD_DIM
RET_WIDTH = RET_HEADS * HEAD_DIM
Q_BLOCK = 128
RET_CHUNK = 128
S5_WIDTH = D_MODEL // 2
S5_GROUP = 16
S5_GROUPS = S5_WIDTH // S5_GROUP
S5_STATE = 64
CONV_WIDTH = D_MODEL // 2
CONV_K = 3
MEM_LEN = 256
XA_HEADS = 4
XA_HEAD_DIM = 128
XA_WIDTH = XA_HEADS * XA_HEAD_DIM
D_FF = 4 * D_MODEL
EVEN_IN = 3 * FOX_WIDTH + FOX_HEADS + 4 * RET_WIDTH
ODD_IN = S5_WIDTH + 3 * CONV_WIDTH
MIX_OUT = FOX_WIDTH + RET_WIDTH
EPS = 1e-6
ROPE_BASE = 10000.0

kernel_name = 'hybrid_fox_retnet_s5_shortconv_trunk'

F32 = jnp.float32

def rmsnorm(x, g):
    xf = x.astype(F32)
    y = xf * lax.rsqrt(jnp.mean(xf * xf, axis=-1, keepdims=True) + EPS)
    return (y * g.astype(F32)).astype(x.dtype)

def to_heads(t, n_heads):
    b, l, _ = t.shape
    return t.reshape(b, l, n_heads, -1).transpose(0, 2, 1, 3)

def fox_attention(q, k, v, f_logit):
    b, h, l, d = q.shape
    nq = l // Q_BLOCK
    c = jnp.cumsum(jax.nn.log_sigmoid(f_logit.astype(F32)), axis=1).transpose(0, 2, 1)
    qb = q.reshape(b, h, nq, Q_BLOCK, d).transpose(2, 0, 1, 3, 4)
    cb = c.reshape(b, h, nq, Q_BLOCK).transpose(2, 0, 1, 3)
    kpos = jnp.arange(l)
    scale = d ** -0.5

    def block(args):
        qi, ci, i = args
        s = jnp.einsum('bhqd,bhkd->bhqk', qi, k, preferred_element_type=F32) * scale
        s = s + ci[..., None] - c[:, :, None, :]
        qpos = i * Q_BLOCK + jnp.arange(Q_BLOCK)
        s = jnp.where(qpos[:, None] >= kpos[None, :], s, -jnp.inf)
        p = jax.nn.softmax(s, axis=-1)
        return jnp.einsum('bhqk,bhkd->bhqd', p.astype(v.dtype), v)

    o = lax.map(block, (qb, cb, jnp.arange(nq)))
    return o.transpose(1, 0, 3, 2, 4).reshape(b, l, h * d)

def rotary(t):
    d = t.shape[-1]
    l = t.shape[2]
    half = d // 2
    inv = ROPE_BASE ** (-jnp.arange(half, dtype=F32) / half)
    ang = jnp.arange(l, dtype=F32)[:, None] * inv[None, :]
    cos, sin = jnp.cos(ang), jnp.sin(ang)
    t1 = t[..., :half].astype(F32)
    t2 = t[..., half:].astype(F32)
    return jnp.concatenate([t1 * cos - t2 * sin, t1 * sin + t2 * cos], axis=-1).astype(t.dtype)

def retention(q, k, v):
    b, h, l, d = q.shape
    cs = RET_CHUNK
    n = l // cs
    q = rotary(q)
    k = rotary(k) * (d ** -0.5)
    log_g = jnp.log1p(-jnp.exp2(-5.0 - jnp.arange(h, dtype=F32)))
    pos = jnp.arange(cs, dtype=F32)
    diff = pos[:, None] - pos[None, :]
    dmask = jnp.where(diff >= 0, jnp.exp(log_g[:, None, None] * jnp.maximum(diff, 0.0)), 0.0)
    zeta = jnp.exp(log_g[:, None] * (cs - 1 - pos)[None, :])
    xi = jnp.exp(log_g[:, None] * (pos + 1)[None, :])
    g_chunk = jnp.exp(log_g * cs)
    qc = q.reshape(b, h, n, cs, d)
    kc = k.reshape(b, h, n, cs, d)
    vc = v.reshape(b, h, n, cs, d)
    s = jnp.einsum('bhnid,bhnjd->bhnij', qc, kc, preferred_element_type=F32) * dmask[None, :, None]
    o_intra = jnp.einsum('bhnij,bhnje->bhnie', s, vc.astype(F32))
    kv = jnp.einsum('bhnjd,hj,bhnje->nbhde', kc.astype(F32), zeta, vc.astype(F32))

    def step(r, kv_n):
        return g_chunk[None, :, None, None] * r + kv_n, r

    _, r_prev = lax.scan(step, jnp.zeros_like(kv[0]), kv)
    o_cross = jnp.einsum('bhnid,nbhde->bhnie', qc.astype(F32), r_prev) * xi[None, :, None, :, None]
    o = (o_intra + o_cross).reshape(b, h, l, d)
    mu = jnp.mean(o, axis=-1, keepdims=True)
    var = jnp.mean(jnp.square(o - mu), axis=-1, keepdims=True)
    o = (o - mu) * lax.rsqrt(var + EPS)
    return o.transpose(0, 2, 1, 3).reshape(b, l, h * d)

def s5_mixer(u, a_re, a_im, b_re, b_im, c_re, c_im, d_skip, log_step, w_glu):
    bsz, l, _ = u.shape
    uf = u.astype(F32).reshape(bsz, l, S5_GROUPS, S5_GROUP)
    lam = lax.complex(jnp.minimum(a_re.astype(F32), -1e-4), a_im.astype(F32))
    step = jnp.exp(log_step.astype(F32))
    a_bar = jnp.exp(lam * step)
    b_bar = ((a_bar - 1.0) / lam)[..., None] * lax.complex(b_re.astype(F32), b_im.astype(F32))
    bu = jnp.einsum('blgc,gpc->blgp', uf.astype(jnp.complex64), b_bar)
    a_seq = jnp.broadcast_to(a_bar, (l,) + a_bar.shape)

    def combine(e1, e2):
        a1, b1 = e1
        a2, b2 = e2
        return a1 * a2, a2 * b1 + b2

    states = jax.vmap(lambda bu_b: lax.associative_scan(combine, (a_seq, bu_b), axis=0)[1])(bu)
    c_mat = lax.complex(c_re.astype(F32), c_im.astype(F32))
    y = jnp.einsum('blgp,gcp->blgc', states, c_mat).real + d_skip.astype(F32) * uf
    y = y.reshape(bsz, l, S5_WIDTH)
    g = jax.nn.gelu(y)
    return (g * jax.nn.sigmoid(g @ w_glu.astype(F32))).astype(u.dtype)

def short_conv_mixer(h, gate_b, gate_c, conv_w):
    z = gate_c * h
    rhs = conv_w[:, None, :].astype(z.dtype)
    y = lax.conv_general_dilated(z, rhs, window_strides=(1,), padding=[(CONV_K - 1, 0)],
                                 dimension_numbers=('NWC', 'WIO', 'NWC'),
                                 feature_group_count=z.shape[-1])
    return gate_b * y

def even_mixer(xn, w_in, b_forget, w_out):
    proj = xn @ w_in
    cuts = [FOX_WIDTH, 2 * FOX_WIDTH, 3 * FOX_WIDTH, 3 * FOX_WIDTH + FOX_HEADS,
            3 * FOX_WIDTH + FOX_HEADS + RET_WIDTH, 3 * FOX_WIDTH + FOX_HEADS + 2 * RET_WIDTH,
            3 * FOX_WIDTH + FOX_HEADS + 3 * RET_WIDTH]
    fq, fk, fv, ff, rq, rk, rv, rg = jnp.split(proj, cuts, axis=-1)
    fox = fox_attention(to_heads(fq, FOX_HEADS), to_heads(fk, FOX_HEADS), to_heads(fv, FOX_HEADS), ff + b_forget)
    ret = retention(to_heads(rq, RET_HEADS), to_heads(rk, RET_HEADS), to_heads(rv, RET_HEADS))
    ret = (jax.nn.silu(rg.astype(F32)) * ret).astype(xn.dtype)
    return jnp.concatenate([fox.astype(xn.dtype), ret], axis=-1) @ w_out

def odd_mixer(xn, w_in, a_re, a_im, b_re, b_im, c_re, c_im, d_skip, log_step, w_glu, conv_w, w_out):
    proj = xn @ w_in
    cuts = [S5_WIDTH, S5_WIDTH + CONV_WIDTH, S5_WIDTH + 2 * CONV_WIDTH]
    u, h, gb, gc = jnp.split(proj, cuts, axis=-1)
    ssm = s5_mixer(u, a_re, a_im, b_re, b_im, c_re, c_im, d_skip, log_step, w_glu)
    conv = short_conv_mixer(h, gb, gc, conv_w).astype(xn.dtype)
    return jnp.concatenate([ssm, conv], axis=-1) @ w_out

def cross_attention(xn, memn, wq, wkv, wo):
    b, l, _ = xn.shape
    m = memn.shape[1]
    q = (xn @ wq).reshape(b, l, XA_HEADS, XA_HEAD_DIM)
    k, v = jnp.split(memn @ wkv, 2, axis=-1)
    k = k.reshape(b, m, XA_HEADS, XA_HEAD_DIM)
    v = v.reshape(b, m, XA_HEADS, XA_HEAD_DIM)
    s = jnp.einsum('blhd,bmhd->bhlm', q, k, preferred_element_type=F32) * (XA_HEAD_DIM ** -0.5)
    p = jax.nn.softmax(s, axis=-1)
    o = jnp.einsum('bhlm,bmhd->blhd', p.astype(v.dtype), v).reshape(b, l, XA_WIDTH)
    return o @ wo

def sq_relu_mlp(xn, w1, w2):
    return jnp.square(jax.nn.relu(xn @ w1)) @ w2

def setup_inputs(seed: int = 0) -> dict:
    key = jax.random.key(seed)
    ks = jax.random.split(key, 32)

    def nrm(k, shape, scale):
        return jax.random.normal(k, shape, F32) * scale

    def gain(k, shape):
        return 1.0 + 0.05 * jax.random.normal(k, shape, F32)

    n_idx = jnp.arange(S5_STATE, dtype=F32)
    a_im0 = jnp.broadcast_to(math.pi * n_idx, (N_ODD, S5_GROUPS, S5_STATE))
    return {
        'x': nrm(ks[0], (BATCH, SEQ, D_MODEL), 1.0),
        'mem': nrm(ks[1], (BATCH, MEM_LEN, D_MODEL), 1.0),
        'norm_mix': gain(ks[2], (DEPTH, D_MODEL)),
        'norm_xattn': gain(ks[3], (DEPTH, D_MODEL)),
        'norm_mlp': gain(ks[4], (DEPTH, D_MODEL)),
        'norm_mem': gain(ks[5], (D_MODEL,)),
        'norm_final': gain(ks[6], (D_MODEL,)),
        'ab_w_in': nrm(ks[7], (N_EVEN, D_MODEL, EVEN_IN), D_MODEL ** -0.5),
        'ab_b_forget': 3.0 + 0.1 * jax.random.normal(ks[8], (N_EVEN, FOX_HEADS), F32),
        'ab_w_out': nrm(ks[9], (N_EVEN, MIX_OUT, D_MODEL), MIX_OUT ** -0.5),
        'cd_w_in': nrm(ks[10], (N_ODD, D_MODEL, ODD_IN), D_MODEL ** -0.5),
        's5_a_re': -0.5 + 0.01 * jax.random.normal(ks[11], (N_ODD, S5_GROUPS, S5_STATE), F32),
        's5_a_im': a_im0 + 0.01 * jax.random.normal(ks[12], (N_ODD, S5_GROUPS, S5_STATE), F32),
        's5_b_re': nrm(ks[13], (N_ODD, S5_GROUPS, S5_STATE, S5_GROUP), (2 * S5_GROUP) ** -0.5),
        's5_b_im': nrm(ks[14], (N_ODD, S5_GROUPS, S5_STATE, S5_GROUP), (2 * S5_GROUP) ** -0.5),
        's5_c_re': nrm(ks[15], (N_ODD, S5_GROUPS, S5_GROUP, S5_STATE), (2 * S5_STATE) ** -0.5),
        's5_c_im': nrm(ks[16], (N_ODD, S5_GROUPS, S5_GROUP, S5_STATE), (2 * S5_STATE) ** -0.5),
        's5_d': nrm(ks[17], (N_ODD, S5_GROUPS, S5_GROUP), 1.0),
        's5_log_step': jax.random.uniform(ks[18], (N_ODD, S5_GROUPS, S5_STATE), F32,
                                          minval=math.log(1e-3), maxval=math.log(1e-1)),
        's5_w_glu': nrm(ks[19], (N_ODD, S5_WIDTH, S5_WIDTH), S5_WIDTH ** -0.5),
        'conv_w': nrm(ks[20], (N_ODD, CONV_K, CONV_WIDTH), CONV_K ** -0.5),
        'cd_w_out': nrm(ks[21], (N_ODD, MIX_OUT, D_MODEL), MIX_OUT ** -0.5),
        'xa_wq': nrm(ks[22], (DEPTH, D_MODEL, XA_WIDTH), D_MODEL ** -0.5),
        'xa_wkv': nrm(ks[23], (DEPTH, D_MODEL, 2 * XA_WIDTH), D_MODEL ** -0.5),
        'xa_wo': nrm(ks[24], (DEPTH, XA_WIDTH, D_MODEL), XA_WIDTH ** -0.5),
        'mlp_w1': nrm(ks[25], (DEPTH, D_MODEL, D_FF), D_MODEL ** -0.5),
        'mlp_w2': nrm(ks[26], (DEPTH, D_FF, D_MODEL), D_FF ** -0.5),
    }

def reference(x, mem, norm_mix, norm_xattn, norm_mlp, norm_mem, norm_final,
              ab_w_in, ab_b_forget, ab_w_out, cd_w_in,
              s5_a_re, s5_a_im, s5_b_re, s5_b_im, s5_c_re, s5_c_im, s5_d, s5_log_step, s5_w_glu,
              conv_w, cd_w_out, xa_wq, xa_wkv, xa_wo, mlp_w1, mlp_w2):
    memn = rmsnorm(mem, norm_mem)
    h = x
    for layer in range(DEPTH):
        xn = rmsnorm(h, norm_mix[layer])
        if layer % 2 == 0:
            e = layer // 2
            mix = even_mixer(xn, ab_w_in[e], ab_b_forget[e], ab_w_out[e])
        else:
            o = layer // 2
            mix = odd_mixer(xn, cd_w_in[o], s5_a_re[o], s5_a_im[o], s5_b_re[o], s5_b_im[o],
                            s5_c_re[o], s5_c_im[o], s5_d[o], s5_log_step[o], s5_w_glu[o],
                            conv_w[o], cd_w_out[o])
        h = h + mix.astype(h.dtype)
        xa = cross_attention(rmsnorm(h, norm_xattn[layer]), memn, xa_wq[layer], xa_wkv[layer], xa_wo[layer])
        h = h + xa.astype(h.dtype)
        ff = sq_relu_mlp(rmsnorm(h, norm_mlp[layer]), mlp_w1[layer], mlp_w2[layer])
        h = h + ff.astype(h.dtype)
    return rmsnorm(h, norm_final)


_drawn_inputs = setup_inputs


def setup_inputs(seed=0):
    import zlib

    import numpy as np

    out = dict(_drawn_inputs(seed))
    spreads = {}
    factors = {'norm_xattn': 8.0,
     'norm_mem': 5.629,
     'ab_b_forget': 23.907,
     's5_a_re': 64.0,
     's5_a_im': 47.704,
     's5_b_re': 64.0,
     's5_b_im': 64.0,
     's5_c_re': 64.0,
     's5_c_im': 64.0,
     's5_log_step': 56.36}
    for name, (base, spread) in spreads.items():
        noise = np.random.default_rng([zlib.crc32(name.encode()), seed]).standard_normal(out[name].shape)
        drawn = base * np.exp(spread * noise) if base else spread * noise
        out[name] = __import__('jax').numpy.asarray(drawn.astype(out[name].dtype))
    for name, factor in factors.items():
        out[name] = (out[name] * factor).astype(out[name].dtype)
    return out
```

```python
from contextlib import ExitStack

import concourse.bass as bass
import numpy as np
from concourse import mybir

F32 = mybir.dt.float32
F32R = mybir.dt.float32r
BF16 = mybir.dt.bfloat16
I32 = mybir.dt.int32
ACT = mybir.ActivationFunctionType
ALU = mybir.AluOpType
AX = mybir.AxisListType

P = 128
D = 2048
L = 256
TOK = L // P
NB = 512
BLOCKS = D // NB
FF = 4 * D
EPS = 1e-6
HD = 128
HALVES = 8
RING = 4
CHUNK = 1024
CHUNKS = FF // CHUNK
G, GC, ST = 64, 16, 64
Q = G // 2
T8 = 8
J = L // T8
GW = T8 * GC
NEG = -1.0e30
MIX, XAT, MLP, MEM = 0, 32, 64, 96


class Place:

    def __init__(self):
        self.n, self.reg, self.rates = {}, None, {}

    def at(self, what, plus=0, by=1):
        v = (self.n.get(what, 0) + plus) // by
        if self.reg is None or not self.rates.get(what):
            return v
        return self.reg * (self.rates[what] // by) + v

    def bump(self, what, k=1):
        self.n[what] = self.n.get(what, 0) + k
        return self.at(what)

    def enter(self, reg, rates):
        self.reg, self.rates, self.entry = reg, rates, dict(self.n)

    def leave(self, trips):
        for k in set(self.n) | set(self.rates):
            got = self.n.get(k, 0) - self.entry.get(k, 0)
            assert got == self.rates.get(k, 0), (k, got, self.rates)
            self.n[k] = self.entry.get(k, 0) + trips * got
        self.reg = None


def plan(kind, order=(0, 1, 2, 3), kbase=0):
    if kind == "full":
        return [(0, order[i // 2] * 4 + 2 * (i % 2), i == 0, i == 7) for i in range(8)]
    if kind == "pair":
        return [((i // 2) % 2, kbase + (i // 4) * 4 + 2 * (i % 2), i < 4 and i % 2 == 0,
                 i >= 4 and i % 2 == 1) for i in range(8)]
    return [(i // 2, 2 * (i % 2), i % 2 == 0, i % 2 == 1) for i in range(8)]


UNIT_BLOCKS = {"full": 1, "pair": 2, "quad": 4}
STEP_RATES = {"half": 32, "unit": 4, "block": 6, "tp": 4, "his": 4, "hid": 2}


def trunk(nc, x, mem, norm_mix, norm_xattn, norm_mlp, norm_mem, norm_final, ab_w_in, ab_b_forget,
          ab_w_out, cd_w_in, s5_a_re, s5_a_im, s5_b_re, s5_b_im, s5_c_re, s5_c_im, s5_d,
          s5_log_step, s5_w_glu, conv_w, cd_w_out, xa_wq, xa_wkv, xa_wo, mlp_w1, mlp_w2,
          rope, decay_in, tri, causal, eye, out):
    ctx = ExitStack()
    with ctx:
        def sb(name, shape, dt=F32):
            return ctx.enter_context(nc.sbuf_tensor(name, shape, dt))

        def sem(name):
            return ctx.enter_context(nc.semaphore(name))

        h = sb("h", [P, TOK, D])
        xt = [sb(f"xt_{n}", [P, 16, L], F32R) for n in ("hi", "lo")]
        yt = [sb(f"yt_{n}", [P, 16, L], F32R) for n in ("hi", "lo")]
        raw = sb("raw", [P, RING, 4, NB])
        whi = sb("whi", [P, RING, 2, NB], F32R)
        wlo = sb("wlo", [P, RING, 2, NB], F32R)
        ident = sb("ident", [P, P])
        mask = sb("mask", [P, P])
        cs = sb("cs", [P, 2, TOK, HD // 2])
        gain = sb("gain", [P, 7 * 16 + 24])
        bfor = sb("bfor", [P, 8])
        rstd = sb("rstd", [P, 9, TOK])
        ssq = sb("ssq", [P, TOK, BLOCKS])
        nrm = sb("nrm", [P, 4, 8])
        junk = sb("junk", [P, TOK, NB], BF16)
        c8 = sb("c8", [8, 2, L])
        smx = sb("smx", [P, 2, 3, 2])
        kvk = sb("kvk", [P, 4, L])
        kvv = sb("kvv", [P, TOK, NB])
        A_SIZE = 11200
        arena = sb("arena", [P, A_SIZE])

        def view(at, n, pattern=None, p=P, **sizes):
            assert at + n <= A_SIZE
            a = arena[0:p, at:at + n]
            return a.rearrange(pattern, **sizes) if pattern else a

        memt = view(0, 4096, "p (t n) -> p t n", t=TOK)
        grow = view(4096, 128)
        crow = view(4224, 128)
        s5row = view(4352, 128)
        s5b = view(4480, 1024, "p (r q c) -> p r q c", r=2, q=Q)
        s5c = view(5504, 1024, "p (r q c) -> p r q c", r=2, q=Q)
        par = view(6528, 16 * 32, "p (k q) -> p k q", k=16)
        pw = view(7040, 576, "p (r k q) -> p r k q", r=2, k=9)
        pb = view(7616, 512, "p (r k q) -> p r k q", r=2, k=8)
        craw = view(8128, 1024, "p (r t k) -> p r t k", r=2, t=4)
        ptmp = view(9152, 512, "p (k q) -> p k q", k=16)
        etab = view(0, 1024, "p (b q r w) -> p b q r w", b=2, q=2, r=2)
        caz = view(1024, 2304, "p (b q r s w) -> p b q r s w", b=2, q=2, r=2, s=2)
        vtmp = view(3328, 288)
        gtmp = view(3616, 288)
        vtmp2 = view(3904, 288)
        gtmp2 = view(4192, 288)
        ets = view(8128, 512)
        ksb = view(9152, 960, "p (g w) -> p g w", p=16, g=4)
        nat = view(0, 1024, "p (t n) -> p t n", t=TOK)
        rot = view(1024, 1024, "p (t n) -> p t n", t=TOK)
        rtmp = view(2048, 1024, "p (a t h n) -> p a t h n", a=2, t=TOK, h=4)
        qT = view(3072, 1024, "p (h n) -> p h n", h=4)
        kT = view(4096, 1024, "p (h n) -> p h n", h=4)
        vn = view(5120, 1024, "p (t n) -> p t n", t=TOK)
        gate = view(6144, 1024, "p (t n) -> p t n", t=TOK)
        ro = view(7168, 1024, "p (t n) -> p t n", t=TOK)
        pr = view(8192, 1024, "p (b n) -> p b n", b=2)
        pT = view(9216, 1024, "p (b n) -> p b n", b=2)
        dec = view(10240, 768, "p (h n) -> p h n", h=2)
        stat = sb("stat", [P, 8, 6])
        mv = sb("mv", [P, 8, 2])
        kst_nat = view(10176, 1024, "p (t n) -> p t n", t=TOK)
        kst = view(10176, 1024)
        trit = sb("trit", [P, L])
        wff = sb("wff", [P, 16, 8])
        lgt = sb("lgt", [P, 4, TOK, 8])
        wffs = [sb(f"wff_{n}", [P, 16, 8], F32R) for n in ("hi", "lo")]
        UT = view(0, 2048, "p (r q j) -> p r q j", r=2, q=Q)
        S = view(2048, 2048, "p (r q j) -> p r q j", r=2, q=Q)
        Ucb = [view(4096, 1024, "p (r q w) -> p r q w", p=J, r=2, q=4),
               kvk[0:J].rearrange("p h n -> p (h n)").rearrange("p (r q w) -> p r q w", r=2, q=4)]
        Yc = view(4096, 1024, "p (b i r n) -> p b i r n", p=J, b=2, i=T8, r=2)
        ETb = [view(5120, 1024, "p (q r w) -> p q r w", q=4, r=2),
               kvv[:, :, :].rearrange("p t n -> p (t n)").rearrange("p (q r w) -> p q r w", q=4, r=2)]
        Tc = view(5120, 1024, "p (b r q w) -> p b r q w", b=2, r=2, q=2)
        CAb = [t.rearrange("p (q r s w) -> p q r s w", q=2, r=2, s=2) for t in (
            kvk[:, :, :].rearrange("p h n -> p (h n)"), kvv[:, :, :].rearrange("p t n -> p (t n)"))]
        rc = view(10432, 768)
        hn = view(6336, 1024, "p (t n) -> p t n", t=TOK)
        zT = view(7360, 1024, "p (k n) -> p k n", k=4)
        cv = view(8384, 1024, "p (k n) -> p k n", k=4)
        a8 = sb("a8", [P, 2, T8, Q])
        onat = view(9408, 1024, "p (t n) -> p t n", t=TOK)
        dsk = view(7360, 1024)
        yy = view(0, 2048, "p (t n) -> p t n", t=TOK)
        uu = view(2048, 2048, "p (t n) -> p t n", t=TOK)
        sg = view(4096, 2048, "p (t n) -> p t n", t=TOK)
        gfin = view(6144, 2048)
        fin = view(2048, 4096, "p (t n) -> p t n", t=TOK)

        acc = ctx.enter_context(nc.psum_tensor("acc", [P, 4, NB], F32))
        tp = ctx.enter_context(nc.psum_tensor("tp", [P, 2, NB], F32))
        at = ctx.enter_context(nc.psum_tensor("at", [P, 2, NB], F32))

        et_d = nc.dram_tensor("et_d", [P, Q, 2, GW], F32, kind="Internal").ap()
        ca_d = nc.dram_tensor("ca_d", [P, Q, 2, 2, 144], F32, kind="Internal").ap()
        k_d = nc.dram_tensor("k_d", [GC, G, 240], F32, kind="Internal").ap()
        u_d = nc.dram_tensor("u_d", [L, G * GC], F32, kind="Internal").ap()
        uc_d = nc.dram_tensor("uc_d", [G, L, GC], F32, kind="Internal").ap()
        kv_d = nc.dram_tensor("kv_d", [2, P, 1024], F32, kind="Internal").ap()
        t_d = nc.dram_tensor("t_d", [P, G, GW], F32, kind="Internal").ap()
        y_d = nc.dram_tensor("y_d", [L, G * GC], F32, kind="Internal").ap()

        raw_landed = [sem(f"raw_landed{s}") for s in range(RING)]
        hi_ready = sem("hi_ready")
        lo_ready = sem("lo_ready")
        half_used = sem("half_used")
        acc_free = [sem(f"acc_free{p}") for p in range(2)]
        tp_full = sem("tp_full")
        tp_free = [sem(f"tp_free{b}") for b in range(2)]
        at_full = sem("at_full")
        at_free = [sem(f"at_free{b}") for b in range(2)]
        hi_put = sem("hi_put")
        hid_ready = sem("hid_ready")
        ssq_ready = sem("ssq_ready")
        var_ready, sd_ready, rstd_ready = sem("var_ready"), sem("sd_ready"), sem("rstd_ready")
        rot_ready = sem("rot_ready")
        hi_in, kv_out, kv_in = sem("hi_in"), sem("kv_out"), sem("kv_in")
        act_step, dve_step, pool_step = sem("act_step"), sem("dve_step"), sem("pool_step")
        cst = {n: sem(f"ld_{n}") for n in ("cst", "grow", "mem", "x", "s5", "ff", "tri", "dsk", "gf")}
        dec_in = [sem(f"dec_in{b}") for b in range(2)]
        rstd8 = sem("rstd8")
        mem_in = [sem(f"mem_in{b}") for b in range(BLOCKS)]
        x_in = [sem(f"x_in{b}") for b in range(BLOCKS)]
        gain_ready = sem("gain_ready")
        sm_max, sm_p = sem("sm_max"), sem("sm_p")
        ro_stat, ro_ready = sem("ro_stat"), sem("ro_ready")
        ff_hi, ff_split, ff_z, ff_log, ff_act = (sem(n) for n in ("ff_hi", "ff_split", "ff_z", "ff_log", "ff_act"))
        c_ready = sem("c_ready")
        t_out = sem("t_out")
        s5_par, s5_sin, s5_lam, s5_inv, s5_pw = (sem(n) for n in (
            "s5_par", "s5_sin", "s5_lam", "s5_inv", "s5_pw"))
        s5_re, s5_im = sem("s5_re"), sem("s5_im")
        s5_used = sem("s5_used")
        et_out, k_out = sem("et_out"), sem("k_out")
        ca_out = [sem(f"ca_out{b}") for b in range(2)]
        ksb_zero, caz_zero = sem("ksb_zero"), sem("caz_zero")
        u_out = sem("u_out")
        uc_in, et_in = ([sem(f"{n}{b}") for b in range(2)] for n in ("uc_in", "et_in"))
        ca_in = [sem(f"ca_in{b}") for b in range(2)]
        t_in = [sem(f"t_in{b}") for b in range(2)]
        ut_ready, x8_ready, scan_ready = sem("ut_ready"), sem("x8_ready"), sem("scan_ready")
        y_out, y_in = [sem(f"y_out{b}") for b in range(2)], sem("y_in")
        z_ready, cv_ready, gb_prod = sem("z_ready"), sem("cv_ready"), sem("gb_prod")
        y_ready, ge_ready, sig_ready, ssm_ready = (sem(n) for n in ("y_ready", "ge_ready", "sig_ready", "ssm_ready"))
        fin_ready, out_done = sem("fin_ready"), sem("out_done")

        par_of = {n: i for i, n in enumerate((
            "lre", "lim", "ls", "step", "k", "r", "e", "mag", "th", "ph", "sin", "cos",
            "t1", "t2", "t3", "t4"))}
        E_UNITS = [("rq", 0), ("rk", 0), ("rv", 0), ("rg", 0), ("rq", 1), ("rk", 1), ("rv", 1),
                   ("rg", 1), ("fq", 0), ("fk", 0), ("fv", 0), ("fq", 1), ("fk", 1), ("fv", 1)]
        FW = 1024
        E_COL = {"fq": 0, "fk": FW, "fv": 2 * FW, "rq": 3 * FW + 8, "rk": 4 * FW + 8,
                 "rv": 5 * FW + 8, "rg": 6 * FW + 8}
        O_UNITS = [("u", 0), ("u", 1), ("h", 0), ("gc", 0), ("gb", 0), ("h", 1), ("gc", 1), ("gb", 1)]
        O_COL = {"u": 0, "h": 1024, "gb": 2048, "gc": 3072}
        OUT_ORDER = (2, 3, 0, 1)
        CHUNK_T = [12 + 7 * k // 4 for k in range(16)]
        X8_T, Y_T = 24, 57
        SCALE = float(HD) ** -0.5
        DVE_T = [t + 2 for t in CHUNK_T]
        at_before_ret = 3 + 2 * 16 + 2
        OB = 4 + 14 + 4 + 1 + 4 + 6 * CHUNKS
        at_before_y = [3 + 2 * 16 + 2 + 8 + 8 + 4 + 8]
        block = ctx.enter_context(nc.Block())


        def wait_freed(eng, p, back):
            b = p.n["block"] - back
            eng.wait_ge(acc_free[b % 2], p.at("block", -back, by=2) + 1)

        def wait_tp_read(eng, token):
            eng.wait_ge(tp_free[token[0]], token[1])

        def tp_token(p):
            return p.n["tp"] % 2, p.at("tp", 0, by=2) + 1

        def root_count(m):
            return m + 1 if m < 2 else m + 3

        def table_parts(coef, power, q0, n):
            shape = [P, 2, n, GC]
            cr, ci = (coef[:, r, q0:q0 + 2, :].unsqueeze(2).to_broadcast(shape) for r in range(2))
            pr_, pi_ = (power[:, r, 0:n, q0:q0 + 2].rearrange("p i q -> p q i").unsqueeze(3).to_broadcast(shape)
                        for r in range(2))
            return cr, ci, pr_, pi_

        def parity(p, back):
            return (p.n["block"] - back) % 2

        @block.sync
        def _(sp):
            p = Place()
            p.n = {"half": 0, "unit": 0}

            def slab(i, src, first=False):
                if not first:
                    sp.wait_ge(lo_ready, p.at("half", 2 * i + 2 - 8))
                sp.dma_start(raw[:, i], src.rearrange("(k p) n -> p k n", p=P)).then_inc(raw_landed[i], 16)

            def load(kind, w, cols, order=(0, 1, 2, 3), row0=0, first=False, hook=None):
                for i in range(RING):
                    if kind == "full":
                        c, r = cols[0], order[i] * NB
                    elif kind == "pair":
                        c, r = cols[i % 2], (i // 2) * NB
                    else:
                        c, r = cols[i], 0
                    rows = slice(row0 + r, row0 + r + NB) if isinstance(row0, int) else bass.ds(row0 + r, NB)
                    cc = slice(c, c + NB) if isinstance(c, int) else bass.ds(c, NB)
                    slab(i, w[rows, cc], first)
                    if hook:
                        hook(i)
                p.bump("half", 8)
                p.bump("unit")

            def mlp(layer):
                def step(c):
                    w1, w2 = mlp_w1[layer], mlp_w2[layer]
                    load("full", w1, [c * CHUNK])
                    load("full", w1, [c * CHUNK + NB])
                    load("pair", w2, [0, NB], row0=c * CHUNK)
                    load("pair", w2, [2 * NB, 3 * NB], row0=c * CHUNK)
                step(0)
                with sp.Fori(0, CHUNKS - 2) as r:
                    p.enter(r, {"half": 32, "unit": 4})
                    step(r + 1)
                    p.leave(CHUNKS - 2)
                step(CHUNKS - 1)

            for dst, src in ((ident[:, :], eye), (mask[:, :], causal),
                             (cs[:, :, :, :], rope.rearrange("p (a t n) -> p a t n", a=2, t=TOK)),
                             (bfor[:, :], ab_b_forget[0:1, :].to_broadcast([P, 8]))):
                sp.dma_start(dst, src).then_inc(cst["cst"], 16)
            for r0, src in ((MIX, norm_mix), (XAT, norm_xattn), (MLP, norm_mlp)):
                sp.dma_start(grow[r0:r0 + 32, :], src.rearrange("l (k p) -> (l k) p", p=P)).then_inc(cst["grow"], 16)
            sp.dma_start(grow[MEM:MEM + 16, :], norm_mem.rearrange("(k p) -> k p", p=P)).then_inc(cst["grow"], 16)
            sp.dma_start(crow[0:24, :], conv_w[0].rearrange("s (k p) -> (s k) p", p=P)).then_inc(cst["grow"], 16)
            for b in range(BLOCKS):
                sp.dma_start(memt[:, :, b * NB:(b + 1) * NB], mem[0].rearrange("(t p) n -> p t n", p=P)[
                    :, :, b * NB:(b + 1) * NB]).then_inc(mem_in[b], 16)
            load("full", xa_wkv[0], [0], first=True)
            for b in range(BLOCKS):
                sp.dma_start(h[:, :, b * NB:(b + 1) * NB], x[0].rearrange("(t p) n -> p t n", p=P)[
                    :, :, b * NB:(b + 1) * NB]).then_inc(x_in[b], 16)
            load("full", xa_wkv[0], [NB])
            for n in range(2):
                load("full", xa_wkv[1], [n * NB])
            for name, g in E_UNITS:
                load("full", ab_w_in[0], [E_COL[name] + g * NB])
            for n in range(BLOCKS):
                load("full", ab_w_out[0], [n * NB], order=OUT_ORDER)
            load("full", xa_wq[0], [0])
            load("quad", xa_wo[0], [n * NB for n in range(4)])
            mlp(0)
            for name, g in O_UNITS:
                load("full", cd_w_in[0], [O_COL[name] + g * NB])

            def y_tables(t):
                for k in (t - 65, t - 64):
                    if 0 <= k < 16:
                        b = k % 2
                        if k >= 2:
                            sp.wait_ge(at_full, at_before_y[0] + k - 1)
                        else:
                            sp.wait_ge(at_full, at_before_y[0])
                        sp.dma_start(CAb[b], ca_d[:, 2 * k:2 * k + 2, :, :, GC:]).then_inc(ca_in[b], 16)
                        sp.dma_start(Tc[:, b], t_d.rearrange("p (s q) w -> p s q w", s=2)[
                            :, :, 2 * k:2 * k + 2, :]).then_inc(t_in[b], 16)

            sp.wait_ge(t_out, 16 * T8)
            for b in range(2):
                sp.wait_ge(ca_out[b], 16 * 8)
            for o, n in ((8, 0), (9, 2)):
                load("pair", cd_w_out[0], [n * NB, n * NB + NB], row0=1024, hook=lambda i, o=o: y_tables(8 * o + 2 * i))
            load("pair", s5_w_glu[0], [0, NB], hook=lambda i: y_tables(80 + 2 * i))
            load("pair", cd_w_out[0], [0, NB])
            sp.wait_ge(at_full, at_before_y[0] + 16)
            sp.wait_ge(kv_out, 32)
            sp.dma_start(kvk[:, :, :], kv_d[0].rearrange("p (h n) -> p h n", h=4)).then_inc(kv_in, 16)
            sp.dma_start(kvv[:, :, :], kv_d[1].rearrange("p (t n) -> p t n", t=TOK)).then_inc(kv_in, 16)
            load("pair", cd_w_out[0], [2 * NB, 3 * NB])
            load("full", xa_wq[1], [0])
            load("quad", xa_wo[1], [n * NB for n in range(4)])
            mlp(1)
            for b in range(BLOCKS):
                sp.wait_ge(fin_ready, b + 1)
                sp.dma_start(out[0].rearrange("(t p) n -> p t n", p=P)[:, :, b * NB:(b + 1) * NB],
                             fin[:, :, b * NB:(b + 1) * NB]).then_inc(out_done, 16)
            sp.wait_ge(out_done, 16 * BLOCKS)

        @block.tensor
        def _(pe):
            p = Place()
            p.n = {"half": 0, "unit": 0, "block": 0, "tp": 0, "hid": 0}
            x_tok, y_tok = {}, {}

            def unit(kind, src, tok, after=None, order=(0, 1, 2, 3), kbase=0):
                hi, lo = src
                for i, (blk, kt0, opens, closes) in enumerate(plan(kind, order, kbase)):
                    par = (p.n["block"] + blk) % 2
                    if opens and p.n["block"] + blk >= 2:
                        pe.wait_ge(acc_free[par], p.at("block", blk, by=2))
                    for kt in (kt0, kt0 + 1):
                        if kt in tok:
                            wait_tp_read(pe, tok.pop(kt))
                    pe.wait_ge(lo_ready, p.at("half", i + 1))
                    for kk in range(2):
                        for t in range(TOK):
                            a = acc[:, 2 * par + t, :]
                            xh, xl = (s[:, kt0 + kk, t * P:(t + 1) * P] for s in (hi, lo))
                            w = i % RING
                            pe.matmul(a, xh, whi[:, w, kk], start=opens and kk == 0, stop=False)
                            pe.matmul(a, xh, wlo[:, w, kk], start=False, stop=False)
                            last = pe.matmul(a, xl, whi[:, w, kk], start=False, stop=closes and kk == 1)
                    last.then_inc(half_used, 1)
                    if after:
                        after(i)
                p.bump("half", 8)
                p.bump("unit")
                p.bump("block", UNIT_BLOCKS[kind])

            def open_tp():
                n = p.n["tp"]
                if n >= 2:
                    pe.wait_ge(tp_free[n % 2], p.at("tp", 0, by=2))
                return tp[:, n % 2, :]

            def close_tp(last):
                last.then_inc(tp_full, 1)
                token = tp_token(p)
                p.bump("tp")
                return token

            def transpose_block(src, tok=None, kt0=0):
                tokens = []
                for b in range(2):
                    bank = open_tp()
                    for kk in range(2):
                        for t in range(TOK):
                            last = pe.transpose(bank[:, kk * L + t * P:kk * L + (t + 1) * P],
                                                src[:, t, (2 * b + kk) * P:(2 * b + kk + 1) * P], ident[:, :])
                    token = close_tp(last)
                    tokens.append(token)
                    if tok is not None:
                        tok[kt0 + 2 * b] = tok[kt0 + 2 * b + 1] = token
                return tokens

            def h_block(n, back):
                wait_freed(pe, p, back)
                transpose_block(h[:, :, n * NB:(n + 1) * NB], x_tok, 4 * n)

            def open_at():
                n = p.n.setdefault("at", 0)
                if n >= 2:
                    pe.wait_ge(at_free[n % 2], n // 2)
                return at[:, n % 2, :]

            def close_at(last):
                last.then_inc(at_full, 1)
                p.bump("at")

            def mm(o, lhsT, rhs, start=True, stop=True):
                return pe.matmul(o, lhsT, rhs, start=start, stop=stop)

            pe.wait_ge(cst["cst"], 64)
            pe.wait_ge(cst["grow"], 80)
            close_tp(pe.transpose(open_tp()[:, 0:112], grow[0:112, :], ident[0:112, 0:112]))
            close_tp(pe.transpose(open_tp()[:, 0:24], crow[0:24, :], ident[0:24, 0:24]))
            for b in range(BLOCKS):
                pe.wait_ge(mem_in[b], 16)
                transpose_block(memt[:, :, b * NB:(b + 1) * NB], y_tok, 4 * b)

            kv_tok = []

            def s5_rows():
                pe.wait_ge(cst["s5"], 16 * 15)
                bank = open_at()
                close_at(pe.transpose(bank[:, 0:96], s5row[0:96, :], ident[0:96, 0:96]))
                for r in range(2):
                    bank = open_at()
                    for t in range(4):
                        last = pe.transpose(bank[:, t * P:(t + 1) * P], craw[:, r, t, :], ident[:, :])
                    close_at(last)

            def s5_chunk(k):
                b = k % 2
                pe.wait_ge(s5_re, k + 1)
                pe.wait_ge(s5_im, k + 1)
                bank = open_at()
                for q in range(2):
                    for r in range(2):
                        last = pe.transpose(bank[:, (2 * q + r) * P:(2 * q + r + 1) * P],
                                            etab[:, b, q, r, :], ident[:, :])
                close_at(last)
                bank = open_at()
                for q in range(2):
                    for s in range(2):
                        o = bank[0:GC, (2 * s + q) * P:(2 * s + q + 1) * P]
                        mm(o, etab[:, b, q, 0, GW - GC:GW], caz[:, b, q, 0, s, 0:GW], True, False)
                        last = mm(o, etab[:, b, q, 1, GW - GC:GW], caz[:, b, q, 1, s, 0:GW], False, True)
                close_at(last)

            def s5_tables(t):
                if t in CHUNK_T:
                    s5_chunk(CHUNK_T.index(t))

            for u in range(4):
                def after(i, u=u):
                    if i == 5:
                        pe.wait_ge(x_in[u], 16)
                        transpose_block(h[:, :, u * NB:(u + 1) * NB], x_tok, 4 * u)
                    if u == 0 and i == 3:
                        s5_rows()
                    if u in (1, 3) and i == 2:
                        wait_freed(pe, p, 1)
                        transpose_block(kst_nat)
                    s5_tables(8 * u + i)
                unit("full", yt, y_tok, after)

            def forget_logits():
                pe.wait_ge(ff_split, 1)
                bank = open_at()
                for t in range(TOK):
                    o = bank[:, t * 8:(t + 1) * 8]
                    for kt in range(16):
                        xh, xl = (s[:, kt, t * P:(t + 1) * P] for s in xt)
                        mm(o, xh, wffs[0][:, kt, :], kt == 0, False)
                        mm(o, xh, wffs[1][:, kt, :], False, False)
                        last = mm(o, xl, wffs[0][:, kt, :], False, kt == 15)
                close_at(last)

            def forget_sums():
                pe.wait_ge(ff_log, 1)
                pe.wait_ge(cst["tri"], 16)
                bank = open_at()
                mm(bank[0:8, 0:L], lgt[:, 0, 0, :], trit[:, :], True, False)
                close_at(mm(bank[0:8, P:L], lgt[:, 0, 1, :], trit[:, 0:P], False, True))

            decayed = {}

            def ret_scores(hh):
                bank = open_at()
                decayed[hh] = (p.n["at"] % 2, p.n["at"] // 2 + 1)
                mm(bank[:, 0:L], kT[:, hh, 0:P], qT[:, hh, :])
                close_at(mm(bank[:, L:L + P], kT[:, hh, P:L], qT[:, hh, P:L]))

            def ret_out(g, hh):
                b = hh % 2
                pe.wait_ge(at_free[decayed[hh][0]], decayed[hh][1])
                bank = open_tp()
                mm(bank[:, 0:P], pT[:, b, 0:P], vn[:, 0, hh * P:(hh + 1) * P])
                mm(bank[:, P:L], pT[:, b, P:L], vn[:, 0, hh * P:(hh + 1) * P], True, False)
                close_tp(mm(bank[:, P:L], pT[:, b, L:L + P], vn[:, 1, hh * P:(hh + 1) * P], False, True))

            def fox_scores(g, hh):
                hd = 4 * g + hh
                bank = open_at()
                for t in range(TOK):
                    o = bank[:, t * P:t * P + (t + 1) * P]
                    n = (t + 1) * P
                    mm(o, qT[:, hh, t * P:(t + 1) * P], kT[:, hh, 0:n], True, False)
                    mm(o, c8[:, 0, t * P:(t + 1) * P], ident[0:8, hd:hd + 1].to_broadcast([8, n]), False, False)
                    mm(o, ident[0:8, hd:hd + 1].to_broadcast([8, P]), c8[:, 1, 0:n], False, False)
                    last = mm(bank[:, (2 * t) * P:(2 * t + 1) * P], ident[:, :], mask[:, :], False, True)
                close_at(last)

            def fox_turn(hh):
                n = p.n.setdefault("sm", 0)
                pe.wait_ge(sm_p, n + 1)
                b = n % 2
                bank = open_tp()
                pe.transpose(bank[:, 0:P], pr[:, b, 0:P], ident[:, :])
                pe.transpose(bank[:, P:L], pr[:, b, P:L], ident[:, :])
                p.bump("sm")
                return close_tp(pe.transpose(bank[:, L:L + P], pr[:, b, L:L + P], ident[:, :]))

            def fox_out(hh, token, kt):
                b = hh % 2
                wait_tp_read(pe, token)
                bank = open_tp()
                mm(bank[:, 0:L], vn[:, 0, hh * P:(hh + 1) * P], pT[:, b, 0:L], True, False)
                y_tok[kt] = close_tp(mm(bank[:, P:L], vn[:, 1, hh * P:(hh + 1) * P], pT[:, b, L:L + P],
                                        False, True))

            turned = {}

            def fox_steps(g, i):
                def turn(hh):
                    turned[hh] = fox_turn(hh)
                if i == 0:
                    for tk in turned_qk:
                        wait_tp_read(pe, tk)
                    turned_qk.clear()
                    pe.wait_ge(c_ready, 1)
                    fox_scores(g, 0)
                    fox_scores(g, 1)
                elif i == 1:
                    turn(0)
                    fox_scores(g, 2)
                elif i == 2:
                    wait_freed(pe, p, 1)
                    fox_out(0, turned[0], 4 * g)
                    turn(1)
                    fox_scores(g, 3)
                elif i in (3, 4):
                    fox_out(i - 2, turned[i - 2], 4 * g + i - 2)
                    turn(i - 1)
                elif i == 5:
                    fox_out(3, turned[3], 4 * g + 3)

            turned_qk = []

            def even_after(e, i):
                if e == 0 and i == 5:
                    forget_logits()
                if e == 1 and i == 5:
                    forget_sums()
                prev = E_UNITS[e - 1] if e else None
                if prev and prev[0] in ("rq", "rk") and i == 6:
                    pe.wait_ge(rot_ready, p.bump("rot"))
                    turned_qk.extend(transpose_block(rot))
                if prev and prev[0] in ("fq", "fk") and i == 6:
                    wait_freed(pe, p, 1)
                    turned_qk.extend(transpose_block(nat))
                if prev and prev[0] == "rv":
                    if i == 1:
                        for tk in turned_qk:
                            wait_tp_read(pe, tk)
                        turned_qk.clear()
                    if 2 <= i <= 5:
                        ret_scores(i - 2)
                    if i == 3:
                        wait_freed(pe, p, 1)
                    if 3 <= i <= 6:
                        ret_out(prev[1], i - 3)
                if e >= 2 and E_UNITS[e - 2][0] == "rg" and i == 1:
                    g = E_UNITS[e - 2][1]
                    pe.wait_ge(ro_ready, g + 1)
                    transpose_block(gate, y_tok, 8 + 4 * g)
                if prev and prev[0] == "fv":
                    fox_steps(prev[1], i)

            for e in range(len(E_UNITS)):
                def after(i, e=e):
                    even_after(e, i)
                    s5_tables(8 * (e + 4) + i)
                unit("full", xt, x_tok, after)

            def out_proj(n, i):
                if n == 0:
                    fox_steps(1, i)
                elif i == 2:
                    h_block(n - 1, 1)

            for n in range(BLOCKS):
                unit("full", yt, y_tok, lambda i, n=n: out_proj(n, i), order=OUT_ORDER)

            def cross(layer):
                wait_freed(pe, p, 1)
                q_tok = transpose_block(nat)
                if layer:
                    pe.wait_ge(kv_in, 32)
                for tk in q_tok:
                    wait_tp_read(pe, tk)

                def scores(hh):
                    bank = open_at()
                    mm(bank[:, 0:L], qT[:, hh, 0:P], kvk[:, hh, :])
                    close_at(mm(bank[:, L:2 * L], qT[:, hh, P:L], kvk[:, hh, :]))

                def turn_and_out(hh):
                    n = p.n.setdefault("sm", 0)
                    b = n % 2
                    pe.wait_ge(sm_p, n + 1)
                    bank = open_tp()
                    for mt in range(TOK):
                        for t in range(TOK):
                            last = pe.transpose(bank[:, mt * L + t * P:mt * L + (t + 1) * P],
                                                pr[:, b, t * L + mt * P:t * L + (mt + 1) * P], ident[:, :])
                    wait_tp_read(pe, close_tp(last))
                    bank = open_tp()
                    mm(bank[:, 0:L], kvv[:, 0, hh * P:(hh + 1) * P], pT[:, b, 0:L], True, False)
                    y_tok[hh] = close_tp(mm(bank[:, 0:L], kvv[:, 1, hh * P:(hh + 1) * P],
                                            pT[:, b, L:2 * L], False, True))
                    p.bump("sm")

                scores(0)
                scores(1)
                for hh in range(4):
                    turn_and_out(hh)
                    if hh < 2:
                        scores(hh + 2)

            def attention_and_out(layer, first_after):
                unit("full", xt, x_tok, first_after)
                cross(layer)

                def after(i):
                    if i == 4:
                        h_block_in(0, 0)
                    if i == 6:
                        h_block_in(1, 1)

                def h_block_in(n, blk):
                    b = p.n["block"] + blk
                    pe.wait_ge(acc_free[b % 2], b // 2 + 1)
                    transpose_block(h[:, :, n * NB:(n + 1) * NB], x_tok, 4 * n)
                unit("quad", yt, y_tok, after)

            def after_pairs(i):
                if i == 0:
                    h_block(2, 2)
                if i == 2:
                    h_block(3, 1)

            def mlp(final):
                def up_after(i):
                    if i == 1:
                        pe.wait_ge(hid_ready, p.bump("hid"))
                        transpose_block(nat, y_tok, up_after.kt)

                def step(first, last):
                    unit("full", xt, x_tok, after_pairs if first else None)
                    up_after.kt = 0
                    unit("full", xt, x_tok, up_after)
                    up_after.kt = 4
                    unit("pair", yt, y_tok, up_after)

                    def last_after(i):
                        if i == 0:
                            h_block(0, 2)
                        if i == 2:
                            h_block(1, 1)
                    unit("pair", yt, y_tok, last_after if last and not final else None)
                step(True, False)
                with pe.Fori(0, CHUNKS - 2) as r:
                    p.enter(r, dict(STEP_RATES, his=0))
                    step(False, False)
                    p.leave(CHUNKS - 2)
                step(False, True)

            attention_and_out(0, lambda i: h_block(3, 1) if i == 2 else None)
            mlp(False)

            def s5_u(k):
                Uc = Ucb[k % 2]
                pe.wait_ge(uc_in[k % 2], 32 * (k // 2 + 1))
                bank = open_tp()
                for q in range(4):
                    for r in range(2):
                        last = pe.transpose(bank[:, (2 * q + r) * J:(2 * q + r + 1) * J],
                                            Uc[:, r, q, :], ident[0:J, 0:J])
                s5_u.token = close_tp(last)

            def s5_x(k):
                wait_tp_read(pe, s5_u.token)
                ETc = ETb[k % 2]
                pe.wait_ge(et_in[k % 2], 16 * (k // 2 + 1))
                bank = open_at()
                for q in range(4):
                    for r in range(2):
                        o = bank[:, (2 * q + r) * 2 * J:(2 * q + r + 1) * 2 * J]
                        last = mm(o, ETc[:, q, r, :], UT[:, :, 4 * k + q, :])
                close_at(last)

            def s5_y(k):
                b = k % 2
                if k == 0:
                    pe.wait_ge(scan_ready, 1)
                pe.wait_ge(ca_in[b], 16 * (k // 2 + 1))
                pe.wait_ge(t_in[b], 16 * (k // 2 + 1))
                bank = open_at()
                for q in range(2):
                    qq = 2 * k + q
                    o = bank[0:J, q * 2 * GW:(q + 1) * 2 * GW]
                    for r in range(2):
                        mm(o, S[:, r, qq, :], CAb[b][:, q, r, :, :], r == 0, False)
                    assert p.n["at"] == at_before_y[0] + k
                    for s in range(2):
                        last = mm(o[:, s * GW:(s + 1) * GW], UT[:, s, qq, :], Tc[:, b, s, q, :], False, s == 1)
                close_at(last)

            def s5_steps(t):
                k, odd = divmod(t - X8_T, 2)
                if 0 <= k < 8:
                    s5_x(k) if odd else s5_u(k)
                if 0 <= t - Y_T < 16:
                    s5_y(t - Y_T)

            def conv_steps(o, i):
                prev = O_UNITS[o - 1] if 0 < o <= 8 else None
                if prev and prev[0] == "gc" and i == 2:
                    wait_freed(pe, p, 1)
                    transpose_block(hn)
                if prev and prev[0] == "gb" and i == 2:
                    wait_freed(pe, p, 1)
                    transpose_block(onat, y_tok, 8 + 4 * prev[1])

            def odd_after(o, i):
                if o == 0:
                    after_pairs(i)
                conv_steps(o, i)
                s5_steps(8 * o + i)

            for o in range(8):
                unit("full", xt, x_tok, lambda i, o=o: odd_after(o, i))
            unit("pair", yt, y_tok, lambda i: odd_after(8, i), kbase=8)
            unit("pair", yt, y_tok, lambda i: odd_after(9, i), kbase=8)
            for b in range(2):
                pe.wait_ge(ge_ready, b + 1)
                transpose_block(yy[:, :, b * NB:(b + 1) * NB], x_tok, 4 * b)
            unit("pair", xt, x_tok)

            pe.wait_ge(ssm_ready, 1)
            transpose_block(sg[:, :, 0:NB], y_tok, 0)

            def gated2(i):
                if i == 2:
                    pe.wait_ge(ssm_ready, 2)
                    transpose_block(sg[:, :, NB:2 * NB], y_tok, 4)
            unit("pair", yt, y_tok, gated2)

            def last_out(i):
                if i == 0:
                    h_block(0, 2)
                if i == 2:
                    h_block(1, 1)
            unit("pair", yt, y_tok, last_out)
            attention_and_out(1, after_pairs)
            mlp(True)

        @block.scalar
        def _(act):
            p = Place()
            p.n = {"half": 0, "unit": 0, "block": 0, "tp": 0, "his": 0, "at": 0}
            steps = [0]

            def link(ins):
                steps[0] += 1
                ins.then_inc(act_step, 1)
                act.wait_ge(act_step, steps[0])

            def split(i):
                if i % 2 == 0:
                    act.wait_ge(raw_landed[i // 2], p.at("unit", 1) * 16)
                if p.n["half"] + i >= RING or p.reg is not None:
                    act.wait_ge(half_used, p.at("half", i - RING + 1))
                act.activation(whi[:, i % RING], raw[:, i // 2, 2 * (i % 2):2 * (i % 2) + 2], ACT.Copy)\
                   .then_inc(hi_ready, 1)

            def unit(kind="full", slot=None):
                for i in range(HALVES):
                    split(i)
                    if slot:
                        slot(i)
                p.bump("half", 8)
                p.bump("unit")
                p.bump("block", UNIT_BLOCKS[kind])

            def scaled(dst, row, func=ACT.Copy, back=1, off=0):
                act.wait_ge(half_used, p.at("half", off))
                act.wait_ge(*((rstd_ready, row + 1) if row < 8 else (rstd8, 1)))
                par = parity(p, back)
                for t in range(TOK):
                    last = act.activation(dst[:, t, :], acc[:, 2 * par + t, :], func, scale=rstd[:, row, t:t + 1])
                last.then_inc(acc_free[par], 1)

            def hi_parts(dst, kt0, row=None):
                for b in range(2):
                    act.wait_ge(tp_full, p.at("tp", 1))
                    bank = tp[:, p.n["tp"] % 2, :]
                    if row is None:
                        last = act.activation(dst[0][:, kt0 + 2 * b:kt0 + 2 * b + 2, :],
                                              bank.rearrange("p (k n) -> p k n", k=2), ACT.Copy)
                    else:
                        for kk in range(2):
                            kt = kt0 + 2 * b + kk
                            last = act.activation(dst[0][:, kt, :], bank[:, kk * L:(kk + 1) * L], ACT.Copy,
                                                  scale=gain[:, row + kt:row + kt + 1])
                    last.then_inc(hi_put, 1)
                    p.bump("his")
                    p.bump("tp")

            def copy_tp(dsts):
                for dst, w in dsts:
                    act.wait_ge(tp_full, p.at("tp", 1))
                    act.activation(dst, tp[:, p.n["tp"] % 2, 0:w], ACT.Copy).then_inc(tp_free[p.n["tp"] % 2], 1)
                    p.bump("tp")

            def flat(t3):
                return t3.rearrange("p a n -> p (a n)")

            def squares(src, n):
                if p.n.get("ssq"):
                    act.wait_ge(ssq_ready, p.n["ssq"])
                p.bump("ssq")
                for t in range(TOK):
                    last = act.activation(junk[:, t], src[:, t, n * NB:(n + 1) * NB], ACT.Square,
                                          accum_out=ssq[:, t, n:n + 1])
                last.then_inc(ssq_ready, 1)

            def root(m, w=2):
                act.wait_ge(var_ready, root_count(m))
                act.activation(nrm[:, 1, 0:w], nrm[:, 0, 0:w], ACT.Sqrt).then_inc(sd_ready, 1)

            def h_squares(n, back):
                wait_freed(act, p, back)
                squares(h, n)

            def at_copy(copies):
                n = p.n["at"]
                act.wait_ge(at_full, n + 1)
                for dst, src in copies(at[:, n % 2, :]):
                    last = act.activation(dst, src, ACT.Copy)
                last.then_inc(at_free[n % 2], 1)
                p.bump("at")

            act.wait_ge(tp_full, 1)
            act.activation(gain[:, 0:112], tp[:, 0, 0:112], ACT.Copy).then_inc(tp_free[0], 1)
            act.wait_ge(tp_full, 2)
            act.activation(gain[:, 112:136], tp[:, 1, 0:24], ACT.Copy).then_inc(tp_free[1], 1)
            p.bump("tp", 2)
            act.wait_ge(tp_free[0], 1)
            for b in range(BLOCKS):
                hi_parts(yt, 4 * b, MEM)

            def s5_param(t):
                if t == 5:
                    at_copy(lambda bank: [(par[:, 0:3, :].rearrange("p k q -> p (k q)"), bank[:, 0:96])])
                    for r in range(2):
                        at_copy(lambda bank: [(s5c[:, r].rearrange("p q c -> p (q c)"), bank)])
                if t == 7:
                    act.wait_ge(s5_par, 1)
                    act.activation(par[:, par_of["sin"], :], par[:, par_of["th"], :], ACT.Sin)
                    act.activation(par[:, par_of["cos"], :], par[:, par_of["ph"], :], ACT.Sin).then_inc(s5_sin, 1)

            def s5_tables(t):
                if t - 4 not in CHUNK_T:
                    return
                k = CHUNK_T.index(t - 4)
                b = k % 2
                if k:
                    act.wait_ge(et_out, 16 * k)
                at_copy(lambda bank: [(ets, bank)])
                n = p.n["at"]
                act.wait_ge(at_free[(n - 1) % 2], (n - 1) // 2 + 1)
                act.dma_start(et_d[:, 2 * k:2 * k + 2].rearrange("p q r w -> p (q r w)"), ets).then_inc(et_out, 16)
                act.dma_start(ca_d[:, 2 * k:2 * k + 2].rearrange("p q r s w -> p (q r s w)"),
                              caz[:, b].rearrange("p q r s w -> p (q r s w)")).then_inc(ca_out[b], 16)
                if k == 0:
                    act.wait_ge(ksb_zero, 1)
                else:
                    act.wait_ge(k_out, 16 * k)
                at_copy(lambda bank: [(ksb[:, :, 112:240], bank[0:GC, :].rearrange("p (g w) -> p g w", g=4))])
                n = p.n["at"]
                act.wait_ge(at_free[(n - 1) % 2], (n - 1) // 2 + 1)
                act.dma_start(k_d.rearrange("c (s k q) w -> c s k (q w)", s=2, q=2)[:, :, k],
                              ksb.rearrange("p (s q) w -> p s (q w)", q=2)).then_inc(k_out, 16)
                if k == 15:
                    act.wait_ge(k_out, 16 * 16)
                    for i in range(T8):
                        act.dma_start(t_d[i * GC:(i + 1) * GC], k_d[:, :, 112 - GC * i:240 - GC * i])\
                           .then_inc(t_out, 16)

            for u in range(4):
                def slot(i, u=u):
                    t = 8 * u + i
                    s5_param(t)
                    s5_tables(t)
                    if u == 0 and i < 4:
                        squares(memt, i)
                    if u == 0 and i == 4:
                        root(0)
                    if u and i == 3:
                        scaled(kvv if u == 2 else kst_nat, 0)
                    if u in (1, 3) and i == 5:
                        if u == 1:
                            copy_tp([(flat(kvk[:, 2 * b:2 * b + 2, :]), 2 * L) for b in range(2)])
                        else:
                            act.wait_ge(tp_full, p.at("tp", 2))
                            copy_tp([(kst[:, b * NB:(b + 1) * NB], 2 * L) for b in range(2)])
                    if i == 6:
                        act.wait_ge(x_in[u], 16)
                        squares(h, u)
                    if i == 7:
                        hi_parts(xt, 4 * u, MIX)
                        if u == 3:
                            n = p.n["tp"]
                            act.wait_ge(tp_free[(n - 4) % 2], (n - 4) // 2 + 1)
                            act.wait_ge(tp_free[(n - 3) % 2], (n - 3) // 2 + 1)
                            act.dma_start(kv_d[0], kst).then_inc(kv_out, 16)
                unit("full", slot)

            def softmax_exp(causal, scale):
                n, m = p.n["at"], p.bump("sm") - 1
                act.wait_ge(sm_max, m + 1)
                for t in range(TOK):
                    c = slice(t * P, t * P + (t + 1) * P) if causal else slice(t * L, (t + 1) * L)
                    last = act.activation(pr[:, m % 2, c], at[:, n % 2, c], ACT.Exp, scale=scale,
                                          bias=smx[:, m % 2, 0, t:t + 1], accum_out=smx[:, m % 2, 1, t:t + 1])
                last.then_inc(at_free[n % 2], 1)
                p.bump("at")

            def copy_turned(hh, w):
                copy_tp([(pT[:, hh % 2, 0:w], w)])

            def hi_head(kt):
                act.wait_ge(tp_full, p.at("tp", 1))
                act.activation(yt[0][:, kt, :], tp[:, p.n["tp"] % 2, 0:L], ACT.Copy).then_inc(hi_put, 1)
                p.bump("his")
                p.bump("tp")

            def fox_slots(g, i):
                if i == 4:
                    softmax_exp(True, 1.0)
                elif 5 <= i <= 7:
                    softmax_exp(True, 1.0)
                    if i >= 6:
                        hi_head(4 * g + i - 6)
                    copy_turned(i - 5, L + P)
                elif i == 8:
                    hi_head(4 * g + 2)
                    copy_turned(3, L + P)
                    hi_head(4 * g + 3)

            def copy_qk(dst):
                copy_tp([(flat(dst[:, 2 * b:2 * b + 2, :]), 2 * L) for b in range(2)])

            def even_slots(e, i):
                prev = E_UNITS[e - 1] if e else None
                if e == 0 and i == 0:
                    act.wait_ge(cst["ff"], 16)
                    act.activation(wffs[0][:, :, :], wff[:, :, :], ACT.Copy).then_inc(ff_hi, 1)
                if e == 0 and i == 2:
                    root(1)
                if e == 0 and i == 3:
                    act.wait_ge(kv_out, 16)
                    scaled(kst.rearrange("p (t n) -> p t n", t=TOK), 0)
                if e == 0 and i == 4:
                    wait_freed(act, p, 1)
                    act.dma_start(kv_d[1], kst).then_inc(kv_out, 16)
                if e == 1 and i == 1:
                    act.wait_ge(ff_z, 1)
                    link(act.activation(lgt[:, 2], lgt[:, 1], ACT.Exp, scale=-1.0))
                    act.activation(lgt[:, 3], lgt[:, 2], ACT.Ln, bias=1.0).then_inc(ff_act, 1)
                    p.bump("at")
                if e == 1 and i == 7:
                    at_copy(lambda bank: [(c8[:, 0, :], bank[0:8, 0:L])])
                two_back = E_UNITS[e - 2] if e >= 2 else None
                if two_back and two_back[0] in ("rq", "rk", "fq", "fk") and i == 1:
                    copy_qk(qT if two_back[0][1] == "q" else kT)
                if prev and prev[0] == "rg" and i < 2:
                    ro_copy(2 + i)
                if two_back and two_back[0] == "fv" and i == 0:
                    fox_slots(two_back[1], 8)
                if prev and i == 3:
                    name = prev[0]
                    if name in ("rq", "rk"):
                        if p.n.get("rot", 0):
                            act.wait_ge(rot_ready, p.n["rot"])
                        scaled(nat, 1)
                        p.bump("rot")
                    elif name == "fq":
                        scaled(nat, 8)
                    elif name == "fk":
                        scaled(nat, 1)
                    elif name in ("rv", "fv"):
                        scaled(vn, 1)
                    else:
                        scaled(gate, 1, ACT.Silu)
                        act.wait_ge(var_ready, 3 + prev[1])
                        act.activation(nrm[:, 1, :], nrm[:, 0, :], ACT.Sqrt).then_inc(sd_ready, 1)
                if prev and prev[0] == "rv":
                    if 4 <= i <= 7:
                        p.bump("at")
                    if i in (6, 7):
                        ro_copy(i - 6)
                if two_back and two_back[0] == "rg" and i == 4:
                    hi_parts(yt, 8 + 4 * two_back[1])
                if prev and prev[0] == "fv":
                    fox_slots(prev[1], i)

            def ro_copy(hh):
                act.wait_ge(tp_full, p.at("tp", 1))
                b = p.n["tp"] % 2
                act.activation(ro[:, :, hh * P:(hh + 1) * P], tp[:, b, 0:L].rearrange("p (t n) -> p t n", t=TOK),
                               ACT.Copy).then_inc(tp_free[b], 1)
                p.bump("tp")

            for e in range(len(E_UNITS)):
                def slot(i, e=e):
                    s5_tables(8 * (e + 4) + i)
                    even_slots(e, i)
                unit("full", slot)

            def out_slots(n, i):
                if n == 0:
                    if i == 3:
                        scaled(vn, 1)
                    if i == 1:
                        copy_qk(kT)
                    fox_slots(1, i)
                if n == 1 and i == 0:
                    fox_slots(1, 8)
                if n and i == 4:
                    h_squares(n - 1, 1)
                if n and i == 5:
                    hi_parts(xt, 4 * (n - 1), XAT)

            for n in range(BLOCKS):
                unit("full", lambda i, n=n: out_slots(n, i))

            def cross(layer, row):
                scaled(nat, row)
                copy_qk(qT)
                for hh in range(4):
                    softmax_exp(False, SCALE)
                    if hh:
                        copy_turned(hh - 1, 2 * L)
                        hi_head(hh - 1)
                copy_turned(3, 2 * L)
                hi_head(3)

            def pair_slots(i, row):
                if i == 2:
                    h_squares(2, 2)
                if i == 3:
                    hi_parts(xt, 8, row)
                if i == 4:
                    h_squares(3, 1)
                if i == 5:
                    hi_parts(xt, 12, row)

            def attention_and_out(layer, first, row, mlp_row):
                unit("full", first)

                def slot(i):
                    if i == 3:
                        cross(layer, row)
                    for n in range(2):
                        if i == 5 + 2 * n:
                            b = p.n["block"] + n
                            act.wait_ge(acc_free[b % 2], b // 2 + 1)
                            squares(h, n)
                    if i == 7:
                        hi_parts(xt, 0, mlp_row)
                unit("quad", slot)

            def mlp(layer, row, next_row, final):
                def up_slot(kt):
                    def slot(i):
                        if i == 3:
                            scaled(nat, row, ACT.Relu)
                        if i == 5:
                            hi_parts(yt, kt)
                    return slot

                def step(first, last):
                    def s0(i):
                        if first:
                            if i == 1:
                                hi_parts(xt, 4, MLP + 16 * layer)
                            pair_slots(i, MLP + 16 * layer)
                            if i == 6:
                                root(row)
                    unit("full", s0)
                    unit("full", up_slot(0))
                    unit("pair", up_slot(4))

                    def s3(i):
                        if not last:
                            return
                        if i == 2:
                            h_squares(0, 2)
                        if i == 4:
                            h_squares(1, 1)
                        if not final and i in (3, 5):
                            hi_parts(xt, 0 if i == 3 else 4, next_row)
                    unit("pair", s3)
                step(True, False)
                with act.Fori(0, CHUNKS - 2) as r:
                    p.enter(r, dict(STEP_RATES, hid=0))
                    step(False, False)
                    p.leave(CHUNKS - 2)
                step(False, True)

            def xq_first(i):
                if i == 4:
                    h_squares(3, 1)
                if i == 5:
                    hi_parts(xt, 12, XAT)
                if i == 6:
                    root(2)
            attention_and_out(0, xq_first, 2, MLP)
            mlp(0, 3, MIX + 16, False)

            def s5_slots(t):
                k, odd = divmod(t - 4 - X8_T, 2)
                if 0 <= k < 8 and not odd:
                    act.wait_ge(tp_full, p.at("tp", 1))
                    b = p.n["tp"] % 2
                    act.activation(UT[:, :, 4 * k:4 * k + 4, :], tp[:, b, 0:2 * 4 * J].rearrange(
                        "p (q r j) -> p r q j", q=4, r=2), ACT.Copy).then_inc(tp_free[b], 1)
                    p.bump("tp")
                if 0 <= k < 8 and odd:
                    at_copy(lambda bank: [
                        (S[64 * s:64 * s + 64, :, 4 * k:4 * k + 4, 1:J],
                         bank[64 * s:64 * s + 64, :].rearrange("p (q r s j) -> p s r q j", q=4, r=2, s=2)[
                             :, s, :, :, 0:J - 1]) for s in range(2)])
                k = t - 4 - Y_T
                if 0 <= k < 16:
                    b = k % 2
                    if k >= 2:
                        act.wait_ge(y_out[b], 32 * (k // 2))
                    at_copy(lambda bank: [
                        (Yc[:, b, :, :, q * GC:(q + 1) * GC], bank[0:J, q * 2 * GW:(q + 1) * 2 * GW].rearrange(
                            "p (s i c) -> p i s c", s=2, i=T8)) for q in range(2)])
                    n = p.n["at"] - 1
                    act.wait_ge(at_free[n % 2], n // 2 + 1)
                    for s in range(2):
                        act.dma_start(y_d.rearrange("(j i) (s n) -> s j i n", i=T8, s=2)[
                            s, :, :, 2 * GC * k:2 * GC * (k + 1)], Yc[:, b, :, s, :]).then_inc(y_out[b], 16)

            def odd_slots(o, i):
                if o == 0:
                    pair_slots(i, MIX + 16)
                    if i == 6:
                        root(4)
                prev = O_UNITS[o - 1] if 1 <= o <= 8 else None
                if prev and i == 3:
                    if prev[0] == "u":
                        if prev[1]:
                            act.wait_ge(u_out, 48)
                        scaled(onat, 4)
                    elif prev[0] == "h":
                        scaled(hn, 4)
                    elif prev[0] == "gb":
                        if prev[1] == 0:
                            act.wait_ge(u_out, 96)
                        scaled(onat, 4)
                if prev and prev[0] == "gc" and i == 5:
                    copy_tp([(flat(zT[:, 2 * b:2 * b + 2, :]), 2 * L) for b in range(2)])
                if prev and prev[0] == "gb" and i == 6:
                    for b in range(2):
                        act.wait_ge(gb_prod, 2 * prev[1] + b + 1)
                        act.activation(yt[0][:, 8 + 4 * prev[1] + 2 * b:8 + 4 * prev[1] + 2 * b + 2, :],
                                       cv[:, 2 * b:2 * b + 2, :], ACT.Copy).then_inc(hi_put, 1)
                        p.bump("his")
                        p.bump("tp")
                s5_slots(8 * o + i)

            for o in range(8):
                unit("full", lambda i, o=o: odd_slots(o, i))
            for o in (8, 9):
                unit("pair", lambda i, o=o: odd_slots(o, i))

            def glu_slots(i):
                odd_slots(10, i)
                if i == 3:
                    for b in range(2):
                        act.wait_ge(y_ready, b + 1)
                        act.activation(yy[:, :, b * NB:(b + 1) * NB], yy[:, :, b * NB:(b + 1) * NB],
                                       ACT.Gelu_apprx_tanh).then_inc(ge_ready, 1)
                    for b in range(2):
                        hi_parts(xt, 4 * b)
            unit("pair", glu_slots)

            def gate_slots(i):
                if i in (1, 3):
                    b = i // 2
                    act.wait_ge(half_used, p.at("half", -2 if b == 0 else 0))
                    par_ = parity(p, 2 - b)
                    for t in range(TOK):
                        last = act.activation(sg[:, t, b * NB:(b + 1) * NB], acc[:, 2 * par_ + t, :], ACT.Sigmoid)
                    last.then_inc(acc_free[par_], 1)
                if i == 3:
                    hi_parts(yt, 0)
                if i == 5:
                    hi_parts(yt, 4)
            unit("pair", gate_slots)

            def last_slots(i):
                if i == 2:
                    h_squares(0, 2)
                if i == 4:
                    h_squares(1, 1)
                if i in (3, 5):
                    hi_parts(xt, 0 if i == 3 else 4, XAT + 16)
            unit("pair", last_slots)

            def xq1_first(i):
                pair_slots(i, XAT + 16)
                if i == 6:
                    root(5)
            attention_and_out(1, xq1_first, 5, MLP + 16)
            mlp(1, 6, None, True)
            act.wait_ge(half_used, p.at("half", -2))
            h_squares(2, 2)
            h_squares(3, 1)
            root(7)

        @block.vector
        def _(dve):
            p = Place()
            p.n = {"half": 0, "unit": 0, "block": 0, "tp": 0, "his": 0, "at": 0, "hid": 0}
            steps = [0]

            def link(ins):
                steps[0] += 1
                ins.then_inc(dve_step, 1)
                dve.wait_ge(dve_step, steps[0])

            def unit(kind="full", slot=None):
                for i in range(HALVES):
                    dve.wait_ge(hi_ready, p.at("half", i + 1))
                    dve.tensor_tensor(wlo[:, i % RING], raw[:, i // 2, 2 * (i % 2):2 * (i % 2) + 2],
                                      whi[:, i % RING].bitcast(F32), ALU.subtract).then_inc(lo_ready, 1)
                    if slot:
                        slot(i)
                p.bump("half", 8)
                p.bump("unit")
                p.bump("block", UNIT_BLOCKS[kind])

            def lo_parts(dst, kt0, row=None, src=None):
                for b in range(2):
                    dve.wait_ge(hi_put, p.at("his", 1))
                    bk = p.n["tp"] % 2
                    kt = kt0 + 2 * b
                    if row is None:
                        v = tp[:, bk, :].rearrange("p (k n) -> p k n", k=2) if src is None else src[:, 2 * b:2 * b + 2, :]
                        last = dve.tensor_tensor(dst[1][:, kt:kt + 2, :], v, dst[0][:, kt:kt + 2, :].bitcast(F32),
                                                 ALU.subtract)
                    else:
                        for kk in range(2):
                            last = dve.scalar_tensor_tensor(
                                out=dst[1][:, kt + kk, :], in0=tp[:, bk, kk * L:(kk + 1) * L],
                                scalar=gain[:, row + kt + kk:row + kt + kk + 1],
                                in1=dst[0][:, kt + kk, :].bitcast(F32), op0=ALU.mult, op1=ALU.subtract)
                    last.then_inc(tp_free[bk], 1)
                    p.bump("his")
                    p.bump("tp")

            def add_block(n, blk_back, off):
                dve.wait_ge(half_used, p.at("half", off))
                par_ = parity(p, blk_back)
                for t in range(TOK):
                    hb = h[:, t, n * NB:(n + 1) * NB]
                    last = dve.tensor_tensor(hb, acc[:, 2 * par_ + t, :], hb, ALU.add)
                last.then_inc(acc_free[par_], 1)

            def mean_square(m):
                dve.wait_ge(ssq_ready, 4 * (m + 1))
                link(dve.tensor_reduce(nrm[:, 2, 0:2], ssq[:, :, :], AX.X, ALU.add))
                dve.tensor_scalar(nrm[:, 0, 0:2], nrm[:, 2, 0:2], 1.0 / D, EPS, ALU.mult, ALU.add)\
                   .then_inc(var_ready, 1)

            def inverse_root(dst, w, count):
                dve.wait_ge(sd_ready, count)
                link(dve.reciprocal(nrm[:, 2, 0:w], nrm[:, 1, 0:w]))
                link(dve.tensor_tensor(nrm[:, 3, 0:w], nrm[:, 2, 0:w], nrm[:, 2, 0:w], ALU.mult))
                link(dve.tensor_tensor(nrm[:, 3, 0:w], nrm[:, 3, 0:w], nrm[:, 0, 0:w], ALU.mult))
                link(dve.tensor_scalar(nrm[:, 3, 0:w], nrm[:, 3, 0:w], -0.5, 1.5, ALU.mult, ALU.add))
                return dve.tensor_tensor(dst, nrm[:, 2, 0:w], nrm[:, 3, 0:w], ALU.mult)

            def rms(m, count):
                inverse_root(rstd[:, m, :], 2, count).then_inc(rstd_ready, 1)

            dve.wait_ge(tp_free[0], 1)
            dve.wait_ge(tp_free[1], 1)
            p.bump("tp", 2)
            for b in range(BLOCKS):
                lo_parts(yt, 4 * b, MEM)

            def re_tables(t):
                if t not in DVE_T:
                    return
                k = DVE_T.index(t)
                b, q0 = k % 2, 2 * k
                if k == 0:
                    dve.wait_ge(s5_pw, 1)
                if k >= 2:
                    dve.wait_ge(at_full, 3 + 2 * (k - 1))
                    dve.wait_ge(ca_out[b], 16 * (k // 2))
                e = etab[:, b, :, 0, :].rearrange("p q (i c) -> p q i c", i=T8)
                br, bi, pbr, pbi = table_parts(s5b, pb, q0, T8)
                tv = vtmp[:, 0:2 * GW].rearrange("p (q i c) -> p q i c", q=2, i=T8)
                link(dve.tensor_tensor(e, br, pbr, ALU.mult))
                link(dve.tensor_tensor(tv, bi, pbi, ALU.mult))
                link(dve.tensor_tensor(e, e, tv, ALU.subtract))
                cr, ci, pr_, pi_ = table_parts(s5c, pw, q0, 9)
                t1 = vtmp2.rearrange("p (q i c) -> p q i c", q=2, i=9)
                t2 = vtmp.rearrange("p (q i c) -> p q i c", q=2, i=9)
                link(dve.tensor_tensor(t1, cr, pr_, ALU.mult))
                link(dve.tensor_tensor(t2, ci, pi_, ALU.mult))
                for s in range(2):
                    ln = slice(64 * s, 64 * s + 64)
                    last = dve.tensor_tensor(
                        caz[ln, b, :, 0, s, :].rearrange("p q (i c) -> p q i c", i=9), t1[ln], t2[ln], ALU.add)
                last.then_inc(s5_re, 1)

            for u in range(4):
                def slot(i, u=u):
                    t = 8 * u + i
                    if u == 0 and i == 4:
                        mean_square(0)
                    if u == 0 and i == 5:
                        rms(0, 1)
                    if u == 0 and i == 5:
                        p.bump("at", 3)
                    if t == 6:
                        dve.wait_ge(s5_lam, 1)
                        dve.reciprocal(par[:, par_of["t2"], :], par[:, par_of["t1"], :]).then_inc(s5_inv, 1)
                    if u in (1, 3) and i == 5:
                        p.bump("tp", 2)
                    if i == 7:
                        lo_parts(xt, 4 * u, MIX)
                    re_tables(t)
                    s5_at(t)

                def s5_at(t):
                    if t - 4 in CHUNK_T:
                        p.bump("at", 2)
                unit("full", slot)

            def softmax_max(causal, scale):
                n, m = p.n["at"], p.bump("sm") - 1
                dve.wait_ge(at_full, n + 1)
                for t in range(TOK):
                    c = slice(t * P, t * P + (t + 1) * P) if causal else slice(t * L, (t + 1) * L)
                    last = dve.tensor_reduce(smx[:, m % 2, 2, t:t + 1], at[:, n % 2, c], AX.X, ALU.max)
                link(last)
                dve.tensor_scalar(smx[:, m % 2, 0, :], smx[:, m % 2, 2, :], -scale, None, ALU.mult)\
                   .then_inc(sm_max, 1)

            def softmax_norm(causal):
                n, m = p.n["at"], p.n["sm"] - 1
                dve.wait_ge(at_free[n % 2], n // 2 + 1)
                link(dve.reciprocal(smx[:, m % 2, 2, :], smx[:, m % 2, 1, :]))
                for t in range(TOK):
                    c = slice(t * P, t * P + (t + 1) * P) if causal else slice(t * L, (t + 1) * L)
                    last = dve.tensor_scalar(pr[:, m % 2, c], pr[:, m % 2, c], smx[:, m % 2, 2, t:t + 1], None,
                                             ALU.mult)
                last.then_inc(sm_p, 1)
                p.bump("at")

            def lo_head(kt):
                p.bump("tp")
                dve.wait_ge(hi_put, p.at("his", 1))
                b = p.n["tp"] % 2
                dve.tensor_tensor(yt[1][:, kt, :], tp[:, b, 0:L], yt[0][:, kt, :].bitcast(F32), ALU.subtract)\
                   .then_inc(tp_free[b], 1)
                p.bump("his")
                p.bump("tp")

            def fox_slots(g, i):
                if 4 <= i <= 7:
                    softmax_max(True, 1.0)
                    softmax_norm(True)
                    if i >= 6:
                        lo_head(4 * g + i - 6)
                elif i == 8:
                    lo_head(4 * g + 2)
                    lo_head(4 * g + 3)

            def decay(g, hh):
                n = p.n["at"]
                dve.wait_ge(at_full, n + 1)
                dve.wait_ge(dec_in[hh % 2], 16 * (2 * g + hh // 2 + 1))
                dve.tensor_tensor(pT[:, hh % 2, 0:L + P], at[:, n % 2, 0:L + P], dec[:, hh % 2, :], ALU.mult)\
                   .then_inc(at_free[n % 2], 1)
                p.bump("at")

            def ro_stats(hh):
                n = p.n["tp"]
                dve.wait_ge(tp_free[n % 2], n // 2 + 1)
                for t in range(TOK):
                    last = dve.bn_stats(stat[:, 4 * t + hh, :], ro[:, t, hh * P:(hh + 1) * P])
                p.bump("tp")
                if hh == 3:
                    link(last)
                    for k in range(8):
                        last = dve.bn_aggr(mv[:, k, :], stat[:, k, :])
                    link(last)
                    dve.tensor_scalar(nrm[:, 0, :], mv[:, :, 1], EPS, None, ALU.add).then_inc(var_ready, 1)

            def even_slots(e, i):
                prev = E_UNITS[e - 1] if e else None
                two_back = E_UNITS[e - 2] if e >= 2 else None
                if e == 0 and i == 1:
                    dve.wait_ge(ff_hi, 1)
                    dve.tensor_tensor(wffs[1][:, :, :], wff[:, :, :], wffs[0][:, :, :].bitcast(F32),
                                      ALU.subtract).then_inc(ff_split, 1)
                    mean_square(1)
                if e == 0 and i == 3:
                    rms(1, 2)
                    dve.wait_ge(rstd_ready, 2)
                    dve.tensor_scalar(rstd[:, 8, :], rstd[:, 1, :], SCALE, None, ALU.mult).then_inc(rstd8, 1)
                if e == 1 and i == 0:
                    n = p.n["at"]
                    dve.wait_ge(at_full, n + 1)
                    dve.wait_ge(cst["cst"], 64)
                    for t in range(TOK):
                        last = dve.scalar_tensor_tensor(
                            out=lgt[:, 0, t, :], in0=at[:, n % 2, t * 8:(t + 1) * 8], scalar=rstd[:, 1, t:t + 1],
                            in1=bfor[:, :], op0=ALU.mult, op1=ALU.add)
                    last.then_inc(at_free[n % 2], 1)
                    p.bump("at")
                    dve.wait_ge(at_free[n % 2], n // 2 + 1)
                    dve.scalar_tensor_tensor(out=lgt[:, 1], in0=lgt[:, 0], scalar=-1.0, in1=lgt[:, 0],
                                             op0=ALU.mult, op1=ALU.max).then_inc(ff_z, 1)
                if e == 1 and i == 2:
                    dve.wait_ge(ff_act, 1)
                    dve.scalar_tensor_tensor(out=lgt[:, 0], in0=lgt[:, 0], scalar=0.0, in1=lgt[:, 3],
                                             op0=ALU.min, op1=ALU.subtract).then_inc(ff_log, 1)
                if e == 2 and i == 0:
                    n = p.n["at"]
                    dve.wait_ge(at_free[n % 2], n // 2 + 1)
                    dve.tensor_scalar(c8[:, 1, :], c8[:, 0, :], -1.0, None, ALU.mult).then_inc(c_ready, 1)
                    p.bump("at")
                if prev and prev[0] == "rg" and i < 2:
                    ro_stats(2 + i)
                if two_back and two_back[0] in ("rq", "rk", "fq", "fk") and i == 1:
                    p.bump("tp", 2)
                if two_back and two_back[0] == "fv" and i == 0:
                    fox_slots(two_back[1], 8)
                if prev and prev[0] == "rg" and i == 4:
                    inverse_root(mv[:, :, 1], 8, 3 + prev[1]).then_inc(ro_stat, 1)
                if prev and prev[0] == "rv":
                    if i in (6, 7):
                        ro_stats(i - 6)
                    if 4 <= i <= 7:
                        decay(prev[1], i - 4)
                if two_back and two_back[0] == "rg" and i == 4:
                    lo_parts(yt, 8 + 4 * two_back[1])
                if prev and prev[0] == "fv":
                    fox_slots(prev[1], i)

            for e in range(len(E_UNITS)):
                def slot(i, e=e):
                    t = 8 * (e + 4) + i
                    if t - 4 in CHUNK_T:
                        p.bump("at", 2)
                    even_slots(e, i)
                    re_tables(t)
                unit("full", slot)

            def out_slots(n, i):
                if n == 0:
                    if i == 1:
                        p.bump("tp", 2)
                    fox_slots(1, i)
                if n == 1 and i == 0:
                    fox_slots(1, 8)
                if n and i == 3:
                    add_block(n - 1, 1, 0)
                if n and i == 6:
                    lo_parts(xt, 4 * (n - 1), XAT)

            for n in range(BLOCKS):
                unit("full", lambda i, n=n: out_slots(n, i))

            def cross():
                p.bump("tp", 2)
                softmax_max(False, SCALE)
                for hh in range(4):
                    softmax_norm(False)
                    if hh < 3:
                        softmax_max(False, SCALE)
                    if hh:
                        lo_head(hh - 1)
                lo_head(3)

            def pair_slots(i, row):
                if i == 1:
                    add_block(2, 2, -2)
                if i == 3:
                    add_block(3, 1, 0)
                if i == 4:
                    lo_parts(xt, 8, row)
                if i == 6:
                    lo_parts(xt, 12, row)

            def attention_and_out(layer, first, mlp_row):
                unit("full", first)

                def slot(i):
                    if i == 3:
                        cross()
                    for n in range(2):
                        if i == 5 + 2 * n:
                            add_block(n, -n, 2 * n + 2)
                    if i == 7:
                        lo_parts(xt, 0, mlp_row)
                unit("quad", slot)

            def mlp(layer, m, next_row, final):
                def up_slot(kt):
                    def slot(i):
                        if i == 3:
                            wait_freed(dve, p, 1)
                            dve.tensor_tensor(nat, nat, nat, ALU.mult).then_inc(hid_ready, 1)
                            p.bump("hid")
                        if i == 5:
                            lo_parts(yt, kt)
                    return slot

                def step(first, last):
                    def s0(i):
                        if first:
                            if i == 1:
                                lo_parts(xt, 4, MLP + 16 * layer)
                            pair_slots(i, MLP + 16 * layer)
                            if i == 6:
                                mean_square(m)
                            if i == 7:
                                rms(m, root_count(m))
                        else:
                            if i == 1:
                                add_block(2, 2, -2)
                            if i == 3:
                                add_block(3, 1, 0)
                    unit("full", s0)
                    unit("full", up_slot(0))
                    unit("pair", up_slot(4))

                    def s3(i):
                        if i == 1:
                            add_block(0, 2, -2)
                        if i == 3:
                            add_block(1, 1, 0)
                        if last and not final and i in (4, 6):
                            lo_parts(xt, 0 if i == 4 else 4, next_row)
                    unit("pair", s3)
                step(True, False)
                with dve.Fori(0, CHUNKS - 2) as r:
                    p.enter(r, dict(STEP_RATES))
                    step(False, False)
                    p.leave(CHUNKS - 2)
                step(False, True)

            def xq_first(i):
                if i == 3:
                    add_block(3, 1, 0)
                if i == 6:
                    lo_parts(xt, 12, XAT)
                    mean_square(2)
                if i == 7:
                    rms(2, root_count(2))
            attention_and_out(0, xq_first, MLP)
            mlp(0, 3, MIX + 16, False)

            def convolve(g):
                n = p.n["tp"]
                for b in range(2):
                    dve.wait_ge(tp_free[(n + b) % 2], (n + b) // 2 + 1)
                for s in range(3):
                    for k in range(4):
                        w = gain[:, 112 + (2 - s) * 8 + 4 * g + k:112 + (2 - s) * 8 + 4 * g + k + 1]
                        if s == 0:
                            last = dve.tensor_scalar(cv[:, k, :], zT[:, k, :], w, None, ALU.mult)
                        else:
                            last = dve.scalar_tensor_tensor(
                                out=cv[:, k, s:], in0=zT[:, k, 0:L - s], scalar=w, in1=cv[:, k, s:],
                                op0=ALU.mult, op1=ALU.add)
                    link(last)
                p.bump("tp", 2)

            def odd_slots(o, i):
                t = 8 * o + i
                if o == 0:
                    pair_slots(i, MIX + 16)
                    if i == 6:
                        mean_square(4)
                    if i == 7:
                        rms(4, root_count(4))
                prev = O_UNITS[o - 1] if 1 <= o <= 8 else None
                if prev and prev[0] == "gc" and i == 3:
                    dve.wait_ge(half_used, p.at("half"))
                    wait_freed(dve, p, 2)
                    par_ = parity(p, 1)
                    for tt in range(TOK):
                        last = dve.scalar_tensor_tensor(
                            out=hn[:, tt, :], in0=acc[:, 2 * par_ + tt, :], scalar=rstd[:, 4, tt:tt + 1],
                            in1=hn[:, tt, :], op0=ALU.mult, op1=ALU.mult)
                    last.then_inc(acc_free[par_], 1)
                if prev and prev[0] == "gc" and i == 6:
                    convolve(prev[1])
                if prev and prev[0] == "gb" and i == 5:
                    n = p.n["tp"]
                    for b in range(2):
                        dve.wait_ge(tp_full, n + b + 1)
                        dve.tensor_tensor(cv[:, 2 * b:2 * b + 2, :], tp[:, (n + b) % 2, :].rearrange(
                            "p (k n) -> p k n", k=2), cv[:, 2 * b:2 * b + 2, :], ALU.mult).then_inc(gb_prod, 1)
                if prev and prev[0] == "gb" and i == 7:
                    lo_parts(yt, 8 + 4 * prev[1], src=cv)
                k, odd = divmod(t - 4 - X8_T, 2)
                if 0 <= k < 8:
                    p.bump("at" if odd else "tp")
                if 0 <= t - 4 - Y_T < 16:
                    p.bump("at")

            for o in range(8):
                unit("full", lambda i, o=o: odd_slots(o, i))
            unit("pair", lambda i: odd_slots(8, i))

            def conv_adds(i, n):
                if i in (1, 3):
                    add_block(n + i // 2, 2 - i // 2, -2 if i == 1 else 0)

            def second(i):
                odd_slots(9, i)
                conv_adds(i, 0)
            unit("pair", second)

            def glu_slots(i):
                odd_slots(10, i)
                conv_adds(i, 2)
                if i == 3:
                    dve.wait_ge(y_in, 32)
                    dve.wait_ge(cst["dsk"], 16)
                    for t in range(TOK):
                        last = dve.tensor_tensor(uu[:, t, :], uu[:, t, :], dsk, ALU.mult)
                    link(last)
                    for b in range(2):
                        c = slice(b * NB, (b + 1) * NB)
                        dve.tensor_tensor(yy[:, :, c], yy[:, :, c], uu[:, :, c], ALU.add).then_inc(y_ready, 1)
                    for b in range(2):
                        lo_parts(xt, 4 * b)
            unit("pair", glu_slots)

            def gate_slots(i):
                if i in (1, 3):
                    b = i // 2
                    c = slice(b * NB, (b + 1) * NB)
                    wait_freed(dve, p, 2 - b)
                    dve.tensor_tensor(sg[:, :, c], sg[:, :, c], yy[:, :, c], ALU.mult).then_inc(ssm_ready, 1)
                if i == 3:
                    lo_parts(yt, 0)
                if i == 5:
                    lo_parts(yt, 4)
            unit("pair", gate_slots)

            def last_slots(i):
                if i == 1:
                    add_block(0, 2, -2)
                if i == 3:
                    add_block(1, 1, 0)
                if i in (4, 6):
                    lo_parts(xt, 0 if i == 4 else 4, XAT + 16)
            unit("pair", last_slots)

            def xq1_first(i):
                pair_slots(i, XAT + 16)
                if i == 6:
                    mean_square(5)
                if i == 7:
                    rms(5, root_count(5))
            attention_and_out(1, xq1_first, MLP + 16)
            mlp(1, 6, None, True)

            add_block(2, 2, -2)
            add_block(3, 1, 0)
            mean_square(7)
            rms(7, root_count(7))
            dve.wait_ge(rstd_ready, 8)
            dve.wait_ge(cst["gf"], 16)
            for b in range(BLOCKS):
                c = slice(b * NB, (b + 1) * NB)
                for t in range(TOK):
                    last = dve.scalar_tensor_tensor(out=fin[:, t, c], in0=h[:, t, c], scalar=rstd[:, 7, t:t + 1],
                                                    in1=gfin[:, c], op0=ALU.mult, op1=ALU.mult)
                last.then_inc(fin_ready, 1)

        @block.gpsimd
        def _(pool):
            steps = [0]

            def link(ins):
                steps[0] += 1
                ins.then_inc(pool_step, 1)
                pool.wait_ge(pool_step, steps[0])

            def tt(o, a, b, op):
                link(pool.tensor_tensor(o, a, b, op))

            def ts(o, a, s1, s2, op0, op1=None):
                if s2 is None:
                    link(pool.tensor_scalar(o, a, s1, None, op0))
                else:
                    link(pool.tensor_scalar(o, a, s1, s2, op0, op1))

            def wait_block(b):
                pool.wait_ge(acc_free[b % 2], b // 2 + 1)

            for v, src in enumerate((s5_a_re, s5_a_im, s5_log_step)):
                pool.dma_start(s5row[32 * v:32 * v + 32, :].rearrange("q (s p) -> q s p", s=2),
                               src[0].rearrange("(s q) p -> q s p", s=2)).then_inc(cst["s5"], 16)
            for r, src in enumerate((s5_b_re, s5_b_im)):
                for s in range(2):
                    pool.dma_start(s5b[64 * s:64 * s + 64, r], src[0].rearrange(
                        "(s q) p c -> s p q c", s=2)[s]).then_inc(cst["s5"], 16)
            for r, src in enumerate((s5_c_re, s5_c_im)):
                v = src[0].rearrange("(s t q) c p -> t s (q c) p", s=2, t=4)
                for t in range(4):
                    ins = pool.dma_start(craw[:, r, t, :].rearrange("p (s k) -> p s k", s=2),
                                         v[t].rearrange("s m p -> m s p"))
                    ins.then_inc(cst["s5"], 16)
            pool.dma_start(wff[:, :, :], ab_w_in[0][:, 3 * FW:3 * FW + 8].rearrange("(k p) n -> p k n", p=P))\
                .then_inc(cst["ff"], 16)
            pool.dma_start(trit[:, :], tri).then_inc(cst["tri"], 16)

            T = {n: par[:, i, :] for n, i in par_of.items()}
            X = [ptmp[:, i, :] for i in range(16)]
            pool.wait_ge(at_free[0], 1)

            def exp_into(o, v, tmp):
                k, r, y, t = tmp
                ts(k, v, 1.4426950408889634, 12582912.0, ALU.mult, ALU.add)
                ts(k, k, -12582912.0, None, ALU.add)
                ts(k, k, 128.0, -127.0, ALU.min, ALU.max)
                ts(t, k, -0.693145751953125, None, ALU.mult)
                tt(r, v, t, ALU.add)
                ts(t, k, -1.4286068203094172e-06, None, ALU.mult)
                tt(r, r, t, ALU.add)
                ts(r, r, 1.0, -1.0, ALU.min, ALU.max)
                ts(y, r, 1.0 / 5040, 1.0 / 720, ALU.mult, ALU.add)
                for c in (1.0 / 120, 1.0 / 24, 1.0 / 6, 0.5, 1.0, 1.0):
                    tt(y, y, r, ALU.mult)
                    ts(y, y, c, None, ALU.add)
                ts(k, k, 127.0, 8388608.0, ALU.add, ALU.mult)
                link(pool.tensor_copy(t.bitcast(I32), k))
                tt(o, y, t, ALU.mult)

            def reduce_angle(o, v, tmp):
                k, t = tmp
                ts(k, v, 0.15915494309189535, 12582912.0, ALU.mult, ALU.add)
                ts(k, k, -12582912.0, None, ALU.add)
                prev = v
                for part in (6.28125, 0.0019350051879882812, 3.019916050561733e-07):
                    ts(t, k, -part, None, ALU.mult)
                    tt(o, prev, t, ALU.add)
                    prev = o

            ts(T["lre"], T["lre"], -1e-4, None, ALU.min)
            exp_into(T["step"], T["ls"], X[0:4])
            tt(X[4], T["lre"], T["step"], ALU.mult)
            exp_into(T["mag"], X[4], X[0:4])
            tt(X[4], T["lim"], T["step"], ALU.mult)
            reduce_angle(T["th"], X[4], X[0:2])
            ts(T["th"], T["th"], 3.1415925, -3.1415925, ALU.min, ALU.max)
            ts(X[5], T["th"], 1.5707963267948966, None, ALU.add)
            ts(X[6], X[5], 3.141592653589793, -6.283185307179586, ALU.is_gt, ALU.mult)
            tt(X[5], X[5], X[6], ALU.add)
            ts(T["ph"], X[5], 3.1415925, -3.1415925, ALU.min, ALU.max)
            tt(X[7], T["lre"], T["lre"], ALU.mult)
            tt(X[8], T["lim"], T["lim"], ALU.mult)
            pool.tensor_tensor(T["t1"], X[7], X[8], ALU.add).then_inc(s5_lam, 1)
            pool.wait_ge(s5_lam, 1)
            ts(X[9], T["ph"], 1.0, None, ALU.mult)
            pool.tensor_copy(X[10], T["th"]).then_inc(s5_par, 1)
            pool.wait_ge(s5_sin, 1)
            pool.wait_ge(s5_inv, 1)
            a_re, a_im = X[11], X[12]
            tt(a_re, T["mag"], T["cos"], ALU.mult)
            tt(a_im, T["mag"], T["sin"], ALU.mult)
            ts(X[0], a_re, -1.0, None, ALU.add)
            tt(X[1], X[0], T["lre"], ALU.mult)
            tt(X[2], a_im, T["lim"], ALU.mult)
            tt(X[1], X[1], X[2], ALU.add)
            tt(X[1], X[1], T["t2"], ALU.mult)
            tt(X[2], a_im, T["lre"], ALU.mult)
            tt(X[3], X[0], T["lim"], ALU.mult)
            tt(X[2], X[2], X[3], ALU.subtract)
            tt(X[2], X[2], T["t2"], ALU.mult)
            link(pool.tensor_copy(pb[:, 0, 7, :], X[1]))
            link(pool.tensor_copy(pb[:, 1, 7, :], X[2]))

            def times(o, v, re, im):
                tt(X[4], v[:, 0], re, ALU.mult)
                tt(X[5], v[:, 1], im, ALU.mult)
                tt(X[6], v[:, 0], im, ALU.mult)
                tt(X[7], v[:, 1], re, ALU.mult)
                tt(o[:, 0], X[4], X[5], ALU.subtract)
                tt(o[:, 1], X[6], X[7], ALU.add)

            for k in range(6, -1, -1):
                times(pb[:, :, k, :], pb[:, :, k + 1, :], a_re, a_im)
            link(pool.memset(pw[:, 0, 0, :], 1.0))
            link(pool.memset(pw[:, 1, 0, :], 0.0))
            for k in range(1, 9):
                times(pw[:, :, k, :], pw[:, :, k - 1, :], a_re, a_im)
            for r in range(2):
                link(pool.tensor_copy(a8[:, r, 0, :], pw[:, r, 8, :]))
            for k in range(1, T8):
                times(a8[:, :, k, :], a8[:, :, k - 1, :], a8[:, 0, 0, :], a8[:, 1, 0, :])
            ts(pw[:, 1, :, :], pw[:, 1, :, :], -1.0, None, ALU.mult)
            pool.wait_ge(tp_full, 2 + 2 * BLOCKS)
            pool.wait_ge(ssq_ready, BLOCKS)
            pool.memset(ksb[:, :, 0:112], 0.0).then_inc(ksb_zero, 1)
            link(pool.memset(caz[:, :, :, :, :, :], 0.0))
            pool.memset(X[0], 0.0).then_inc(s5_pw, 1)

            for k in range(16):
                b, q0 = k % 2, 2 * k
                if k >= 2:
                    pool.wait_ge(at_full, 3 + 2 * (k - 1))
                    pool.wait_ge(ca_out[b], 16 * (k // 2))
                e = etab[:, b, :, 1, :].rearrange("p q (i c) -> p q i c", i=T8)
                br, bi, pbr, pbi = table_parts(s5b, pb, q0, T8)
                tv = gtmp[:, 0:2 * GW].rearrange("p (q i c) -> p q i c", q=2, i=T8)
                tt(e, br, pbi, ALU.mult)
                tt(tv, bi, pbr, ALU.mult)
                tt(e, e, tv, ALU.add)
                cr, ci, pr_, pi_ = table_parts(s5c, pw, q0, 9)
                t1 = gtmp2.rearrange("p (q i c) -> p q i c", q=2, i=9)
                t2 = gtmp.rearrange("p (q i c) -> p q i c", q=2, i=9)
                tt(t1, cr, pi_, ALU.mult)
                tt(t2, ci, pr_, ALU.mult)
                for s in range(2):
                    ln = slice(64 * s, 64 * s + 64)
                    last = pool.tensor_tensor(
                        caz[ln, b, :, 1, s, :].rearrange("p q (i c) -> p q i c", i=9), t1[ln], t2[ln], ALU.subtract)
                last.then_inc(s5_im, 1)
                pool.wait_ge(s5_im, k + 1)

            def load_decay(g, hh):
                n = at_before_ret + 4 * g + hh - 2
                if g or hh >= 2:
                    pool.wait_ge(at_free[n % 2], n // 2 + 1)
                pool.dma_start(dec[:, hh % 2, :], decay_in[:, 4 * g + hh, :]).then_inc(dec_in[hh % 2], 16)

            rotated = [0]

            def rotary(b):
                wait_block(b)
                n4 = nat.rearrange("p t (h m) -> p t h m", h=4)
                r4 = rot.rearrange("p t (h m) -> p t h m", h=4)
                t1, t2 = n4[:, :, :, 0:64], n4[:, :, :, 64:128]
                c, s = (cs[:, a].unsqueeze(2).to_broadcast([P, TOK, 4, 64]) for a in range(2))
                tt(rtmp[:, 0], t2, s, ALU.mult)
                tt(rtmp[:, 1], t1, s, ALU.mult)
                tt(r4[:, :, :, 0:64], t1, c, ALU.mult)
                tt(r4[:, :, :, 64:128], t2, c, ALU.mult)
                tt(r4[:, :, :, 0:64], r4[:, :, :, 0:64], rtmp[:, 0], ALU.subtract)
                pool.tensor_tensor(r4[:, :, :, 64:128], r4[:, :, :, 64:128], rtmp[:, 1], ALU.add)\
                    .then_inc(rot_ready, 1)
                rotated[0] += 1
                pool.wait_ge(rot_ready, rotated[0])

            def norm_and_gate(g):
                pool.wait_ge(ro_stat, g + 1)
                wait_block(4 + 4 * g + 3)
                r3, g3 = (v.rearrange("p t (h m) -> p (t h) m", h=4) for v in (ro, gate))
                tt(r3, r3, mv[:, :, 0:1].to_broadcast([P, 8, P]), ALU.subtract)
                tt(r3, r3, mv[:, :, 1:2].to_broadcast([P, 8, P]), ALU.mult)
                pool.tensor_tensor(g3, g3, r3, ALU.mult).then_inc(ro_ready, 1)
                pool.wait_ge(ro_ready, g + 1)

            pool.wait_ge(kv_out, 32)
            for g in range(2):
                for hh in range(2):
                    load_decay(g, hh)
                rotary(4 + 4 * g)
                rotary(4 + 4 * g + 1)
                for hh in (2, 3):
                    load_decay(g, hh)
                norm_and_gate(g)

            for g in range(2):
                wait_block(OB + g)
                pool.dma_start(u_d.rearrange("(t p) n -> p t n", p=P)[:, :, g * NB:(g + 1) * NB], onat)\
                    .then_inc(u_out, 16)
                for t in range(TOK):
                    pool.dma_start(uc_d.rearrange("g (t p) c -> t p g c", t=TOK)[
                        t, :, g * Q:(g + 1) * Q, :], onat[:, t, :].rearrange("p (g c) -> p g c", c=GC))\
                        .then_inc(u_out, 16)
            link(pool.memset(S[:, :, :, 0:1], 0.0))
            pool.wait_ge(u_out, 96)
            pool.wait_ge(et_out, 16 * 16)
            x8_0 = at_before_y[0] - 8
            for k in range(8):
                b = k % 2
                if k >= 2:
                    pool.wait_ge(at_full, x8_0 + k - 1)
                for s in range(2):
                    pool.dma_start(Ucb[b][:, s], uc_d.rearrange("(s q) (j i) c -> s j q (i c)", s=2, i=T8)[
                        s, :, 4 * k:4 * k + 4, :]).then_inc(uc_in[b], 16)
                pool.dma_start(ETb[b], et_d[:, 4 * k:4 * k + 4]).then_inc(et_in[b], 16)
            for n in (x8_0 + 6, x8_0 + 7):
                pool.wait_ge(at_free[n % 2], n // 2 + 1)
            S5 = S.rearrange("p r q (c i) -> p r q c i", i=T8)
            CB = J // T8

            def advance(now, before, shape, powers):
                n = shape[1] * shape[2]
                t1 = rc[:, 0:2 * n].rearrange("p (r q i) -> p r q i", r=2, q=Q)
                t2 = rc[:, 512:512 + n].rearrange("p (q i) -> p q i", q=Q)
                for r in range(2):
                    tt(t1[:, r], before(r), powers(0), ALU.mult)
                for r, op in ((0, ALU.subtract), (1, ALU.add)):
                    tt(t2, before(1 - r), powers(1), ALU.mult)
                    tt(t1[:, r], t1[:, r], t2, op)
                tt(now, now, t1, ALU.add)

            for i in range(1, T8):
                advance(S5[:, :, :, :, i], lambda r: S5[:, r, :, :, i - 1], [P, Q, CB],
                        lambda r: a8[:, r, 0, :].unsqueeze(2).to_broadcast([P, Q, CB]))
            for c in range(1, CB):
                advance(S5[:, :, :, c, :], lambda r: S5[:, r, :, c - 1, T8 - 1:T8].to_broadcast([P, Q, T8]),
                        [P, Q, T8], lambda r: a8[:, r].rearrange("p k q -> p q k"))
            pool.memset(rc[:, 0:1], 0.0).then_inc(scan_ready, 1)
            pool.wait_ge(gb_prod, 4)
            pool.dma_start(dsk, s5_d[0].rearrange("(a g) c -> a (g c)", a=1).to_broadcast([P, G * GC]))\
                .then_inc(cst["dsk"], 16)
            for b in range(2):
                pool.wait_ge(y_out[b], 32 * 8)
            pool.dma_start(yy, y_d.rearrange("(t p) n -> p t n", p=P)).then_inc(y_in, 16)
            pool.dma_start(uu, u_d.rearrange("(t p) n -> p t n", p=P)).then_inc(y_in, 16)
            wait_block(OB + 8 + 4 + 2 + 4 + 1 + 4)
            pool.dma_start(gfin, norm_final.rearrange("(a n) -> a n", a=1).to_broadcast([P, D]))\
                .then_inc(cst["gf"], 16)


_INS = ["x", "mem", "norm_mix", "norm_xattn", "norm_mlp", "norm_mem", "norm_final", "ab_w_in", "ab_b_forget",
        "ab_w_out", "cd_w_in", "s5_a_re", "s5_a_im", "s5_b_re", "s5_b_im", "s5_c_re", "s5_c_im", "s5_d",
        "s5_log_step", "s5_w_glu", "conv_w", "cd_w_out", "xa_wq", "xa_wkv", "xa_wo", "mlp_w1", "mlp_w2"]


def _shape_constants():
    f = np.float32
    half = HD // 2
    inv = (f(10000.0) ** (-np.arange(half, dtype=f) / f(half))).astype(f)
    ang = np.arange(L, dtype=f)[:, None] * inv[None, :]
    by_token = lambda v: v.astype(f).reshape(TOK, P, half).transpose(1, 0, 2).reshape(P, -1)
    rope = np.concatenate([by_token(np.cos(ang)), by_token(np.sin(ang))], axis=1)
    log_g = np.log1p(-np.exp2(-5.0 - np.arange(8, dtype=np.float64)))
    diff = np.arange(L)[None, :] - np.arange(P)[:, None]
    d = np.where(diff >= 0, np.exp(log_g[:, None, None] * np.maximum(diff, 0)), 0.0) * HD ** -0.5
    decay = np.concatenate([d, d[:, :, 0:P]], axis=2).transpose(1, 0, 2).astype(f)
    tri = (np.arange(L)[None, :] >= np.arange(P)[:, None]).astype(f)
    causal = np.where(np.arange(P)[None, :] <= np.arange(P)[:, None], 0.0, NEG).astype(f)
    return {"rope": rope, "decay": decay, "tri": tri, "causal": causal, "eye": np.eye(P, dtype=f)}


def kernel(**inputs):
    import concourse.bacc as bacc
    from concourse.bass_utils import run_bass_kernel_spmd

    nc = bacc.Bacc("TRN2", target_bir_lowering=False, num_devices=1)
    arrays, args = {}, []
    given = {n: np.ascontiguousarray(inputs[n]) for n in _INS}
    given.update({n: np.ascontiguousarray(a) for n, a in _shape_constants().items()})
    for name, a in given.items():
        arrays[f"in_{name}"] = a
        args.append(nc.dram_tensor(f"in_{name}", a.shape, mybir.dt.from_np(a.dtype), kind="ExternalInput").ap())
    args.append(nc.dram_tensor("out_0", (1, L, D), F32, kind="ExternalOutput").ap())
    trunk(nc, *args)
    r = run_bass_kernel_spmd(nc, [arrays], core_ids=[0])
    return r.results[0]["out_0"]
```

```python
from contextlib import ExitStack

import concourse.bass as bass
import numpy as np
from concourse import mybir

F32 = mybir.dt.float32
F32R = mybir.dt.float32r
BF16 = mybir.dt.bfloat16
I32 = mybir.dt.int32
ACT = mybir.ActivationFunctionType
ALU = mybir.AluOpType
AX = mybir.AxisListType

P = 128
D = 2048
L = 256
TOK = L // P
NB = 512
BLOCKS = D // NB
FF = 4 * D
EPS = 1e-6
HD = 128
HALVES = 8
RING = 4
CHUNK = 1024
CHUNKS = FF // CHUNK
G, GC, ST = 64, 16, 64
Q = G // 2
T8 = 8
J = L // T8
GW = T8 * GC
NEG = -1.0e30
MIX, XAT, MLP, MEM = 0, 32, 64, 96


class Place:

    def __init__(self):
        self.n, self.reg, self.rates = {}, None, {}

    def at(self, what, plus=0, by=1):
        v = (self.n.get(what, 0) + plus) // by
        if self.reg is None or not self.rates.get(what):
            return v
        return self.reg * (self.rates[what] // by) + v

    def bump(self, what, k=1):
        self.n[what] = self.n.get(what, 0) + k
        return self.at(what)

    def enter(self, reg, rates):
        self.reg, self.rates, self.entry = reg, rates, dict(self.n)

    def leave(self, trips):
        for k in set(self.n) | set(self.rates):
            got = self.n.get(k, 0) - self.entry.get(k, 0)
            assert got == self.rates.get(k, 0), (k, got, self.rates)
            self.n[k] = self.entry.get(k, 0) + trips * got
        self.reg = None


def plan(kind, order=(0, 1, 2, 3), kbase=0):
    if kind == "full":
        return [(0, order[i // 2] * 4 + 2 * (i % 2), i == 0, i == 7) for i in range(8)]
    if kind == "pair":
        return [((i // 2) % 2, kbase + (i // 4) * 4 + 2 * (i % 2), i < 4 and i % 2 == 0,
                 i >= 4 and i % 2 == 1) for i in range(8)]
    if kind == "mixed":
        return [(0, 0, True, False), (1, 0, True, False), (0, 2, False, True), (1, 2, False, True),
                (2, 0, True, False), (2, 2, False, True), (3, 0, True, False), (3, 2, False, True)]
    if kind == "seq":
        return [(i // 4, 2 * (i % 4), i % 4 == 0, i % 4 == 3) for i in range(8)]
    raise ValueError(kind)


UNIT_BLOCKS = {"full": 1, "pair": 2, "seq": 2, "mixed": 4, "heads": 2}
STEP_RATES = {"half": 32, "unit": 4, "block": 6, "tp": 4, "his": 4, "hid": 2}


def trunk(nc, x, mem, norm_mix, norm_xattn, norm_mlp, norm_mem, norm_final, ab_w_in, ab_b_forget,
          ab_w_out, cd_w_in, s5_a_re, s5_a_im, s5_b_re, s5_b_im, s5_c_re, s5_c_im, s5_d,
          s5_log_step, s5_w_glu, conv_w, cd_w_out, xa_wq, xa_wkv, xa_wo, mlp_w1, mlp_w2,
          rope, decay_in, tri, causal, eye, out):
    ctx = ExitStack()
    with ctx:
        def sb(name, shape, dt=F32):
            return ctx.enter_context(nc.sbuf_tensor(name, shape, dt))

        def sem(name):
            return ctx.enter_context(nc.semaphore(name))

        h = sb("h", [P, TOK, D])
        xt = [sb(f"xt_{n}", [P, 16, L], F32R) for n in ("hi", "lo")]
        yt = [sb(f"yt_{n}", [P, 16, L], F32R) for n in ("hi", "lo")]
        raw = sb("raw", [P, RING, 4, NB])
        whi = sb("whi", [P, RING, 2, NB], F32R)
        wlo = sb("wlo", [P, RING, 2, NB], F32R)
        ident = sb("ident", [P, P])
        mask = sb("mask", [P, P])
        cs = sb("cs", [P, 2, TOK, HD // 2])
        gain = sb("gain", [P, 7 * 16 + 24])
        bfor = sb("bfor", [P, 8])
        rstd = sb("rstd", [P, 13, TOK])
        ssq = sb("ssq", [P, TOK, BLOCKS])
        nrm = sb("nrm", [P, 4, 8])
        warm = sb("warm", [P, 2])
        junk = sb("junk", [P, TOK, NB], BF16)
        c8 = sb("c8", [8, 2, L])
        smx = sb("smx", [P, 2, 3, 2])
        kvk = sb("kvk", [P, 4, L])
        kvv = sb("kvv", [P, TOK, NB])
        A_SIZE = 11200
        arena = sb("arena", [P, A_SIZE])

        def view(at, n, pattern=None, p=P, **sizes):
            assert at + n <= A_SIZE
            a = arena[0:p, at:at + n]
            return a.rearrange(pattern, **sizes) if pattern else a

        memt = view(0, 4096, "p (t n) -> p t n", t=TOK)
        grow = view(4096, 128)
        crow = view(4224, 128)
        s5row = view(4352, 128)
        s5b = view(4480, 1024, "p (r q c) -> p r q c", r=2, q=Q)
        s5c = view(5504, 1024, "p (r q c) -> p r q c", r=2, q=Q)
        pw = view(6528, 576, "p (r k q) -> p r k q", r=2, k=9)
        pb = view(7104, 512, "p (r k q) -> p r k q", r=2, k=8)
        prep = view(4480, 3136)
        par = view(9664, 16 * 32, "p (k q) -> p k q", k=16)
        craw = view(8128, 1024, "p (r t k) -> p r t k", r=2, t=4)
        ptmp = view(9152, 512, "p (k q) -> p k q", k=16)
        etab = view(1024, 1024, "p (b q r w) -> p b q r w", b=2, q=2, r=2)
        vtmp = view(2048, 288)
        gtmp = view(2336, 288)
        vtmp2 = view(2624, 288)
        gtmp2 = view(4192, 288)
        vtmp3 = view(2912, 288)
        ksb = view(3200, 480, "p (q w) -> p q w", p=2 * GC, q=2)
        ets = view(3680, 512)
        cz = [view(at_, 576, "p (q r w) -> p q r w", q=2, r=2) for at_ in (7616, 10240)]
        eb = view(10816, 256, "p (b q r w) -> p b q r w", b=2, q=2, r=2)

        nat = view(0, 1024, "p (t n) -> p t n", t=TOK)
        rot = view(1024, 1024, "p (t n) -> p t n", t=TOK)
        rtmp = view(2048, 1024, "p (a t h n) -> p a t h n", a=2, t=TOK, h=4)
        qT = view(3072, 1024, "p (h n) -> p h n", h=4)
        kT = view(4096, 1024, "p (h n) -> p h n", h=4)
        vn = view(5120, 1024, "p (t n) -> p t n", t=TOK)
        gate = view(6144, 1024, "p (t n) -> p t n", t=TOK)
        ro = view(7168, 1024, "p (t n) -> p t n", t=TOK)
        pr = view(8192, 1024, "p (b n) -> p b n", b=2)
        pT = view(9216, 1024, "p (b n) -> p b n", b=2)
        dec = view(10240, 768, "p (h n) -> p h n", h=2)
        stat = sb("stat", [P, 8, 6])
        mv = sb("mv", [P, 8, 2])
        kst_nat = view(10176, 1024, "p (t n) -> p t n", t=TOK)
        kst = view(10176, 1024)
        trit = sb("trit", [P, L])
        lgt = sb("lgt", [P, 4, TOK, 8])
        wff = view(0, 2048, "p (k n) -> p k n", k=16)
        wffs = [v[:, 0:8, :].rearrange("p k (a n) -> p (k a) n", n=P) for v in yt]
        zT8 = sb("zT8", [8, L])
        UT = view(0, 2048, "p (r q j) -> p r q j", r=2, q=Q)
        S = view(2048, 2048, "p (r q j) -> p r q j", r=2, q=Q)
        Ucb = [view(4096, 1024, "p (r q w) -> p r q w", p=J, r=2, q=4),
               kvk[0:J].rearrange("p h n -> p (h n)").rearrange("p (r q w) -> p r q w", r=2, q=4)]
        Ucb.append(view(7360, 1024, "p (r q w) -> p r q w", p=J, r=2, q=4))
        Yc = view(4096, 1024, "p (b i r n) -> p b i r n", p=J, b=2, i=T8, r=2)
        ETb = [view(5120, 1024, "p (q r w) -> p q r w", q=4, r=2),
               kvv[:, :, :].rearrange("p t n -> p (t n)").rearrange("p (q r w) -> p q r w", q=4, r=2)]
        ETb.append(view(8384, 1024, "p (q r w) -> p q r w", q=4, r=2))
        Tc = view(5120, 1024, "p (b s q w) -> p b s q w", b=2, s=2, q=2)
        CAb = [t.rearrange("p (q r s w) -> p q r s w", q=2, r=2, s=2) for t in (
            kvk[:, :, :].rearrange("p h n -> p (h n)"), kvv[:, :, :].rearrange("p t n -> p (t n)"))]
        rc = view(10432, 768)
        hn = view(6336, 1024, "p (t n) -> p t n", t=TOK)
        zT = view(7360, 1024, "p (k n) -> p k n", k=4)
        cv = view(8384, 1024, "p (k n) -> p k n", k=4)
        a8 = sb("a8", [P, 2, T8, Q])
        onat = view(9408, 1024, "p (t n) -> p t n", t=TOK)
        dsk = view(5120, 1024)
        yy = view(0, 2048, "p (t n) -> p t n", t=TOK)
        uu = view(2048, 2048, "p (t n) -> p t n", t=TOK)
        sg = view(4096, 2048, "p (t n) -> p t n", t=TOK)
        gfin = view(6144, 2048)
        fin = view(2048, 4096, "p (t n) -> p t n", t=TOK)

        acc = ctx.enter_context(nc.psum_tensor("acc", [P, 4, NB], F32))
        tp = ctx.enter_context(nc.psum_tensor("tp", [P, 2, NB], F32))
        at = ctx.enter_context(nc.psum_tensor("at", [P, 2, NB], F32))

        et_d = nc.dram_tensor("et_d", [P, Q, 2, GW], F32, kind="Internal").ap()
        ca_d = nc.dram_tensor("ca_d", [P, Q, 2, 144], F32, kind="Internal").ap()
        k_d = nc.dram_tensor("k_d", [GC, G, 240], F32, kind="Internal").ap()
        u_d = nc.dram_tensor("u_d", [L, G * GC], F32, kind="Internal").ap()
        uc_d = nc.dram_tensor("uc_d", [G, L, GC], F32, kind="Internal").ap()
        prep_d = nc.dram_tensor("prep_d", [P, 3136], F32, kind="Internal").ap()
        kv_d = nc.dram_tensor("kv_d", [2, P, 1024], F32, kind="Internal").ap()
        t_d = nc.dram_tensor("t_d", [P, G, GW], F32, kind="Internal").ap()
        y_d = nc.dram_tensor("y_d", [L, G * GC], F32, kind="Internal").ap()

        raw_landed = [sem(f"raw_landed{s}") for s in range(RING)]
        hi_ready = sem("hi_ready")
        lo_ready = sem("lo_ready")
        half_used = sem("half_used")
        acc_free = [sem(f"acc_free{p}") for p in range(2)]
        tp_full = sem("tp_full")
        tp_free = [sem(f"tp_free{b}") for b in range(2)]
        at_full = sem("at_full")
        at_free = [sem(f"at_free{b}") for b in range(2)]
        hi_put = sem("hi_put")
        hid_ready = sem("hid_ready")
        ssq_ready = sem("ssq_ready")
        var_ready, sd_ready, rstd_ready = sem("var_ready"), sem("sd_ready"), sem("rstd_ready")
        rot_ready = sem("rot_ready")
        kv_out, kv_in = sem("kv_out"), sem("kv_in")
        act_step, dve_step, pool_step = sem("act_step"), sem("dve_step"), sem("pool_step")
        cst = {n: sem(f"ld_{n}") for n in ("id", "cst", "grow", "mem", "x", "s5", "ff", "tri", "dsk", "gf")}
        dec_in = [sem(f"dec_in{b}") for b in range(2)]
        q_ready = sem("q_ready")
        rstd8 = sem("rstd8")
        mem_in = [sem(f"mem_in{b}") for b in range(BLOCKS)]
        x_in = [sem(f"x_in{b}") for b in range(BLOCKS)]
        sm_max, sm_p = sem("sm_max"), sem("sm_p")
        ro_stat, ro_ready = sem("ro_stat"), sem("ro_ready")
        ff_hi, ff_split, ff_z, ff_log, ff_act = (sem(n) for n in ("ff_hi", "ff_split", "ff_z", "ff_log", "ff_act"))
        c_ready = sem("c_ready")
        t_out = sem("t_out")
        s5_par, s5_sin, s5_lam, s5_inv = (sem(n) for n in ("s5_par", "s5_sin", "s5_lam", "s5_inv"))
        s5_re, s5_im = sem("s5_re"), sem("s5_im")
        et_out, k_out = sem("et_out"), sem("k_out")
        ca_out = [sem(f"ca_out{b}") for b in range(2)]
        prep_out, prep_in, tab_zero = sem("prep_out"), sem("prep_in"), sem("tab_zero")
        ksb_zero = sem("ksb_zero")
        u_out = sem("u_out")
        uc_in, et_in = ([sem(f"{n}{b}") for b in range(3)] for n in ("uc_in", "et_in"))
        ca_in = [sem(f"ca_in{b}") for b in range(2)]
        t_in = [sem(f"t_in{b}") for b in range(2)]
        scan_ready = sem("scan_ready")
        ca_zero = sem("ca_zero")
        y_out, y_in = [sem(f"y_out{b}") for b in range(2)], sem("y_in")
        gb_prod = sem("gb_prod")
        y_ready, ge_ready = sem("y_ready"), sem("ge_ready")
        ssm_ready = sem("ssm_ready")
        hg_ready, fin_act = sem("hg_ready"), sem("fin_act")
        fin_ready, out_done = sem("fin_ready"), sem("out_done")

        par_of = {n: i for i, n in enumerate((
            "lre", "lim", "ls", "step", "k", "r", "e", "mag", "th", "ph", "sin", "cos",
            "t1", "t2", "t3", "t4"))}
        E_UNITS = [("rq", 0), ("rk", 0), ("rv", 0), ("rg", 0), ("rq", 1), ("rk", 1), ("rv", 1),
                   ("rg", 1), ("fq", 0), ("fk", 0), ("fv", 0), ("fq", 1), ("fk", 1), ("fv", 1)]
        FW = 1024
        E_COL = {"fq": 0, "fk": FW, "fv": 2 * FW, "rq": 3 * FW + 8, "rk": 4 * FW + 8,
                 "rv": 5 * FW + 8, "rg": 6 * FW + 8}
        O_UNITS = [("u", 0), ("u", 1), ("h", 0), ("gc", 0), ("gb", 0), ("h", 1), ("gc", 1), ("gb", 1)]
        O_COL = {"u": 0, "h": 1024, "gb": 2048, "gc": 3072}
        OUT_ORDER = (2, 3, 0, 1)
        CHUNK_T = [k * 27 // 15 for k in range(16)]
        DVE_T = [t + 2 for t in CHUNK_T]
        X8_T, Y_T = 22, 50
        SCALE = float(HD) ** -0.5
        at_before_ret = 3 + 3
        at_before_tab = at_before_ret + 8 + 8 + 4
        at_before_x = at_before_tab + 2 * 16
        at_before_y = at_before_x + 8
        tp_before_u = 2 + 2 * (4 + 4 + 2 + 8 + 2) + 8 + 16 + 2 * 12 + 8 + 4 * CHUNKS
        OB = 4 + 14 + 4 + 2 + 4 + 6 * CHUNKS
        block = ctx.enter_context(nc.Block())


        def wait_freed(eng, p, back):
            b = p.n["block"] - back
            eng.wait_ge(acc_free[b % 2], p.at("block", -back, by=2) + 1)

        def wait_tp_read(eng, token):
            eng.wait_ge(tp_free[token[0]], token[1])

        def tp_token(p):
            return p.n["tp"] % 2, p.at("tp", 0, by=2) + 1

        def root_count(m):
            return m + 1 if m < 2 else m + 3

        def table_parts(coef, power, q0, n):
            shape = [P, 2, n, GC]
            cr, ci = (coef[:, r, q0:q0 + 2, :].unsqueeze(2).to_broadcast(shape) for r in range(2))
            pr_, pi_ = (power[:, r, 0:n, q0:q0 + 2].rearrange("p i q -> p q i").unsqueeze(3).to_broadcast(shape)
                        for r in range(2))
            return cr, ci, pr_, pi_

        def half_weights(t, kind, i):
            if kind == "heads":
                return t[:, i // 2].rearrange("p a n -> p (a n)").rearrange("p (k h n) -> p h k n", k=8, h=2)[:, i % 2]
            return t[:, i // 2, 2 * (i % 2):2 * (i % 2) + 2]

        def split_weights(t, kind, i):
            v = t[:, i % RING]
            return v.rearrange("p a n -> p (a n)").rearrange("p (k n) -> p k n", k=8) if kind == "heads" else v

        def parity(p, back):
            return (p.n["block"] - back) % 2

        @block.sync
        def _(sp):
            p = Place()
            p.n = {"half": 0, "unit": 0}

            def slab(i, src, first=False):
                if not first:
                    sp.wait_ge(lo_ready, p.at("half", 2 * i + 2 - 8))
                sp.dma_start(raw[:, i], src.rearrange("(k p) n -> p k n", p=P)).then_inc(raw_landed[i], 16)

            def load(kind, w, cols, order=(0, 1, 2, 3), row0=0, first=False, hook=None):
                for i in range(RING):
                    if kind == "heads":
                        if not first:
                            sp.wait_ge(lo_ready, p.at("half", 2 * i + 2 - 8))
                        sp.dma_start(raw[:, i].rearrange("p a (b n) -> p (a b) n", b=2),
                                     w[(i // 2) * 1024:(i // 2 + 1) * 1024, (i % 2) * 256:(i % 2 + 1) * 256]
                                     .rearrange("(k p) n -> p k n", p=P)).then_inc(raw_landed[i], 16)
                        continue
                    if kind == "mixed" and i < 2:
                        if not first:
                            sp.wait_ge(lo_ready, p.at("half", 2 * i + 2 - 8))
                        for b in range(2):
                            sp.dma_start(raw[:, i, 2 * b:2 * b + 2], w[i * 256:(i + 1) * 256, b * NB:(b + 1) * NB]
                                         .rearrange("(k p) n -> p k n", p=P)).then_inc(raw_landed[i], 16)
                        continue
                    if kind == "full":
                        c, r = cols[0], order[i] * NB
                    elif kind == "pair":
                        c, r = cols[i % 2], (i // 2) * NB
                    elif kind == "seq":
                        c, r = cols[i // 2], (i % 2) * NB
                    else:
                        c, r = cols[i], 0
                    rows = slice(row0 + r, row0 + r + NB) if isinstance(row0, int) else bass.ds(row0 + r, NB)
                    cc = slice(c, c + NB) if isinstance(c, int) else bass.ds(c, NB)
                    slab(i, w[rows, cc], first)
                    if hook:
                        hook(i)
                p.bump("half", 8)
                p.bump("unit")

            def mlp(layer):
                def step(c):
                    w1, w2 = mlp_w1[layer], mlp_w2[layer]
                    load("full", w1, [c * CHUNK])
                    load("full", w1, [c * CHUNK + NB])
                    load("pair", w2, [0, NB], row0=c * CHUNK)
                    load("pair", w2, [2 * NB, 3 * NB], row0=c * CHUNK)
                step(0)
                with sp.Fori(0, CHUNKS - 2) as r:
                    p.enter(r, {"half": 32, "unit": 4})
                    step(r + 1)
                    p.leave(CHUNKS - 2)
                step(CHUNKS - 1)

            sp.dma_start(ident[:, :], eye).then_inc(cst["id"], 16)
            for r0, src in ((MIX, norm_mix), (XAT, norm_xattn), (MLP, norm_mlp)):
                sp.dma_start(grow[r0:r0 + 32, :], src.rearrange("l (k p) -> (l k) p", p=P)).then_inc(cst["grow"], 16)
            sp.dma_start(grow[MEM:MEM + 16, :], norm_mem.rearrange("(k p) -> k p", p=P)).then_inc(cst["grow"], 16)
            sp.dma_start(crow[0:24, :], conv_w[0].rearrange("s (k p) -> (s k) p", p=P)).then_inc(cst["grow"], 16)

            def load_mem(b):
                sp.dma_start(memt[:, :, b * NB:(b + 1) * NB], mem[0].rearrange("(t p) n -> p t n", p=P)[
                    :, :, b * NB:(b + 1) * NB]).then_inc(mem_in[b], 16)
            load_mem(0)
            load("full", xa_wkv[0], [0], first=True, hook=lambda i: load_mem(1 + i) if i < 3 else None)
            for dst, src in ((mask[:, :], causal), (cs[:, :, :, :], rope.rearrange("p (a t n) -> p a t n", a=2, t=TOK)),
                             (bfor[:, :], ab_b_forget[0:1, :].to_broadcast([P, 8]))):
                sp.dma_start(dst, src).then_inc(cst["cst"], 16)
            for b in range(BLOCKS):
                sp.dma_start(h[:, :, b * NB:(b + 1) * NB], x[0].rearrange("(t p) n -> p t n", p=P)[
                    :, :, b * NB:(b + 1) * NB]).then_inc(x_in[b], 16)
            load("full", xa_wkv[0], [NB])
            for n in range(2):
                load("full", xa_wkv[1], [n * NB])
            for name, g in E_UNITS:
                load("full", ab_w_in[0], [E_COL[name] + g * NB])
            for n in range(BLOCKS):
                load("full", ab_w_out[0], [n * NB], order=OUT_ORDER)
            load("heads", xa_wq[0], [0])
            load("mixed", xa_wo[0], [n * NB for n in range(4)])
            mlp(0)

            def s5_loads(s):
                for k in (s - X8_T - 6, s - X8_T - 5):
                    if 0 <= k < 8:
                        b = k % 3
                        if k == 0:
                            sp.wait_ge(u_out, 96)
                            sp.wait_ge(et_out, 16 * 16)
                        if k >= 3:
                            sp.wait_ge(tp_full, tp_before_u + k - 2)
                        for g in range(2):
                            sp.dma_start(Ucb[b][:, g], uc_d.rearrange("(s q) (j i) c -> s j q (i c)", s=2, i=T8)[
                                g, :, 4 * k:4 * k + 4, :]).then_inc(uc_in[b], 16)
                        if k >= 3:
                            sp.wait_ge(at_full, at_before_x + k - 2)
                        sp.dma_start(ETb[b], et_d[:, 4 * k:4 * k + 4]).then_inc(et_in[b], 16)
                for k in (s - Y_T - 6, s - Y_T - 5):
                    if 0 <= k < 16:
                        b = k % 2
                        if k == 0:
                            sp.wait_ge(t_out, 16 * T8)
                            for c in range(2):
                                sp.wait_ge(ca_out[c], 16 * 8)
                            sp.wait_ge(ca_zero, 2)
                        sp.wait_ge(at_full, at_before_y + max(k - 1, 0))
                        for g in range(2):
                            ln = slice(64 * g, 64 * g + 64)
                            sp.dma_start(CAb[b][ln, :, :, g, :], ca_d[ln, 2 * k:2 * k + 2, :, GC:])\
                                .then_inc(ca_in[b], 16)
                        sp.dma_start(Tc[:, b], t_d.rearrange("p (s q) w -> p s q w", s=2)[
                            :, :, 2 * k:2 * k + 2, :]).then_inc(t_in[b], 16)

            for o, (name, g) in enumerate(O_UNITS):
                load("full", cd_w_in[0], [O_COL[name] + g * NB], hook=lambda i, o=o: s5_loads(8 * o + 2 * i))
            for o in range(2):
                load("pair", cd_w_out[0], [2 * o * NB, (2 * o + 1) * NB], row0=1024,
                     hook=lambda i, o=o: s5_loads(8 * (8 + o) + 2 * i))
            load("seq", s5_w_glu[0], [0, NB])
            load("pair", cd_w_out[0], [0, NB])
            sp.wait_ge(at_full, at_before_y + 16)
            sp.wait_ge(kv_out, 32)
            sp.dma_start(kvk[:, :, :], kv_d[0].rearrange("p (h n) -> p h n", h=4)).then_inc(kv_in, 16)
            sp.dma_start(kvv[:, :, :], kv_d[1].rearrange("p (t n) -> p t n", t=TOK)).then_inc(kv_in, 16)
            load("pair", cd_w_out[0], [2 * NB, 3 * NB])
            load("heads", xa_wq[1], [0])
            load("mixed", xa_wo[1], [n * NB for n in range(4)])
            mlp(1)
            for b in (0, 2, 1, 3):
                sp.wait_ge(*((fin_act, b + 1) if b < 2 else (fin_ready, b - 1)))
                sp.dma_start(out[0].rearrange("(t p) n -> p t n", p=P)[:, :, b * NB:(b + 1) * NB],
                             fin[:, :, b * NB:(b + 1) * NB]).then_inc(out_done, 16)
            sp.wait_ge(out_done, 16 * BLOCKS)

        @block.tensor
        def _(pe):
            p = Place()
            p.n = {"half": 0, "unit": 0, "block": 0, "tp": 0, "hid": 0}
            x_tok, y_tok = {}, {}

            def unit(kind, src, tok, after=None, order=(0, 1, 2, 3), kbase=0):
                hi, lo = src
                for i, (blk, kt0, opens, closes) in enumerate(plan(kind, order, kbase)):
                    par = (p.n["block"] + blk) % 2
                    if opens and p.n["block"] + blk >= 2:
                        pe.wait_ge(acc_free[par], p.at("block", blk, by=2))
                    for kt in (kt0, kt0 + 1):
                        if kt in tok:
                            wait_tp_read(pe, tok.pop(kt))
                    pe.wait_ge(lo_ready, p.at("half", i + 1))
                    for kk in range(2):
                        for t in range(TOK):
                            a = acc[:, 2 * par + t, :]
                            xh, xl = (s[:, kt0 + kk, t * P:(t + 1) * P] for s in (hi, lo))
                            w = i % RING
                            pe.matmul(a, xh, whi[:, w, kk], start=opens and kk == 0, stop=False)
                            pe.matmul(a, xh, wlo[:, w, kk], start=False, stop=False)
                            last = pe.matmul(a, xl, whi[:, w, kk], start=False, stop=closes and kk == 1)
                    last.then_inc(half_used, 1)
                    if after:
                        after(i)
                p.bump("half", 8)
                p.bump("unit")
                p.bump("block", UNIT_BLOCKS[kind])

            def open_tp():
                n = p.n["tp"]
                if n >= 2:
                    pe.wait_ge(tp_free[n % 2], p.at("tp", 0, by=2))
                return tp[:, n % 2, :]

            def close_tp(last):
                last.then_inc(tp_full, 1)
                token = tp_token(p)
                p.bump("tp")
                return token

            def transpose_block(src, tok=None, kt0=0):
                tokens = []
                for b in range(2):
                    bank = open_tp()
                    for kk in range(2):
                        for t in range(TOK):
                            last = pe.transpose(bank[:, kk * L + t * P:kk * L + (t + 1) * P],
                                                src[:, t, (2 * b + kk) * P:(2 * b + kk + 1) * P], ident[:, :])
                    token = close_tp(last)
                    tokens.append(token)
                    if tok is not None:
                        tok[kt0 + 2 * b] = tok[kt0 + 2 * b + 1] = token
                return tokens

            def h_block(n, back):
                wait_freed(pe, p, back)
                transpose_block(h[:, :, n * NB:(n + 1) * NB], x_tok, 4 * n)

            def open_at():
                n = p.n.setdefault("at", 0)
                if n >= 2:
                    pe.wait_ge(at_free[n % 2], n // 2)
                return at[:, n % 2, :]

            def close_at(last):
                last.then_inc(at_full, 1)
                p.bump("at")

            def mm(o, lhsT, rhs, start=True, stop=True):
                return pe.matmul(o, lhsT, rhs, start=start, stop=stop)

            pe.wait_ge(cst["id"], 16)
            pe.wait_ge(cst["grow"], 80)
            close_tp(pe.transpose(open_tp()[:, 0:112], grow[0:112, :], ident[0:112, 0:112]))
            close_tp(pe.transpose(open_tp()[:, 0:24], crow[0:24, :], ident[0:24, 0:24]))

            def mem_block(b):
                pe.wait_ge(mem_in[b], 16)
                transpose_block(memt[:, :, b * NB:(b + 1) * NB], y_tok, 4 * b)
            mem_block(0)
            mem_block(1)

            def s5_rows():
                pe.wait_ge(cst["s5"], 16 * 15)
                bank = open_at()
                close_at(pe.transpose(bank[:, 0:96], s5row[0:96, :], ident[0:96, 0:96]))
                for r in range(2):
                    bank = open_at()
                    for t in range(4):
                        last = pe.transpose(bank[:, t * P:(t + 1) * P], craw[:, r, t, :], ident[:, :])
                    close_at(last)

            def s5_chunk(k):
                b = k % 2
                pe.wait_ge(s5_re, k + 1)
                pe.wait_ge(s5_im, k + 1)
                bank = open_at()
                for q in range(2):
                    for r in range(2):
                        last = pe.transpose(bank[:, (2 * q + r) * P:(2 * q + r + 1) * P],
                                            etab[:, b, q, r, :], ident[:, :])
                close_at(last)
                bank = open_at()
                for q in range(2):
                    o = bank[0:2 * GC, q * P:(q + 1) * P]
                    mm(o, eb[:, b, q, 0, :], cz[b][:, q, 0, 0:GW], True, False)
                    last = mm(o, eb[:, b, q, 1, :], cz[b][:, q, 1, 0:GW], False, True)
                close_at(last)

            def s5_tables(t):
                if t in CHUNK_T:
                    s5_chunk(CHUNK_T.index(t))

            for u in range(4):
                def after(i, u=u):
                    if i == 5:
                        pe.wait_ge(x_in[u], 16)
                        transpose_block(h[:, :, u * NB:(u + 1) * NB], x_tok, 4 * u)
                    if u == 0 and i in (0, 2):
                        mem_block(2 + i // 2)
                    if u == 1 and i == 3:
                        s5_rows()
                    if u in (1, 3) and i == 2:
                        wait_freed(pe, p, 1)
                        transpose_block(kst_nat)
                unit("full", yt, y_tok, after)

            def forget_logits():
                pe.wait_ge(ff_split, 1)
                bank = open_at()
                for kt in range(16):
                    xh, xl = (v[:, kt, :] for v in xt)
                    mm(bank[:, 0:L], wffs[0][:, kt, :], xh, kt == 0, False)
                    mm(bank[:, 0:L], wffs[0][:, kt, :], xl, False, False)
                    last = mm(bank[:, 0:L], wffs[1][:, kt, :], xh, False, kt == 15)
                close_at(last)

            def forget_turn():
                n = p.n["at"] - 1
                pe.wait_ge(at_free[n % 2], n // 2 + 1)
                bank = open_at()
                for t in range(TOK):
                    last = pe.transpose(bank[:, t * 8:(t + 1) * 8], zT8[:, t * P:(t + 1) * P], ident[0:8, 0:8])
                close_at(last)

            def forget_sums():
                pe.wait_ge(ff_log, 1)
                pe.wait_ge(cst["tri"], 16)
                bank = open_at()
                mm(bank[0:8, 0:L], lgt[:, 0, 0, :], trit[:, :], True, False)
                close_at(mm(bank[0:8, P:L], lgt[:, 0, 1, :], trit[:, 0:P], False, True))

            decayed = {}

            def ret_scores(hh):
                bank = open_at()
                decayed[hh] = (p.n["at"] % 2, p.n["at"] // 2 + 1)
                mm(bank[:, 0:L], kT[:, hh, 0:P], qT[:, hh, :])
                close_at(mm(bank[:, L:L + P], kT[:, hh, P:L], qT[:, hh, P:L]))

            def ret_out(g, hh):
                b = hh % 2
                pe.wait_ge(at_free[decayed[hh][0]], decayed[hh][1])
                bank = open_tp()
                mm(bank[:, 0:P], pT[:, b, 0:P], vn[:, 0, hh * P:(hh + 1) * P])
                mm(bank[:, P:L], pT[:, b, P:L], vn[:, 0, hh * P:(hh + 1) * P], True, False)
                close_tp(mm(bank[:, P:L], pT[:, b, L:L + P], vn[:, 1, hh * P:(hh + 1) * P], False, True))

            def fox_scores(g, hh):
                if g == 0 and hh == 0:
                    pe.wait_ge(cst["cst"], 48)
                """q.k + c_q - c_k + mask, queries on partitions: [q0 x k0 | q1 x k0, k1]."""
                hd = 4 * g + hh
                bank = open_at()
                for t in range(TOK):
                    o = bank[:, t * P:t * P + (t + 1) * P]
                    n = (t + 1) * P
                    mm(o, qT[:, hh, t * P:(t + 1) * P], kT[:, hh, 0:n], True, False)
                    mm(o, c8[:, 0, t * P:(t + 1) * P], ident[0:8, hd:hd + 1].to_broadcast([8, n]), False, False)
                    mm(o, ident[0:8, hd:hd + 1].to_broadcast([8, P]), c8[:, 1, 0:n], False, False)
                    last = mm(bank[:, (2 * t) * P:(2 * t + 1) * P], ident[:, :], mask[:, :], False, True)
                close_at(last)

            def fox_turn(hh):
                n = p.n.setdefault("sm", 0)
                pe.wait_ge(sm_p, n + 1)
                b = n % 2
                bank = open_tp()
                pe.transpose(bank[:, 0:P], pr[:, b, 0:P], ident[:, :])
                pe.transpose(bank[:, P:L], pr[:, b, P:L], ident[:, :])
                p.bump("sm")
                return close_tp(pe.transpose(bank[:, L:L + P], pr[:, b, L:L + P], ident[:, :]))

            def fox_out(hh, token, kt):
                b = hh % 2
                wait_tp_read(pe, token)
                bank = open_tp()
                mm(bank[:, 0:L], vn[:, 0, hh * P:(hh + 1) * P], pT[:, b, 0:L], True, False)
                y_tok[kt] = close_tp(mm(bank[:, P:L], vn[:, 1, hh * P:(hh + 1) * P], pT[:, b, L:L + P],
                                        False, True))

            turned = {}

            def fox_steps(g, i):
                def turn(hh):
                    turned[hh] = fox_turn(hh)
                if i == 0:
                    for tk in turned_qk:
                        wait_tp_read(pe, tk)
                    turned_qk.clear()
                    pe.wait_ge(c_ready, 1)
                    fox_scores(g, 0)
                    fox_scores(g, 1)
                elif i == 1:
                    turn(0)
                    fox_scores(g, 2)
                elif i == 2:
                    wait_freed(pe, p, 1)
                    fox_out(0, turned[0], 4 * g)
                    turn(1)
                    fox_scores(g, 3)
                elif i == 3:
                    fox_out(1, turned[1], 4 * g + 1)
                    turn(2)
                elif i == 4:
                    turn(3)
                elif i == 5:
                    fox_out(2, turned[2], 4 * g + 2)
                elif i == 6:
                    fox_out(3, turned[3], 4 * g + 3)

            turned_qk = []

            def even_after(e, i):
                if e == 0 and i == 6:
                    forget_logits()
                if e == 1 and i == 2:
                    forget_turn()
                if e == 1 and i == 7:
                    forget_sums()
                prev = E_UNITS[e - 1] if e else None
                if prev and prev[0] in ("rq", "rk") and i == 6:
                    pe.wait_ge(rot_ready, p.bump("rot"))
                    turned_qk.extend(transpose_block(rot))
                if prev and prev[0] in ("fq", "fk") and i == 6:
                    wait_freed(pe, p, 1)
                    turned_qk.extend(transpose_block(nat))
                if prev and prev[0] == "rv":
                    if i == 1:
                        for tk in turned_qk:
                            wait_tp_read(pe, tk)
                        turned_qk.clear()
                    if 2 <= i <= 5:
                        ret_scores(i - 2)
                    if i == 3:
                        wait_freed(pe, p, 1)
                    if 3 <= i <= 6:
                        ret_out(prev[1], i - 3)
                if e >= 2 and E_UNITS[e - 2][0] == "rg" and i == 1:
                    g = E_UNITS[e - 2][1]
                    pe.wait_ge(ro_ready, g + 1)
                    transpose_block(gate, y_tok, 8 + 4 * g)
                if prev and prev[0] == "fv":
                    fox_steps(prev[1], i)

            for e in range(len(E_UNITS)):
                def after(i, e=e):
                    even_after(e, i)
                unit("full", xt, x_tok, after)

            def out_proj(n, i):
                if n == 0:
                    fox_steps(1, i)
                elif i == 2:
                    h_block(n - 1, 1)

            for n in range(BLOCKS):
                unit("full", yt, y_tok, lambda i, n=n: out_proj(n, i), order=OUT_ORDER)

            def query_unit(after):
                b0 = p.n["block"]
                for i in range(HALVES):
                    hh, k0 = i % 4, 8 * (i // 4)
                    if i in (0, 2):
                        pe.wait_ge(acc_free[(b0 + i // 2) % 2], p.at("block", i // 2, by=2))
                    for kt in range(k0, k0 + 8):
                        if kt in x_tok:
                            wait_tp_read(pe, x_tok.pop(kt))
                    pe.wait_ge(lo_ready, p.at("half", i + 1))
                    w_hi, w_lo = (split_weights(v, "heads", i) for v in (whi, wlo))
                    o = acc[:, 2 * ((b0 + hh // 2) % 2) + hh % 2, 0:L]
                    for kk in range(8):
                        xh, xl = (v[:, k0 + kk, :] for v in xt)
                        pe.matmul(o, w_hi[:, kk, :], xh, start=i < 4 and kk == 0, stop=False)
                        pe.matmul(o, w_hi[:, kk, :], xl, start=False, stop=False)
                        last = pe.matmul(o, w_lo[:, kk, :], xh, start=False, stop=i >= 4 and kk == 7)
                    last.then_inc(half_used, 1)
                    after(i)
                p.bump("half", 8)
                p.bump("unit")
                p.bump("block", 2)

            def attention_and_out(layer, first_after):
                turned = {}
                b0 = p.n["block"]

                def scores(hh):
                    if hh % 2:
                        pe.wait_ge(acc_free[(b0 + hh // 2) % 2], (b0 + hh // 2) // 2 + 1)
                    else:
                        pe.wait_ge(q_ready, 2 * layer + hh // 2 + 1)
                    bank = open_at()
                    mm(bank[:, 0:L], qT[:, hh, 0:P], kvk[:, hh, :])
                    close_at(mm(bank[:, L:2 * L], qT[:, hh, P:L], kvk[:, hh, :]))

                def turn(hh):
                    pe.wait_ge(sm_p, p.bump("sm"))
                    b = hh % 2
                    bank = open_tp()
                    for mt in range(TOK):
                        for t in range(TOK):
                            last = pe.transpose(bank[:, mt * L + t * P:mt * L + (t + 1) * P],
                                                pr[:, b, t * L + mt * P:t * L + (mt + 1) * P], ident[:, :])
                    turned[hh] = close_tp(last)

                def head_out(hh):
                    wait_tp_read(pe, turned[hh])
                    b = hh % 2
                    bank = open_tp()
                    mm(bank[:, 0:L], kvv[:, 0, hh * P:(hh + 1) * P], pT[:, b, 0:L], True, False)
                    y_tok[hh] = close_tp(mm(bank[:, 0:L], kvv[:, 1, hh * P:(hh + 1) * P],
                                            pT[:, b, L:2 * L], False, True))

                def queries_after(i):
                    first_after(i)
                    if i == 5:
                        if layer:
                            pe.wait_ge(kv_in, 32)
                        scores(0)
                    if i == 6:
                        scores(1)
                        turn(0)
                    if i == 7:
                        scores(2)
                        head_out(0)
                        turn(1)
                        scores(3)
                        head_out(1)
                query_unit(queries_after)

                def after(i):
                    if i == 0:
                        turn(2)
                        turn(3)
                    if i == 1:
                        head_out(2)
                        head_out(3)
                    if i == 4:
                        h_block_in(0, 0)
                    if i == 6:
                        h_block_in(1, 1)

                def h_block_in(n, blk):
                    b = p.n["block"] + blk
                    pe.wait_ge(acc_free[b % 2], b // 2 + 1)
                    transpose_block(h[:, :, n * NB:(n + 1) * NB], x_tok, 4 * n)
                unit("mixed", yt, y_tok, after)

            def after_pairs(i):
                if i == 0:
                    h_block(2, 2)
                if i == 2:
                    h_block(3, 1)

            def mlp(final, tables=lambda t: None):
                def up_after(i):
                    if i == 1:
                        pe.wait_ge(hid_ready, p.bump("hid"))
                        transpose_block(nat, y_tok, up_after.kt)

                def step(first, last):
                    def u_after(u):
                        def after(i):
                            if first and u == 0:
                                after_pairs(i)
                            if u in (1, 2):
                                up_after(i)
                            if first:
                                tables(8 * u + i)
                        return after
                    unit("full", xt, x_tok, u_after(0))
                    up_after.kt = 0
                    unit("full", xt, x_tok, u_after(1))
                    up_after.kt = 4
                    unit("pair", yt, y_tok, u_after(2))

                    def last_after(i):
                        if i == 0:
                            h_block(0, 2)
                        if i == 2:
                            h_block(1, 1)
                    unit("pair", yt, y_tok, last_after if last and not final else u_after(3))
                step(True, False)
                with pe.Fori(0, CHUNKS - 2) as r:
                    p.enter(r, dict(STEP_RATES, his=0))
                    step(False, False)
                    p.leave(CHUNKS - 2)
                step(False, True)

            attention_and_out(0, lambda i: h_block(3, 1) if i == 1 else None)
            assert p.n["at"] == at_before_tab
            mlp(False, s5_tables)

            u_tok = {}

            def s5_u(k):
                Uc = Ucb[k % 3]
                assert p.n["tp"] == tp_before_u + k, p.n["tp"]
                pe.wait_ge(uc_in[k % 3], 32 * (k // 3 + 1))
                bank = open_tp()
                for q in range(4):
                    for r in range(2):
                        last = pe.transpose(bank[:, (2 * q + r) * J:(2 * q + r + 1) * J],
                                            Uc[:, r, q, :], ident[0:J, 0:J])
                u_tok[k] = close_tp(last)

            def s5_x(k):
                wait_tp_read(pe, u_tok.pop(k))
                ETc = ETb[k % 3]
                pe.wait_ge(et_in[k % 3], 16 * (k // 3 + 1))
                bank = open_at()
                for q in range(4):
                    for r in range(2):
                        o = bank[:, (2 * q + r) * 2 * J:(2 * q + r + 1) * 2 * J]
                        last = mm(o, ETc[:, q, r, :], UT[:, :, 4 * k + q, :])
                close_at(last)

            def s5_y(k):
                b = k % 2
                if k == 0:
                    pe.wait_ge(scan_ready, 1)
                pe.wait_ge(ca_in[b], 32 * (k // 2 + 1))
                pe.wait_ge(t_in[b], 16 * (k // 2 + 1))
                bank = open_at()
                assert p.n["at"] == at_before_y + k
                for q in range(2):
                    qq = 2 * k + q
                    o = bank[0:J, q * 2 * GW:(q + 1) * 2 * GW]
                    for r in range(2):
                        mm(o, S[:, r, qq, :], CAb[b][:, q, r, :, :], r == 0, False)
                    for s in range(2):
                        last = mm(o[:, s * GW:(s + 1) * GW], UT[:, s, qq, :], Tc[:, b, s, q, :], False, s == 1)
                close_at(last)

            def s5_steps(t):
                if 0 <= t - X8_T - 2 < 8:
                    s5_x(t - X8_T - 2)
                if 0 <= t - X8_T < 8:
                    s5_u(t - X8_T)
                if 0 <= t - Y_T < 16:
                    s5_y(t - Y_T)

            def conv_steps(o, i):
                prev = O_UNITS[o - 1] if 0 < o <= 8 else None
                if prev and prev[0] == "gc" and i == 2:
                    wait_freed(pe, p, 1)
                    transpose_block(hn)
                if prev and prev[0] == "gb" and i == 1:
                    wait_freed(pe, p, 1)
                    transpose_block(onat, y_tok, 8 + 4 * prev[1])

            def odd_after(o, i):
                if o == 0:
                    after_pairs(i)
                conv_steps(o, i)
                s5_steps(8 * o + i)

            for o in range(8):
                unit("full", xt, x_tok, lambda i, o=o: odd_after(o, i))

            def conv_out(i):
                odd_after(9, i)
                if i in (4, 5):
                    b = i - 4
                    pe.wait_ge(ge_ready, b + 1)
                    transpose_block(yy[:, :, b * NB:(b + 1) * NB], x_tok, 4 * b)

            def gated(b):
                pe.wait_ge(ssm_ready, b + 1)
                transpose_block(sg[:, :, b * NB:(b + 1) * NB], y_tok, 4 * b)
            unit("pair", yt, y_tok, lambda i: odd_after(8, i), kbase=8)
            unit("pair", yt, y_tok, conv_out, kbase=8)
            unit("seq", xt, x_tok, lambda i: gated(0) if i == 6 else None)
            unit("pair", yt, y_tok, lambda i: gated(1) if i == 1 else None)

            def last_out(i):
                if i == 0:
                    h_block(0, 2)
                if i == 2:
                    h_block(1, 1)
            unit("pair", yt, y_tok, last_out)
            attention_and_out(1, lambda i: h_block(2 + i, 2 - i) if i < 2 else None)
            mlp(True)

        @block.scalar
        def _(act):
            p = Place()
            p.n = {"half": 0, "unit": 0, "block": 0, "tp": 0, "his": 0, "at": 0}
            p.n.update({f"slab{b}": 0 for b in range(RING)})
            steps = [0]

            def link(ins):
                steps[0] += 1
                ins.then_inc(act_step, 1)
                act.wait_ge(act_step, steps[0])

            def split(i, kind):
                if i % 2 == 0:
                    loads = p.bump(f"slab{i // 2}", 2 if kind == "mixed" and i < 4 else 1)
                    act.wait_ge(raw_landed[i // 2], loads * 16)
                if p.n["half"] + i >= RING or p.reg is not None:
                    act.wait_ge(half_used, p.at("half", i - RING + 1))
                act.activation(split_weights(whi, kind, i), half_weights(raw, kind, i), ACT.Copy)\
                   .then_inc(hi_ready, 1)

            def unit(kind="full", slot=None):
                for i in range(HALVES):
                    split(i, kind)
                    if slot:
                        slot(i)
                p.bump("half", 8)
                p.bump("unit")
                p.bump("block", UNIT_BLOCKS[kind])

            def scaled(dst, row, func=ACT.Copy, back=1, off=0):
                act.wait_ge(half_used, p.at("half", off))
                act.wait_ge(*((rstd_ready, row + 1) if row < 8 else (rstd8, 1)))
                par = parity(p, back)
                for t in range(TOK):
                    last = act.activation(dst[:, t, :], acc[:, 2 * par + t, :], func, scale=rstd[:, row, t:t + 1])
                last.then_inc(acc_free[par], 1)

            def hi_parts(dst, kt0, row=None):
                for b in range(2):
                    act.wait_ge(tp_full, p.at("tp", 1))
                    bank = tp[:, p.n["tp"] % 2, :]
                    if row is None:
                        last = act.activation(dst[0][:, kt0 + 2 * b:kt0 + 2 * b + 2, :],
                                              bank.rearrange("p (k n) -> p k n", k=2), ACT.Copy)
                    else:
                        for kk in range(2):
                            kt = kt0 + 2 * b + kk
                            last = act.activation(dst[0][:, kt, :], bank[:, kk * L:(kk + 1) * L], ACT.Copy,
                                                  scale=gain[:, row + kt:row + kt + 1])
                    last.then_inc(hi_put, 1)
                    p.bump("his")
                    p.bump("tp")

            def copy_tp(dsts):
                for dst, w in dsts:
                    act.wait_ge(tp_full, p.at("tp", 1))
                    act.activation(dst, tp[:, p.n["tp"] % 2, 0:w], ACT.Copy).then_inc(tp_free[p.n["tp"] % 2], 1)
                    p.bump("tp")

            def flat(t3):
                return t3.rearrange("p a n -> p (a n)")

            def squares(src, n):
                if p.n.get("ssq"):
                    act.wait_ge(ssq_ready, p.n["ssq"])
                p.bump("ssq")
                for t in range(TOK):
                    last = act.activation(junk[:, t], src[:, t, n * NB:(n + 1) * NB], ACT.Square,
                                          accum_out=ssq[:, t, n:n + 1])
                last.then_inc(ssq_ready, 1)

            def root(m, w=2):
                act.wait_ge(var_ready, root_count(m))
                act.activation(nrm[:, 1, 0:w], nrm[:, 0, 0:w], ACT.Sqrt).then_inc(sd_ready, 1)

            def h_squares(n, back):
                wait_freed(act, p, back)
                squares(h, n)

            def at_copy(copies):
                n = p.n["at"]
                act.wait_ge(at_full, n + 1)
                for dst, src in copies(at[:, n % 2, :]):
                    last = act.activation(dst, src, ACT.Copy)
                last.then_inc(at_free[n % 2], 1)
                p.bump("at")

            act.wait_ge(tp_full, 1)
            act.activation(gain[:, 0:112], tp[:, 0, 0:112], ACT.Copy).then_inc(tp_free[0], 1)
            act.wait_ge(tp_full, 2)
            act.activation(gain[:, 112:136], tp[:, 1, 0:24], ACT.Copy).then_inc(tp_free[1], 1)
            p.bump("tp", 2)
            act.wait_ge(tp_free[0], 1)
            hi_parts(yt, 0, MEM)

            def s5_param(t):
                if t == 14:
                    at_copy(lambda bank: [(par[:, 0:3, :].rearrange("p k q -> p (k q)"), bank[:, 0:96])])
                    for r in range(2):
                        at_copy(lambda bank: [(s5c[:, r].rearrange("p q c -> p (q c)"), bank)])
                if t == 29:
                    act.wait_ge(s5_par, 1)
                    act.activation(par[:, par_of["sin"], :], par[:, par_of["th"], :], ACT.Sin)
                    act.activation(par[:, par_of["cos"], :], par[:, par_of["ph"], :], ACT.Sin).then_inc(s5_sin, 1)

            def s5_tables(t):
                if t - 4 not in CHUNK_T:
                    return
                k = CHUNK_T.index(t - 4)
                b = k % 2
                if k:
                    act.wait_ge(et_out, 16 * k)
                at_copy(lambda bank: [(ets, bank)])
                n = p.n["at"]
                act.wait_ge(at_free[(n - 1) % 2], (n - 1) // 2 + 1)
                act.dma_start(et_d[:, 2 * k:2 * k + 2].rearrange("p q r w -> p (q r w)"), ets).then_inc(et_out, 16)
                act.dma_start(ca_d[:, 2 * k:2 * k + 2].rearrange("p q r w -> p (q r w)"),
                              cz[b].rearrange("p q r w -> p (q r w)")).then_inc(ca_out[b], 16)
                act.wait_ge(*((k_out, 16 * k) if k else (ksb_zero, 1)))
                at_copy(lambda bank: [(ksb[:, :, 112:240], bank[0:2 * GC, 0:2 * GW].rearrange("p (q w) -> p q w", q=2))])
                n = p.n["at"]
                act.wait_ge(at_free[(n - 1) % 2], (n - 1) // 2 + 1)
                act.dma_start(k_d.rearrange("c (s k q) w -> s c k (q w)", s=2, q=2)[:, :, k],
                              ksb.rearrange("p q w -> p (q w)")).then_inc(k_out, 16)

            for u in range(4):
                def slot(i, u=u):
                    t = 8 * u + i
                    s5_param(t)
                    if u == 0 and i in (1, 3, 5):
                        hi_parts(yt, 4 + 4 * (i // 2), MEM)
                    if u == 0 and i in (2, 4, 5, 6):
                        squares(memt, (2, 4, 5, 6).index(i))
                    if u == 0 and i == 7:
                        root(0)
                    if u and i == 3:
                        scaled(kvv if u == 2 else kst_nat, 0)
                    if u in (1, 3) and i == 5:
                        if u == 1:
                            copy_tp([(flat(kvk[:, 2 * b:2 * b + 2, :]), 2 * L) for b in range(2)])
                        else:
                            act.wait_ge(tp_full, p.at("tp", 2))
                            copy_tp([(kst[:, b * NB:(b + 1) * NB], 2 * L) for b in range(2)])
                    if (u, i) == (1, 1) or u and i == 6:
                        b = u if i == 6 else 0
                        act.wait_ge(x_in[b], 16)
                        squares(h, b)
                    if i == 7:
                        hi_parts(xt, 4 * u, MIX)
                        if u == 3:
                            n = p.n["tp"]
                            act.wait_ge(tp_free[(n - 4) % 2], (n - 4) // 2 + 1)
                            act.wait_ge(tp_free[(n - 3) % 2], (n - 3) // 2 + 1)
                            act.dma_start(kv_d[0], kst).then_inc(kv_out, 16)
                unit("full", slot)

            def softmax_exp(causal, scale=None, row=None):
                n, m = p.n["at"], p.bump("sm") - 1
                act.wait_ge(sm_max, m + 1)
                for t in range(TOK):
                    c = slice(t * P, t * P + (t + 1) * P) if causal else slice(t * L, (t + 1) * L)
                    last = act.activation(pr[:, m % 2, c], at[:, n % 2, c], ACT.Exp,
                                          scale=scale if row is None else rstd[:, row, t:t + 1],
                                          bias=smx[:, m % 2, 0, t:t + 1], accum_out=smx[:, m % 2, 1, t:t + 1])
                last.then_inc(at_free[n % 2], 1)
                p.bump("at")

            def copy_turned(hh, w):
                copy_tp([(pT[:, hh % 2, 0:w], w)])

            def hi_head(kt):
                act.wait_ge(tp_full, p.at("tp", 1))
                act.activation(yt[0][:, kt, :], tp[:, p.n["tp"] % 2, 0:L], ACT.Copy).then_inc(hi_put, 1)
                p.bump("his")
                p.bump("tp")

            def fox_slots(g, i):
                if i == 4:
                    softmax_exp(True, 1.0)
                elif 5 <= i <= 7:
                    softmax_exp(True, 1.0)
                    if i >= 6:
                        hi_head(4 * g + i - 6)
                    copy_turned(i - 5, L + P)
                elif i == 8:
                    copy_turned(3, L + P)
                    hi_head(4 * g + 2)
                    hi_head(4 * g + 3)

            def copy_qk(dst):
                copy_tp([(flat(dst[:, 2 * b:2 * b + 2, :]), 2 * L) for b in range(2)])

            def even_slots(e, i):
                prev = E_UNITS[e - 1] if e else None
                if e == 0 and i == 3:
                    act.wait_ge(half_used, p.at("half"))
                    act.wait_ge(cst["ff"], 16)
                    act.activation(wffs[0], wff, ACT.Copy).then_inc(ff_hi, 1)
                if e == 1 and i == 1:
                    at_copy(lambda bank: [(zT8[:, :], bank[0:8, 0:L])])
                if e == 0 and i == 2:
                    root(1)
                if e == 0 and i == 3:
                    act.wait_ge(kv_out, 16)
                    scaled(kst.rearrange("p (t n) -> p t n", t=TOK), 0)
                if e == 0 and i == 4:
                    wait_freed(act, p, 1)
                    act.dma_start(kv_d[1], kst).then_inc(kv_out, 16)
                if e == 1 and i == 5:
                    act.wait_ge(ff_z, 1)
                    link(act.activation(lgt[:, 2], lgt[:, 1], ACT.Exp, scale=-1.0))
                    act.activation(lgt[:, 3], lgt[:, 2], ACT.Ln, bias=1.0).then_inc(ff_act, 1)
                    p.bump("at")
                if e == 2 and i == 2:
                    at_copy(lambda bank: [(c8[:, 0, :], bank[0:8, 0:L])])
                two_back = E_UNITS[e - 2] if e >= 2 else None
                if two_back and two_back[0] in ("rq", "rk", "fq", "fk") and i == 1:
                    copy_qk(qT if two_back[0][1] == "q" else kT)
                if prev and prev[0] == "rg" and i < 2:
                    ro_copy(2 + i)
                if two_back and two_back[0] == "fv" and i == 0:
                    fox_slots(two_back[1], 8)
                if prev and i == 3:
                    name = prev[0]
                    if name in ("rq", "rk"):
                        if p.n.get("rot", 0):
                            act.wait_ge(rot_ready, p.n["rot"])
                        scaled(nat, 1)
                        p.bump("rot")
                    elif name == "fq":
                        scaled(nat, 8)
                    elif name == "fk":
                        scaled(nat, 1)
                    elif name in ("rv", "fv"):
                        scaled(vn, 1)
                    else:
                        scaled(gate, 1, ACT.Silu)
                        act.wait_ge(var_ready, 3 + prev[1])
                        act.activation(nrm[:, 1, :], nrm[:, 0, :], ACT.Sqrt).then_inc(sd_ready, 1)
                if prev and prev[0] == "rv":
                    if 4 <= i <= 7:
                        p.bump("at")
                    if i in (6, 7):
                        ro_copy(i - 6)
                if two_back and two_back[0] == "rg" and i == 4:
                    hi_parts(yt, 8 + 4 * two_back[1])
                if prev and prev[0] == "fv":
                    fox_slots(prev[1], i)

            def ro_copy(hh):
                act.wait_ge(tp_full, p.at("tp", 1))
                b = p.n["tp"] % 2
                act.activation(ro[:, :, hh * P:(hh + 1) * P], tp[:, b, 0:L].rearrange("p (t n) -> p t n", t=TOK),
                               ACT.Copy).then_inc(tp_free[b], 1)
                p.bump("tp")

            for e in range(len(E_UNITS)):
                def slot(i, e=e):
                    if (e, i) == (3, 1):
                        act.wait_ge(prep_out, 16)
                    even_slots(e, i)
                unit("full", slot)

            def out_slots(n, i):
                if n == 0:
                    if i == 3:
                        scaled(vn, 1)
                    if i == 1:
                        copy_qk(kT)
                    fox_slots(1, i)
                if n == 1 and i == 0:
                    fox_slots(1, 8)
                if n and i == 4:
                    h_squares(n - 1, 1)
                if n and i == 5:
                    hi_parts(xt, 4 * (n - 1), XAT)

            for n in range(BLOCKS):
                unit("full", lambda i, n=n: out_slots(n, i))

            def pair_slots(i, row):
                if i == 2:
                    h_squares(2, 2)
                if i == 3:
                    hi_parts(xt, 8, row)
                if i == 4:
                    h_squares(3, 1)
                if i == 5:
                    hi_parts(xt, 12, row)

            def attention_and_out(layer, first, mlp_row):
                b0 = p.n["block"]
                h0 = p.n["half"]

                def copy_query(hh):
                    act.wait_ge(half_used, h0 + 5 + hh)
                    par_ = (b0 + hh // 2) % 2
                    act.activation(qT[:, hh, :], acc[:, 2 * par_ + hh % 2, 0:L], ACT.Copy)\
                       .then_inc(acc_free[par_] if hh % 2 else q_ready, 1)

                def query_slots(i):
                    first(i)
                    if i == 7:
                        act.activation(warm[:, layer:layer + 1], ident[:, 0:1], ACT.Exp)
                        copy_query(0)
                unit("heads", query_slots)

                def slot(i):
                    if i == 0:
                        copy_query(1)
                        softmax_exp(False, row=9 + layer)
                        copy_query(2)
                    if i == 1:
                        softmax_exp(False, row=9 + layer)
                        copy_turned(0, 2 * L)
                        copy_query(3)
                        hi_head(0)
                        copy_turned(1, 2 * L)
                        softmax_exp(False, row=9 + layer)
                        hi_head(1)
                    if i == 2:
                        softmax_exp(False, row=9 + layer)
                    if i == 3:
                        copy_turned(2, 2 * L)
                        copy_turned(3, 2 * L)
                        hi_head(2)
                        hi_head(3)
                    for n in range(2):
                        if i == 5 + 2 * n:
                            b = p.n["block"] + n
                            act.wait_ge(acc_free[b % 2], b // 2 + 1)
                            squares(h, n)
                    if i == 7:
                        hi_parts(xt, 0, mlp_row)
                unit("mixed", slot)

            def mlp(layer, row, next_row, final, tables=lambda t: None):
                def step(first, last):
                    def slot_of(u):
                        def slot(i):
                            if first:
                                tables(8 * u + i)
                            if u in (1, 2):
                                if i == 3:
                                    scaled(nat, row, ACT.Relu)
                                if i == 5:
                                    hi_parts(yt, 4 * (u - 1))
                            if first and u == 0:
                                if i == 1:
                                    hi_parts(xt, 4, MLP + 16 * layer)
                                pair_slots(i, MLP + 16 * layer)
                                if i == 6:
                                    root(row)
                            if last and u == 3:
                                if i == 2:
                                    h_squares(0, 2)
                                if i == 4:
                                    h_squares(1, 1)
                                if not final and i in (3, 5):
                                    hi_parts(xt, 0 if i == 3 else 4, next_row)
                        return slot
                    for u, kind in enumerate(("full", "full", "pair", "pair")):
                        unit(kind, slot_of(u))
                step(True, False)
                with act.Fori(0, CHUNKS - 2) as r:
                    p.enter(r, dict(STEP_RATES, hid=0, **{f"slab{b}": 4 for b in range(RING)}))
                    step(False, False)
                    p.leave(CHUNKS - 2)
                step(False, True)

            def xq_first(i):
                if i == 4:
                    hi_parts(xt, 12, XAT)
                if i == 5:
                    h_squares(3, 1)
                if i == 6:
                    root(2)
            attention_and_out(0, xq_first, MLP)
            mlp(0, 3, MIX + 16, False, s5_tables)

            def s5_slots(t):
                k = t - 3 - X8_T
                if 0 <= k < 8:
                    act.wait_ge(tp_full, p.at("tp", 1))
                    b = p.n["tp"] % 2
                    act.activation(UT[:, :, 4 * k:4 * k + 4, :], tp[:, b, 0:2 * 4 * J].rearrange(
                        "p (q r j) -> p r q j", q=4, r=2), ACT.Copy).then_inc(tp_free[b], 1)
                    p.bump("tp")
                k = t - 5 - X8_T
                if 0 <= k < 8:
                    at_copy(lambda bank: [
                        (S[64 * s:64 * s + 64, :, 4 * k:4 * k + 4, 1:J],
                         bank[64 * s:64 * s + 64, :].rearrange("p (q r s j) -> p s r q j", q=4, r=2, s=2)[
                             :, s, :, :, 0:J - 1]) for s in range(2)])
                k = t - 3 - Y_T
                if 0 <= k < 16:
                    b = k % 2
                    if k >= 2:
                        act.wait_ge(y_out[b], 32 * (k // 2))
                    at_copy(lambda bank: [
                        (Yc[:, b, :, :, q * GC:(q + 1) * GC], bank[0:J, q * 2 * GW:(q + 1) * 2 * GW].rearrange(
                            "p (s i c) -> p i s c", s=2, i=T8)) for q in range(2)])
                    n = p.n["at"] - 1
                    act.wait_ge(at_free[n % 2], n // 2 + 1)
                    for s in range(2):
                        act.dma_start(y_d.rearrange("(j i) (s n) -> s j i n", i=T8, s=2)[
                            s, :, :, 2 * GC * k:2 * GC * (k + 1)], Yc[:, b, :, s, :]).then_inc(y_out[b], 16)

            def odd_slots(o, i):
                if o == 0:
                    pair_slots(i, MIX + 16)
                    if i == 6:
                        root(4)
                prev = O_UNITS[o - 1] if 1 <= o <= 8 else None
                if prev and i == (2 if prev[0] == "gb" else 3):
                    if prev[0] == "u":
                        if prev[1]:
                            act.wait_ge(u_out, 48)
                        scaled(onat, 4)
                    elif prev[0] == "h":
                        scaled(hn, 4)
                    elif prev[0] == "gb":
                        if prev[1] == 0:
                            act.wait_ge(u_out, 96)
                        scaled(onat, 4)
                if prev and prev[0] == "gc" and i == 5:
                    copy_tp([(flat(zT[:, 2 * b:2 * b + 2, :]), 2 * L) for b in range(2)])
                if prev and prev[0] == "gb" and i == 5:
                    for b in range(2):
                        act.wait_ge(gb_prod, 2 * prev[1] + b + 1)
                        act.activation(yt[0][:, 8 + 4 * prev[1] + 2 * b:8 + 4 * prev[1] + 2 * b + 2, :],
                                       cv[:, 2 * b:2 * b + 2, :], ACT.Copy).then_inc(hi_put, 1)
                        p.bump("his")
                        p.bump("tp")
                s5_slots(8 * o + i)

            act.wait_ge(et_out, 16 * 16)
            for b in range(2):
                act.wait_ge(ca_out[b], 16 * 8)
            for o in range(8):
                unit("full", lambda i, o=o: odd_slots(o, i))

            unit("pair", lambda i: odd_slots(8, i))

            def conv_out_slots(i):
                odd_slots(9, i)
                if i == 4:
                    for b in range(2):
                        act.wait_ge(y_ready, b + 1)
                        act.activation(yy[:, :, b * NB:(b + 1) * NB], yy[:, :, b * NB:(b + 1) * NB],
                                       ACT.Gelu_apprx_tanh).then_inc(ge_ready, 1)
                if i == 7:
                    for b in range(2):
                        hi_parts(xt, 4 * b)
            unit("pair", conv_out_slots)

            def open_gate(b, par_, off):
                act.wait_ge(half_used, p.at("half", off))
                for t in range(TOK):
                    last = act.activation(sg[:, t, b * NB:(b + 1) * NB], acc[:, 2 * par_ + t, :], ACT.Sigmoid)
                last.then_inc(acc_free[par_], 1)
            unit("seq", lambda i: open_gate(0, parity(p, 0), 4) if i == 6 else None)

            def gate_slots(i):
                if i == 1:
                    hi_parts(yt, 0)
                if i == 2:
                    open_gate(1, parity(p, 1), 0)
                if i == 4:
                    hi_parts(yt, 4)
            unit("pair", gate_slots)

            def last_slots(i):
                if i == 2:
                    h_squares(0, 2)
                if i == 4:
                    h_squares(1, 1)
                if i in (3, 5):
                    hi_parts(xt, 0 if i == 3 else 4, XAT + 16)
            unit("pair", last_slots)

            def xq1_first(i):
                if i == 2:
                    h_squares(2, 2)
                if i in (3, 4):
                    hi_parts(xt, 8 + 4 * (i - 3), XAT + 16)
                if i == 5:
                    h_squares(3, 1)
                if i == 6:
                    root(5)
            attention_and_out(1, xq1_first, MLP + 16)
            mlp(1, 6, None, True)
            act.wait_ge(half_used, p.at("half", -2))
            h_squares(2, 2)
            h_squares(3, 1)
            root(7)
            act.wait_ge(hg_ready, 2)
            act.wait_ge(rstd_ready, 8)
            for b in range(2):
                for t in range(TOK):
                    hb = fin[:, t, b * NB:(b + 1) * NB]
                    last = act.activation(hb, hb, ACT.Copy, scale=rstd[:, 7, t:t + 1])
                last.then_inc(fin_act, 1)

        @block.vector
        def _(dve):
            p = Place()
            p.n = {"half": 0, "unit": 0, "block": 0, "tp": 0, "his": 0, "at": 0, "hid": 0}
            steps = [0]

            def link(ins):
                steps[0] += 1
                ins.then_inc(dve_step, 1)
                dve.wait_ge(dve_step, steps[0])

            def unit(kind="full", slot=None):
                for i in range(HALVES):
                    dve.wait_ge(hi_ready, p.at("half", i + 1))
                    dve.tensor_tensor(split_weights(wlo, kind, i), half_weights(raw, kind, i),
                                      split_weights(whi, kind, i).bitcast(F32), ALU.subtract).then_inc(lo_ready, 1)
                    if slot:
                        slot(i)
                p.bump("half", 8)
                p.bump("unit")
                p.bump("block", UNIT_BLOCKS[kind])

            def lo_parts(dst, kt0, row=None, src=None):
                for b in range(2):
                    dve.wait_ge(hi_put, p.at("his", 1))
                    bk = p.n["tp"] % 2
                    kt = kt0 + 2 * b
                    if row is None:
                        v = tp[:, bk, :].rearrange("p (k n) -> p k n", k=2) if src is None else src[:, 2 * b:2 * b + 2, :]
                        last = dve.tensor_tensor(dst[1][:, kt:kt + 2, :], v, dst[0][:, kt:kt + 2, :].bitcast(F32),
                                                 ALU.subtract)
                    else:
                        for kk in range(2):
                            last = dve.scalar_tensor_tensor(
                                out=dst[1][:, kt + kk, :], in0=tp[:, bk, kk * L:(kk + 1) * L],
                                scalar=gain[:, row + kt + kk:row + kt + kk + 1],
                                in1=dst[0][:, kt + kk, :].bitcast(F32), op0=ALU.mult, op1=ALU.subtract)
                    last.then_inc(tp_free[bk], 1)
                    p.bump("his")
                    p.bump("tp")

            def add_block(n, blk_back, off):
                dve.wait_ge(half_used, p.at("half", off))
                par_ = parity(p, blk_back)
                for t in range(TOK):
                    hb = h[:, t, n * NB:(n + 1) * NB]
                    last = dve.tensor_tensor(hb, acc[:, 2 * par_ + t, :], hb, ALU.add)
                last.then_inc(acc_free[par_], 1)

            def mean_square(m):
                dve.wait_ge(ssq_ready, 4 * (m + 1))
                link(dve.tensor_reduce(nrm[:, 2, 0:2], ssq[:, :, :], AX.X, ALU.add))
                dve.tensor_scalar(nrm[:, 0, 0:2], nrm[:, 2, 0:2], 1.0 / D, EPS, ALU.mult, ALU.add)\
                   .then_inc(var_ready, 1)

            def inverse_root(dst, w, count):
                dve.wait_ge(sd_ready, count)
                link(dve.reciprocal(nrm[:, 2, 0:w], nrm[:, 1, 0:w]))
                link(dve.tensor_tensor(nrm[:, 3, 0:w], nrm[:, 2, 0:w], nrm[:, 2, 0:w], ALU.mult))
                link(dve.tensor_tensor(nrm[:, 3, 0:w], nrm[:, 3, 0:w], nrm[:, 0, 0:w], ALU.mult))
                link(dve.tensor_scalar(nrm[:, 3, 0:w], nrm[:, 3, 0:w], -0.5, 1.5, ALU.mult, ALU.add))
                return dve.tensor_tensor(dst, nrm[:, 2, 0:w], nrm[:, 3, 0:w], ALU.mult)

            def rms(m, count):
                inverse_root(rstd[:, m, :], 2, count).then_inc(rstd_ready, 1)

            dve.wait_ge(tp_free[0], 1)
            dve.wait_ge(tp_free[1], 1)
            p.bump("tp", 2)
            lo_parts(yt, 0, MEM)

            def re_tables(t):
                if t not in DVE_T:
                    return
                k = DVE_T.index(t)
                b, q0 = k % 2, 2 * k
                if k == 0:
                    dve.wait_ge(prep_in, 16)
                    dve.wait_ge(tab_zero, 1)
                if k >= 2:
                    dve.wait_ge(at_full, at_before_tab + 2 * (k - 1))
                    dve.wait_ge(ca_out[b], 16 * (k // 2))
                e = etab[:, b, :, 0, :].rearrange("p q (i c) -> p q i c", i=T8)
                br, bi, pbr, pbi = table_parts(s5b, pb, q0, T8)
                tv = vtmp3[:, 0:2 * GW].rearrange("p (q i c) -> p q i c", q=2, i=T8)
                cr, ci, pr_, pi_ = table_parts(s5c, pw, q0, 9)
                t1 = vtmp2.rearrange("p (q i c) -> p q i c", q=2, i=9)
                t2 = vtmp.rearrange("p (q i c) -> p q i c", q=2, i=9)
                dve.tensor_tensor(e, br, pbr, ALU.mult)
                dve.tensor_tensor(tv, bi, pbi, ALU.mult)
                dve.tensor_tensor(t1, cr, pr_, ALU.mult)
                link(dve.tensor_tensor(t2, ci, pi_, ALU.mult))
                dve.tensor_tensor(e, e, tv, ALU.subtract)
                link(dve.tensor_tensor(cz[b][:, :, 0, :].rearrange("p q (i c) -> p q i c", i=9), t1, t2, ALU.add))
                for s in range(2):
                    ln = slice(64 * s, 64 * s + 64)
                    last = dve.tensor_copy(eb[ln, b, :, 0, s * GC:(s + 1) * GC], e[ln, :, T8 - 1, :])
                last.then_inc(s5_re, 1)

            for u in range(4):
                def slot(i, u=u):
                    t = 8 * u + i
                    if u == 0 and i in (1, 3, 5):
                        lo_parts(yt, 4 + 4 * (i // 2), MEM)
                    if u == 0 and i == 7:
                        mean_square(0)
                    if u == 1 and i == 0:
                        rms(0, 1)
                    if u == 0 and i == 5:
                        p.bump("at", 3)
                    if t == 28:
                        dve.wait_ge(s5_lam, 1)
                        dve.reciprocal(par[:, par_of["t2"], :], par[:, par_of["t1"], :]).then_inc(s5_inv, 1)
                    if u in (1, 3) and i == 5:
                        p.bump("tp", 2)
                    if i == 7:
                        lo_parts(xt, 4 * u, MIX)
                unit("full", slot)

            def softmax_max(causal, scale=None, row=None, ahead=0):
                n, m = p.n["at"] + ahead, p.bump("sm") - 1
                dve.wait_ge(at_full, n + 1)
                for t in range(TOK):
                    c = slice(t * P, t * P + (t + 1) * P) if causal else slice(t * L, (t + 1) * L)
                    last = dve.tensor_reduce(smx[:, m % 2, 2, t:t + 1], at[:, n % 2, c], AX.X, ALU.max)
                link(last)
                if row is None:
                    dve.tensor_scalar(smx[:, m % 2, 0, :], smx[:, m % 2, 2, :], -scale, None, ALU.mult)\
                       .then_inc(sm_max, 1)
                else:
                    dve.tensor_tensor(smx[:, m % 2, 0, :], smx[:, m % 2, 2, :], rstd[:, row, :], ALU.mult)\
                       .then_inc(sm_max, 1)

            def softmax_norm(causal, ahead=0):
                n, m = p.n["at"], p.n["sm"] - 1 - ahead
                dve.wait_ge(at_free[n % 2], n // 2 + 1)
                link(dve.reciprocal(smx[:, m % 2, 2, :], smx[:, m % 2, 1, :]))
                for t in range(TOK):
                    c = slice(t * P, t * P + (t + 1) * P) if causal else slice(t * L, (t + 1) * L)
                    last = dve.tensor_scalar(pr[:, m % 2, c], pr[:, m % 2, c], smx[:, m % 2, 2, t:t + 1], None,
                                             ALU.mult)
                last.then_inc(sm_p, 1)
                p.bump("at")

            def lo_head(kt, turned=1):
                p.bump("tp", turned)
                dve.wait_ge(hi_put, p.at("his", 1))
                b = p.n["tp"] % 2
                dve.tensor_tensor(yt[1][:, kt, :], tp[:, b, 0:L], yt[0][:, kt, :].bitcast(F32), ALU.subtract)\
                   .then_inc(tp_free[b], 1)
                p.bump("his")
                p.bump("tp")

            def fox_slots(g, i):
                if 4 <= i <= 7:
                    softmax_max(True, 1.0)
                    softmax_norm(True)
                    if i >= 6:
                        lo_head(4 * g + i - 6)
                elif i == 8:
                    lo_head(4 * g + 2, turned=2)
                    lo_head(4 * g + 3, turned=0)

            def decay(g, hh):
                n = p.n["at"]
                dve.wait_ge(at_full, n + 1)
                dve.wait_ge(dec_in[hh % 2], 16 * (2 * g + hh // 2 + 1))
                dve.tensor_tensor(pT[:, hh % 2, 0:L + P], at[:, n % 2, 0:L + P], dec[:, hh % 2, :], ALU.mult)\
                   .then_inc(at_free[n % 2], 1)
                p.bump("at")

            def ro_stats(hh):
                n = p.n["tp"]
                dve.wait_ge(tp_free[n % 2], n // 2 + 1)
                for t in range(TOK):
                    last = dve.bn_stats(stat[:, 4 * t + hh, :], ro[:, t, hh * P:(hh + 1) * P])
                p.bump("tp")
                if hh == 3:
                    link(last)
                    for k in range(8):
                        last = dve.bn_aggr(mv[:, k, :], stat[:, k, :])
                    link(last)
                    dve.tensor_scalar(nrm[:, 0, :], mv[:, :, 1], EPS, None, ALU.add).then_inc(var_ready, 1)

            def even_slots(e, i):
                prev = E_UNITS[e - 1] if e else None
                two_back = E_UNITS[e - 2] if e >= 2 else None
                if e == 0 and i == 4:
                    dve.wait_ge(ff_hi, 1)
                    dve.tensor_tensor(wffs[1], wff, wffs[0].bitcast(F32), ALU.subtract).then_inc(ff_split, 1)
                if e == 0 and i == 1:
                    mean_square(1)
                if e == 0 and i == 3:
                    rms(1, 2)
                    dve.wait_ge(rstd_ready, 2)
                    dve.tensor_scalar(rstd[:, 8, :], rstd[:, 1, :], SCALE, None, ALU.mult).then_inc(rstd8, 1)
                if e == 1 and i == 4:
                    p.bump("at")
                    n = p.n["at"]
                    dve.wait_ge(at_full, n + 1)
                    dve.wait_ge(cst["cst"], 48)
                    for t in range(TOK):
                        last = dve.scalar_tensor_tensor(
                            out=lgt[:, 0, t, :], in0=at[:, n % 2, t * 8:(t + 1) * 8], scalar=rstd[:, 1, t:t + 1],
                            in1=bfor[:, :], op0=ALU.mult, op1=ALU.add)
                    last.then_inc(at_free[n % 2], 1)
                    p.bump("at")
                    dve.wait_ge(at_free[n % 2], n // 2 + 1)
                    dve.scalar_tensor_tensor(out=lgt[:, 1], in0=lgt[:, 0], scalar=-1.0, in1=lgt[:, 0],
                                             op0=ALU.mult, op1=ALU.max).then_inc(ff_z, 1)
                if e == 1 and i == 6:
                    dve.wait_ge(ff_act, 1)
                    dve.scalar_tensor_tensor(out=lgt[:, 0], in0=lgt[:, 0], scalar=0.0, in1=lgt[:, 3],
                                             op0=ALU.min, op1=ALU.subtract).then_inc(ff_log, 1)
                if e == 2 and i == 3:
                    n = p.n["at"]
                    dve.wait_ge(at_free[n % 2], n // 2 + 1)
                    dve.tensor_scalar(c8[:, 1, :], c8[:, 0, :], -1.0, None, ALU.mult).then_inc(c_ready, 1)
                    p.bump("at")
                if prev and prev[0] == "rg" and i < 2:
                    ro_stats(2 + i)
                if two_back and two_back[0] in ("rq", "rk", "fq", "fk") and i == 1:
                    p.bump("tp", 2)
                if two_back and two_back[0] == "fv" and i == 0:
                    fox_slots(two_back[1], 8)
                if prev and prev[0] == "rg" and i == 4:
                    inverse_root(mv[:, :, 1], 8, 3 + prev[1]).then_inc(ro_stat, 1)
                if prev and prev[0] == "rv":
                    if i in (6, 7):
                        ro_stats(i - 6)
                    if 4 <= i <= 7:
                        decay(prev[1], i - 4)
                if two_back and two_back[0] == "rg" and i == 4:
                    lo_parts(yt, 8 + 4 * two_back[1])
                if prev and prev[0] == "fv":
                    fox_slots(prev[1], i)

            for e in range(len(E_UNITS)):
                unit("full", lambda i, e=e: even_slots(e, i))

            def out_slots(n, i):
                if n == 0:
                    if i == 1:
                        p.bump("tp", 2)
                    fox_slots(1, i)
                if n == 1 and i == 0:
                    fox_slots(1, 8)
                if n and i == 3:
                    add_block(n - 1, 1, 0)
                if n and i == 6:
                    lo_parts(xt, 4 * (n - 1), XAT)

            for n in range(BLOCKS):
                unit("full", lambda i, n=n: out_slots(n, i))

            def pair_slots(i, row):
                if i == 1:
                    add_block(2, 2, -2)
                if i == 3:
                    add_block(3, 1, 0)
                if i == 4:
                    lo_parts(xt, 8, row)
                if i == 6:
                    lo_parts(xt, 12, row)

            def attention_and_out(layer, first, m, mlp_row):
                def query_slots(i):
                    first(i)
                    if i == 7:
                        dve.wait_ge(rstd_ready, m + 1)
                        for row, f in ((9 + layer, SCALE), (11 + layer, -SCALE)):
                            last = dve.tensor_scalar(rstd[:, row, :], rstd[:, m, :], f, None, ALU.mult)
                        link(last)
                unit("heads", query_slots)

                def slot(i):
                    if i < 2:
                        softmax_max(False, row=11 + layer)
                        softmax_norm(False)
                    if i == 1:
                        softmax_max(False, row=11 + layer)
                        lo_head(0)
                        softmax_max(False, row=11 + layer, ahead=1)
                        lo_head(1)
                        softmax_norm(False, ahead=1)
                    if i == 2:
                        softmax_norm(False)
                    if i == 3:
                        lo_head(2, turned=2)
                        lo_head(3, turned=0)
                    for n in range(2):
                        if i == 5 + 2 * n:
                            add_block(n, -n, n + 3)
                    if i == 7:
                        lo_parts(xt, 0, mlp_row)
                unit("mixed", slot)

            def mlp(layer, m, next_row, final, tables=lambda t: None):
                def step(first, last):
                    def slot_of(u):
                        def slot(i):
                            if u in (1, 2):
                                if i == 3:
                                    wait_freed(dve, p, 1)
                                    dve.tensor_tensor(nat, nat, nat, ALU.mult).then_inc(hid_ready, 1)
                                    p.bump("hid")
                                if i == 5:
                                    lo_parts(yt, 4 * (u - 1))
                            if u == 0 and first:
                                if i == 1:
                                    lo_parts(xt, 4, MLP + 16 * layer)
                                pair_slots(i, MLP + 16 * layer)
                                if i == 6:
                                    mean_square(m)
                                if i == 7:
                                    rms(m, root_count(m))
                            elif u == 0:
                                if i == 1:
                                    add_block(2, 2, -2)
                                if i == 3:
                                    add_block(3, 1, 0)
                            if u == 3:
                                if i == 1:
                                    add_block(0, 2, -2)
                                if i == 3:
                                    add_block(1, 1, 0)
                                if last and not final and i in (4, 6):
                                    lo_parts(xt, 0 if i == 4 else 4, next_row)
                            if first:
                                tables(8 * u + i)
                        return slot
                    for u, kind in enumerate(("full", "full", "pair", "pair")):
                        unit(kind, slot_of(u))
                step(True, False)
                with dve.Fori(0, CHUNKS - 2) as r:
                    p.enter(r, dict(STEP_RATES))
                    step(False, False)
                    p.leave(CHUNKS - 2)
                step(False, True)

            def xq_first(i):
                if i == 3:
                    add_block(3, 1, 0)
                if i == 4:
                    lo_parts(xt, 12, XAT)
                if i == 6:
                    mean_square(2)
                if i == 7:
                    rms(2, root_count(2))
            attention_and_out(0, xq_first, 2, MLP)
            mlp(0, 3, MIX + 16, False, re_tables)
            p.bump("at", 2 * 16)

            def convolve(g):
                n = p.n["tp"]
                for b in range(2):
                    dve.wait_ge(tp_free[(n + b) % 2], (n + b) // 2 + 1)
                for s in range(3):
                    for k in range(4):
                        w = gain[:, 112 + (2 - s) * 8 + 4 * g + k:112 + (2 - s) * 8 + 4 * g + k + 1]
                        if s == 0:
                            last = dve.tensor_scalar(cv[:, k, :], zT[:, k, :], w, None, ALU.mult)
                        else:
                            last = dve.scalar_tensor_tensor(
                                out=cv[:, k, s:], in0=zT[:, k, 0:L - s], scalar=w, in1=cv[:, k, s:],
                                op0=ALU.mult, op1=ALU.add)
                    link(last)
                p.bump("tp", 2)

            def odd_slots(o, i):
                t = 8 * o + i
                if o == 0:
                    pair_slots(i, MIX + 16)
                    if i == 6:
                        mean_square(4)
                    if i == 7:
                        rms(4, root_count(4))
                prev = O_UNITS[o - 1] if 1 <= o <= 8 else None
                if prev and prev[0] == "gc" and i == 3:
                    dve.wait_ge(half_used, p.at("half"))
                    wait_freed(dve, p, 2)
                    par_ = parity(p, 1)
                    for tt in range(TOK):
                        last = dve.scalar_tensor_tensor(
                            out=hn[:, tt, :], in0=acc[:, 2 * par_ + tt, :], scalar=rstd[:, 4, tt:tt + 1],
                            in1=hn[:, tt, :], op0=ALU.mult, op1=ALU.mult)
                    last.then_inc(acc_free[par_], 1)
                if prev and prev[0] == "gc" and i == 6:
                    convolve(prev[1])
                if prev and prev[0] == "gb" and i == 4:
                    n = p.n["tp"]
                    for b in range(2):
                        dve.wait_ge(tp_full, n + b + 1)
                        dve.tensor_tensor(cv[:, 2 * b:2 * b + 2, :], tp[:, (n + b) % 2, :].rearrange(
                            "p (k n) -> p k n", k=2), cv[:, 2 * b:2 * b + 2, :], ALU.mult).then_inc(gb_prod, 1)
                if prev and prev[0] == "gb" and i == 5:
                    lo_parts(yt, 8 + 4 * prev[1], src=cv)
                if t - X8_T - 13 in (0, 1):
                    dve.wait_ge(at_full, at_before_y)
                    dve.memset((kvk, kvv)[t - X8_T - 13][:, :, :], 0.0).then_inc(ca_zero, 1)
                if 0 <= t - 3 - X8_T < 8:
                    p.bump("tp")

            for o in range(8):
                unit("full", lambda i, o=o: odd_slots(o, i))

            def conv_adds(i, n):
                if i in (1, 3):
                    add_block(n + i // 2, 2 - i // 2, -2 if i == 1 else 0)

            unit("pair", lambda i: odd_slots(8, i))

            def conv_out_slots(i):
                odd_slots(9, i)
                conv_adds(i, 0)
                if i == 4:
                    dve.wait_ge(y_in, 32)
                    dve.wait_ge(cst["dsk"], 16)
                    for b in range(2):
                        c = slice(b * NB, (b + 1) * NB)
                        for t in range(TOK):
                            last = dve.tensor_tensor(uu[:, t, c], uu[:, t, c], dsk[:, c], ALU.mult)
                        link(last)
                        dve.tensor_tensor(yy[:, :, c], yy[:, :, c], uu[:, :, c], ALU.add).then_inc(y_ready, 1)
                if i == 7:
                    for b in range(2):
                        lo_parts(xt, 4 * b)
            unit("pair", conv_out_slots)

            def open_gate(b, block):
                c = slice(b * NB, (b + 1) * NB)
                dve.wait_ge(acc_free[block % 2], block // 2 + 1)
                dve.tensor_tensor(sg[:, :, c], sg[:, :, c], yy[:, :, c], ALU.mult).then_inc(ssm_ready, 1)

            def glu_slots(i):
                conv_adds(i, 2)
                if i == 6:
                    open_gate(0, p.n["block"])
            unit("seq", glu_slots)

            def gate_slots(i):
                if i == 1:
                    lo_parts(yt, 0)
                if i == 2:
                    open_gate(1, p.n["block"] - 1)
                if i == 4:
                    lo_parts(yt, 4)
            unit("pair", gate_slots)

            def last_slots(i):
                if i == 1:
                    add_block(0, 2, -2)
                if i == 3:
                    add_block(1, 1, 0)
                if i in (4, 6):
                    lo_parts(xt, 0 if i == 4 else 4, XAT + 16)
            unit("pair", last_slots)

            def xq1_first(i):
                if i in (1, 3):
                    add_block(2 + i // 2, 2 - i // 2, -2 if i == 1 else 0)
                if i in (3, 4):
                    lo_parts(xt, 8 + 4 * (i - 3), XAT + 16)
                if i == 6:
                    mean_square(5)
                if i == 7:
                    rms(5, root_count(5))
            p.bump("at", 8 + 16)
            attention_and_out(1, xq1_first, 5, MLP + 16)
            mlp(1, 6, None, True)

            add_block(2, 2, -2)
            add_block(3, 1, 0)
            mean_square(7)
            rms(7, root_count(7))
            dve.wait_ge(rstd_ready, 8)
            dve.wait_ge(cst["gf"], 16)
            for b in (2, 3):
                c = slice(b * NB, (b + 1) * NB)
                for t in range(TOK):
                    last = dve.scalar_tensor_tensor(out=fin[:, t, c], in0=h[:, t, c], scalar=rstd[:, 7, t:t + 1],
                                                    in1=gfin[:, c], op0=ALU.mult, op1=ALU.mult)
                last.then_inc(fin_ready, 1)

        @block.gpsimd
        def _(pool):
            steps = [0]

            def link(ins):
                steps[0] += 1
                ins.then_inc(pool_step, 1)
                pool.wait_ge(pool_step, steps[0])

            def tt(o, a, b, op):
                link(pool.tensor_tensor(o, a, b, op))

            def ts(o, a, s1, s2, op0, op1=None):
                if s2 is None:
                    link(pool.tensor_scalar(o, a, s1, None, op0))
                else:
                    link(pool.tensor_scalar(o, a, s1, s2, op0, op1))

            def wait_block(b):
                pool.wait_ge(acc_free[b % 2], b // 2 + 1)

            for v, src in enumerate((s5_a_re, s5_a_im, s5_log_step)):
                pool.dma_start(s5row[32 * v:32 * v + 32, :].rearrange("q (s p) -> q s p", s=2),
                               src[0].rearrange("(s q) p -> q s p", s=2)).then_inc(cst["s5"], 16)
            for r, src in enumerate((s5_b_re, s5_b_im)):
                for s in range(2):
                    pool.dma_start(s5b[64 * s:64 * s + 64, r], src[0].rearrange(
                        "(s q) p c -> s p q c", s=2)[s]).then_inc(cst["s5"], 16)
            for r, src in enumerate((s5_c_re, s5_c_im)):
                v = src[0].rearrange("(s t q) c p -> t s (q c) p", s=2, t=4)
                for t in range(4):
                    ins = pool.dma_start(craw[:, r, t, :].rearrange("p (s k) -> p s k", s=2),
                                         v[t].rearrange("s m p -> m s p"))
                    ins.then_inc(cst["s5"], 16)
            pool.dma_start(trit[:, :], tri).then_inc(cst["tri"], 16)
            pool.wait_ge(tp_full, 2 + 2 * BLOCKS)
            pool.wait_ge(ssq_ready, BLOCKS)
            pool.dma_start(wff, ab_w_in[0][:, 3 * FW:3 * FW + P].rearrange("(k p) n -> p k n", p=P))\
                .then_inc(cst["ff"], 16)

            T = {n: par[:, i, :] for n, i in par_of.items()}
            X = [ptmp[:, i, :] for i in range(16)]
            pool.wait_ge(at_free[0], 1)

            def exp_into(o, v, tmp):
                k, r, y, t = tmp
                ts(k, v, 1.4426950408889634, 12582912.0, ALU.mult, ALU.add)
                ts(k, k, -12582912.0, None, ALU.add)
                ts(k, k, 128.0, -127.0, ALU.min, ALU.max)
                ts(t, k, -0.693145751953125, None, ALU.mult)
                tt(r, v, t, ALU.add)
                ts(t, k, -1.4286068203094172e-06, None, ALU.mult)
                tt(r, r, t, ALU.add)
                ts(r, r, 1.0, -1.0, ALU.min, ALU.max)
                ts(y, r, 1.0 / 5040, 1.0 / 720, ALU.mult, ALU.add)
                for c in (1.0 / 120, 1.0 / 24, 1.0 / 6, 0.5, 1.0, 1.0):
                    tt(y, y, r, ALU.mult)
                    ts(y, y, c, None, ALU.add)
                ts(k, k, 127.0, 8388608.0, ALU.add, ALU.mult)
                link(pool.tensor_copy(t.bitcast(I32), k))
                tt(o, y, t, ALU.mult)

            def reduce_angle(o, v, tmp):
                k, t = tmp
                ts(k, v, 0.15915494309189535, 12582912.0, ALU.mult, ALU.add)
                ts(k, k, -12582912.0, None, ALU.add)
                prev = v
                for part in (6.28125, 0.0019350051879882812, 3.019916050561733e-07):
                    ts(t, k, -part, None, ALU.mult)
                    tt(o, prev, t, ALU.add)
                    prev = o

            ts(T["lre"], T["lre"], -1e-4, None, ALU.min)
            exp_into(T["step"], T["ls"], X[0:4])
            tt(X[4], T["lre"], T["step"], ALU.mult)
            exp_into(T["mag"], X[4], X[0:4])
            tt(X[4], T["lim"], T["step"], ALU.mult)
            reduce_angle(T["th"], X[4], X[0:2])
            ts(T["th"], T["th"], 3.1415925, -3.1415925, ALU.min, ALU.max)
            ts(X[5], T["th"], 1.5707963267948966, None, ALU.add)
            ts(X[6], X[5], 3.141592653589793, -6.283185307179586, ALU.is_gt, ALU.mult)
            tt(X[5], X[5], X[6], ALU.add)
            ts(T["ph"], X[5], 3.1415925, -3.1415925, ALU.min, ALU.max)
            tt(X[7], T["lre"], T["lre"], ALU.mult)
            tt(X[8], T["lim"], T["lim"], ALU.mult)
            pool.tensor_tensor(T["t1"], X[7], X[8], ALU.add).then_inc(s5_lam, 1)
            pool.wait_ge(s5_lam, 1)
            ts(X[9], T["ph"], 1.0, None, ALU.mult)
            pool.tensor_copy(X[10], T["th"]).then_inc(s5_par, 1)
            pool.wait_ge(s5_sin, 1)
            pool.wait_ge(s5_inv, 1)
            a_re, a_im = X[11], X[12]
            tt(a_re, T["mag"], T["cos"], ALU.mult)
            tt(a_im, T["mag"], T["sin"], ALU.mult)
            ts(X[0], a_re, -1.0, None, ALU.add)
            tt(X[1], X[0], T["lre"], ALU.mult)
            tt(X[2], a_im, T["lim"], ALU.mult)
            tt(X[1], X[1], X[2], ALU.add)
            tt(X[1], X[1], T["t2"], ALU.mult)
            tt(X[2], a_im, T["lre"], ALU.mult)
            tt(X[3], X[0], T["lim"], ALU.mult)
            tt(X[2], X[2], X[3], ALU.subtract)
            tt(X[2], X[2], T["t2"], ALU.mult)
            link(pool.tensor_copy(pb[:, 0, 7, :], X[1]))
            link(pool.tensor_copy(pb[:, 1, 7, :], X[2]))

            def times(o, v, re, im):
                tt(X[4], v[:, 0], re, ALU.mult)
                tt(X[5], v[:, 1], im, ALU.mult)
                tt(X[6], v[:, 0], im, ALU.mult)
                tt(X[7], v[:, 1], re, ALU.mult)
                tt(o[:, 0], X[4], X[5], ALU.subtract)
                tt(o[:, 1], X[6], X[7], ALU.add)

            for k in range(6, -1, -1):
                times(pb[:, :, k, :], pb[:, :, k + 1, :], a_re, a_im)
            link(pool.memset(pw[:, 0, 0, :], 1.0))
            link(pool.memset(pw[:, 1, 0, :], 0.0))
            for k in range(1, 9):
                times(pw[:, :, k, :], pw[:, :, k - 1, :], a_re, a_im)
            for r in range(2):
                link(pool.tensor_copy(a8[:, r, 0, :], pw[:, r, 8, :]))
            for k in range(1, T8):
                times(a8[:, :, k, :], a8[:, :, k - 1, :], a8[:, 0, 0, :], a8[:, 1, 0, :])
            ts(pw[:, 1, :, :], pw[:, 1, :, :], -1.0, None, ALU.mult)
            for n in (1, 2):
                pool.wait_ge(at_free[n % 2], n // 2 + 1)
            pool.dma_start(prep_d, prep).then_inc(prep_out, 16)

            def load_decay(g, hh):
                n = at_before_ret + 4 * g + hh - 2
                if g or hh >= 2:
                    pool.wait_ge(at_free[n % 2], n // 2 + 1)
                pool.dma_start(dec[:, hh % 2, :], decay_in[:, 4 * g + hh, :]).then_inc(dec_in[hh % 2], 16)

            rotated = [0]

            def rotary(b):
                wait_block(b)
                n4 = nat.rearrange("p t (h m) -> p t h m", h=4)
                r4 = rot.rearrange("p t (h m) -> p t h m", h=4)
                t1, t2 = n4[:, :, :, 0:64], n4[:, :, :, 64:128]
                c, s = (cs[:, a].unsqueeze(2).to_broadcast([P, TOK, 4, 64]) for a in range(2))
                tt(rtmp[:, 0], t2, s, ALU.mult)
                tt(rtmp[:, 1], t1, s, ALU.mult)
                tt(r4[:, :, :, 0:64], t1, c, ALU.mult)
                tt(r4[:, :, :, 64:128], t2, c, ALU.mult)
                tt(r4[:, :, :, 0:64], r4[:, :, :, 0:64], rtmp[:, 0], ALU.subtract)
                pool.tensor_tensor(r4[:, :, :, 64:128], r4[:, :, :, 64:128], rtmp[:, 1], ALU.add)\
                    .then_inc(rot_ready, 1)
                rotated[0] += 1
                pool.wait_ge(rot_ready, rotated[0])

            def norm_and_gate(g):
                pool.wait_ge(ro_stat, g + 1)
                wait_block(4 + 4 * g + 3)
                r3, g3 = (v.rearrange("p t (h m) -> p (t h) m", h=4) for v in (ro, gate))
                tt(r3, r3, mv[:, :, 0:1].to_broadcast([P, 8, P]), ALU.subtract)
                tt(r3, r3, mv[:, :, 1:2].to_broadcast([P, 8, P]), ALU.mult)
                pool.tensor_tensor(g3, g3, r3, ALU.mult).then_inc(ro_ready, 1)
                pool.wait_ge(ro_ready, g + 1)

            pool.wait_ge(kv_out, 32)
            for g in range(2):
                for hh in range(2):
                    load_decay(g, hh)
                rotary(4 + 4 * g)
                rotary(4 + 4 * g + 1)
                for hh in (2, 3):
                    load_decay(g, hh)
                norm_and_gate(g)

            wait_block(4 + 14)
            pool.dma_start(prep, prep_d).then_inc(prep_in, 16)
            pool.memset(eb, 0.0).then_inc(tab_zero, 1)
            pool.wait_ge(tab_zero, 1)
            pool.wait_ge(prep_in, 16)
            for k in range(16):
                b, q0 = k % 2, 2 * k
                if k == 2:
                    wait_block(4 + 14 + 4 + 2)
                    link(pool.memset(ksb[:, :, 0:112], 0.0))
                    pool.memset(gtmp[:, 0:1], 0.0).then_inc(ksb_zero, 1)
                    pool.wait_ge(ksb_zero, 1)
                if k >= 2:
                    pool.wait_ge(at_full, at_before_tab + 2 * (k - 1))
                    pool.wait_ge(ca_out[b], 16 * (k // 2))
                e = etab[:, b, :, 1, :].rearrange("p q (i c) -> p q i c", i=T8)
                br, bi, pbr, pbi = table_parts(s5b, pb, q0, T8)
                tv = gtmp[:, 0:2 * GW].rearrange("p (q i c) -> p q i c", q=2, i=T8)
                tt(e, br, pbi, ALU.mult)
                tt(tv, bi, pbr, ALU.mult)
                tt(e, e, tv, ALU.add)
                cr, ci, pr_, pi_ = table_parts(s5c, pw, q0, 9)
                t1 = gtmp2.rearrange("p (q i c) -> p q i c", q=2, i=9)
                t2 = gtmp.rearrange("p (q i c) -> p q i c", q=2, i=9)
                tt(t1, cr, pi_, ALU.mult)
                tt(t2, ci, pr_, ALU.mult)
                for s in range(2):
                    ln = slice(64 * s, 64 * s + 64)
                    link(pool.tensor_copy(eb[ln, b, :, 1, s * GC:(s + 1) * GC], e[ln, :, T8 - 1, :]))
                last = pool.tensor_tensor(cz[b][:, :, 1, :].rearrange("p q (i c) -> p q i c", i=9), t1, t2,
                                          ALU.subtract)
                last.then_inc(s5_im, 1)
                pool.wait_ge(s5_im, k + 1)

            pool.wait_ge(k_out, 16 * 16)
            for i in range(T8):
                pool.dma_start(t_d[i * GC:(i + 1) * GC], k_d[:, :, 112 - GC * i:240 - GC * i]).then_inc(t_out, 16)

            for g in range(2):
                wait_block(OB + g)
                pool.dma_start(u_d.rearrange("(t p) n -> p t n", p=P)[:, :, g * NB:(g + 1) * NB], onat)\
                    .then_inc(u_out, 16)
                for t in range(TOK):
                    pool.dma_start(uc_d.rearrange("g (t p) c -> t p g c", t=TOK)[
                        t, :, g * Q:(g + 1) * Q, :], onat[:, t, :].rearrange("p (g c) -> p g c", c=GC))\
                        .then_inc(u_out, 16)
            link(pool.memset(S[:, :, :, 0:1], 0.0))
            for n in (at_before_x + 6, at_before_x + 7):
                pool.wait_ge(at_free[n % 2], n // 2 + 1)
            S5 = S.rearrange("p r q (c i) -> p r q c i", i=T8)
            CB = J // T8

            def advance(now, before, shape, powers):
                n = shape[1] * shape[2]
                t1 = rc[:, 0:2 * n].rearrange("p (r q i) -> p r q i", r=2, q=Q)
                t2 = rc[:, 512:512 + n].rearrange("p (q i) -> p q i", q=Q)
                for r in range(2):
                    tt(t1[:, r], before(r), powers(0), ALU.mult)
                for r, op in ((0, ALU.subtract), (1, ALU.add)):
                    tt(t2, before(1 - r), powers(1), ALU.mult)
                    tt(t1[:, r], t1[:, r], t2, op)
                tt(now, now, t1, ALU.add)

            for i in range(1, T8):
                advance(S5[:, :, :, :, i], lambda r: S5[:, r, :, :, i - 1], [P, Q, CB],
                        lambda r: a8[:, r, 0, :].unsqueeze(2).to_broadcast([P, Q, CB]))
            for c in range(1, CB):
                advance(S5[:, :, :, c, :], lambda r: S5[:, r, :, c - 1, T8 - 1:T8].to_broadcast([P, Q, T8]),
                        [P, Q, T8], lambda r: a8[:, r].rearrange("p k q -> p q k"))
            pool.memset(rc[:, 0:1], 0.0).then_inc(scan_ready, 1)
            for b in range(2):
                pool.wait_ge(y_out[b], 32 * 8)
            pool.dma_start(dsk, s5_d[0].rearrange("(a g) c -> a (g c)", a=1).to_broadcast([P, G * GC]))\
                .then_inc(cst["dsk"], 16)
            pool.dma_start(yy, y_d.rearrange("(t p) n -> p t n", p=P)).then_inc(y_in, 16)
            pool.dma_start(uu, u_d.rearrange("(t p) n -> p t n", p=P)).then_inc(y_in, 16)
            wait_block(OB + 8 + 4 + 2 + 4 + 2 + 4)
            pool.dma_start(gfin, norm_final.rearrange("(a n) -> a n", a=1).to_broadcast([P, D]))\
                .then_inc(cst["gf"], 16)
            pool.wait_ge(cst["gf"], 16)
            for b in range(2):
                wait_block(OB + 8 + 4 + 2 + 4 + 2 + 4 + 6 * CHUNKS - 4 + b)
                c = slice(b * NB, (b + 1) * NB)
                pool.tensor_tensor(fin[:, :, c], h[:, :, c], gfin[:, c].unsqueeze(1).to_broadcast([P, TOK, NB]),
                                   ALU.mult).then_inc(hg_ready, 1)
                pool.wait_ge(hg_ready, b + 1)


_INS = ["x", "mem", "norm_mix", "norm_xattn", "norm_mlp", "norm_mem", "norm_final", "ab_w_in", "ab_b_forget",
        "ab_w_out", "cd_w_in", "s5_a_re", "s5_a_im", "s5_b_re", "s5_b_im", "s5_c_re", "s5_c_im", "s5_d",
        "s5_log_step", "s5_w_glu", "conv_w", "cd_w_out", "xa_wq", "xa_wkv", "xa_wo", "mlp_w1", "mlp_w2"]


def _shape_constants():
    f = np.float32
    half = HD // 2
    inv = (f(10000.0) ** (-np.arange(half, dtype=f) / f(half))).astype(f)
    ang = np.arange(L, dtype=f)[:, None] * inv[None, :]
    by_token = lambda v: v.astype(f).reshape(TOK, P, half).transpose(1, 0, 2).reshape(P, -1)
    rope = np.concatenate([by_token(np.cos(ang)), by_token(np.sin(ang))], axis=1)
    log_g = np.log1p(-np.exp2(-5.0 - np.arange(8, dtype=np.float64)))
    diff = np.arange(L)[None, :] - np.arange(P)[:, None]
    d = np.where(diff >= 0, np.exp(log_g[:, None, None] * np.maximum(diff, 0)), 0.0) * HD ** -0.5
    decay = np.concatenate([d, d[:, :, 0:P]], axis=2).transpose(1, 0, 2).astype(f)
    tri = (np.arange(L)[None, :] >= np.arange(P)[:, None]).astype(f)
    causal = np.where(np.arange(P)[None, :] <= np.arange(P)[:, None], 0.0, NEG).astype(f)
    return {"rope": rope, "decay": decay, "tri": tri, "causal": causal, "eye": np.eye(P, dtype=f)}


def kernel(**inputs):
    import concourse.bacc as bacc
    from concourse.bass_utils import run_bass_kernel_spmd

    nc = bacc.Bacc("TRN2", target_bir_lowering=False, num_devices=1)
    arrays, args = {}, []
    given = {n: np.ascontiguousarray(inputs[n]) for n in _INS}
    given.update({n: np.ascontiguousarray(a) for n, a in _shape_constants().items()})
    for name, a in given.items():
        arrays[f"in_{name}"] = a
        args.append(nc.dram_tensor(f"in_{name}", a.shape, mybir.dt.from_np(a.dtype), kind="ExternalInput").ap())
    args.append(nc.dram_tensor("out_0", (1, L, D), F32, kind="ExternalOutput").ap())
    trunk(nc, *args)
    r = run_bass_kernel_spmd(nc, [arrays], core_ids=[0])
    return r.results[0]["out_0"]
```
